# Optimizing a Trainium2 kernel written in Bass

```python
import jax, jax.numpy as jnp
from jax import lax
import numpy as np

D_MODEL = 2048
BATCH = 1
SEQ = 256
DEPTH = 1

GRID_W = 64
CTX_LEN = 256
F32 = jnp.float32

N_BRANCH = 4
RMS_EPS = 1e-6
CONV_DIM = 512
CONV_WIDTH = 31
LN_EPS = 1e-5
SSD_HEADS = 12
SSD_HEAD_DIM = 64
SSD_DIM = SSD_HEADS * SSD_HEAD_DIM
SSD_GROUPS = 4
SSD_STATE = 128
SSD_CONV = 5
SSD_CHUNK = 128
SSD_XBC = SSD_DIM + 2 * SSD_GROUPS * SSD_STATE
SSD_IN = SSD_DIM + SSD_XBC + 2 * SSD_HEADS
FOURIER_GROUPS = 4
FOURIER_GROUP_DIM = 128
FOURIER_DIM = FOURIER_GROUPS * FOURIER_GROUP_DIM
RWKV_HEADS = 8
RWKV_HEAD_DIM = 64
RWKV_DIM = RWKV_HEADS * RWKV_HEAD_DIM
DECAY_LORA = 64
ICL_LORA = 64
GATE_LORA = 128
GN_EPS = 64e-5
RWKV_IN = 3 * RWKV_DIM + 2 * DECAY_LORA + ICL_LORA + GATE_LORA
RWKV_OFFSETS = [RWKV_DIM, 2 * RWKV_DIM, 3 * RWKV_DIM, 3 * RWKV_DIM + DECAY_LORA, 3 * RWKV_DIM + 2 * DECAY_LORA, 3 * RWKV_DIM + 2 * DECAY_LORA + ICL_LORA]
REC_IN = SSD_IN + RWKV_IN
IN_OFFSETS = [SSD_IN, REC_IN, REC_IN + 2 * CONV_DIM, REC_IN + 2 * CONV_DIM + FOURIER_DIM]
IN_DIM = REC_IN + 2 * CONV_DIM + FOURIER_DIM + N_BRANCH * D_MODEL
D_FF = 4 * D_MODEL


def rms_norm(v, g):
    vf = v.astype(F32)
    y = vf * lax.rsqrt(jnp.mean(vf * vf, axis=-1, keepdims=True) + RMS_EPS)
    return (y * g.astype(F32)).astype(v.dtype)

def layer_norm(v, g, b, eps):
    vf = v.astype(F32)
    mu = jnp.mean(vf, axis=-1, keepdims=True)
    var = jnp.mean(jnp.square(vf - mu), axis=-1, keepdims=True)
    return ((vf - mu) * lax.rsqrt(var + eps) * g.astype(F32) + b.astype(F32)).astype(v.dtype)

def _flip(t):
    return jnp.flip(t, axis=1)

def dwconv1d(v, w, bias):
    k, ch = w.shape
    y = lax.conv_general_dilated(v, w.astype(v.dtype)[:, None, :], (1,), [((k - 1) // 2, k // 2)],
                                 dimension_numbers=('NWC', 'WIO', 'NWC'), feature_group_count=ch)
    return y + bias.astype(v.dtype)

def token_shift(v):
    z = jnp.zeros_like(v[:, :1])
    prev = jnp.concatenate([z, v[:, :-1]], axis=1)
    nxt = jnp.concatenate([v[:, 1:], z], axis=1)
    return 0.5 * (prev + nxt) - v

def to_cols(t, rows):
    b, l, ch = t.shape
    return t.reshape(b, rows, GRID_W, ch).transpose(0, 2, 1, 3).reshape(b, l, ch)

def to_rows(t, rows):
    b, l, ch = t.shape
    return t.reshape(b, GRID_W, rows, ch).transpose(0, 2, 1, 3).reshape(b, l, ch)

def segsum(a):
    t = a.shape[-1]
    cs = jnp.cumsum(a, axis=-1)
    diff = cs[..., :, None] - cs[..., None, :]
    return jnp.where(jnp.tril(jnp.ones((t, t), dtype=bool)), diff, -jnp.inf)

def ssd_scan(xs, dt, A, Bm, Cm, h0, need_y):
    b, l, nh, p = xs.shape
    g, n = Bm.shape[2], Bm.shape[3]
    r = nh // g
    c, q = l // SSD_CHUNK, SSD_CHUNK
    xd = (xs * dt[..., None]).reshape(b, c, q, g, r, p)
    a = (dt * A).reshape(b, c, q, g, r)
    a_cs = jnp.cumsum(a, axis=2)
    Bc = Bm.reshape(b, c, q, g, n)
    decay_s = jnp.exp(a_cs[:, :, -1:] - a_cs)
    states = jnp.einsum('bcsgn,bcsgrp->bcgrpn', Bc, xd * decay_s[..., None])
    states = jnp.concatenate([h0.reshape(b, 1, g, r, p, n), states], axis=1)
    chunk_tot = jnp.pad(a_cs[:, :, -1], ((0, 0), (1, 0), (0, 0), (0, 0))).transpose(0, 2, 3, 1)
    decay_c = jnp.exp(segsum(chunk_tot))
    states = jnp.einsum('bgrzc,bcgrpn->bzgrpn', decay_c, states)
    final = states[:, -1].reshape(b, nh, p, n)
    if not need_y:
        return None, final
    Cc = Cm.reshape(b, c, q, g, n)
    L = jnp.exp(segsum(a.transpose(0, 3, 4, 1, 2)))
    CB = jnp.einsum('bclgn,bcsgn->bgcls', Cc, Bc)
    y_diag = jnp.einsum('bgrcls,bcsgrp->bclgrp', CB[:, :, None] * L, xd)
    y_off = jnp.einsum('bclgn,bcgrpn->bclgrp', Cc, states[:, :-1]) * jnp.exp(a_cs)[..., None]
    return (y_diag + y_off).reshape(b, l, nh, p), final

def ssd_branch(u, uc, ctx_out, conv_w, conv_b, A_log, dt_bias, D_skip, norm_g, w_out):
    A = -jnp.exp(A_log.astype(F32))
    dtb = dt_bias.astype(F32)
    Dsk = D_skip.astype(F32)[:, None]

    def prep(v):
        b, l, _ = v.shape
        z, xbc, dt = jnp.split(v, [SSD_DIM, SSD_DIM + SSD_XBC], axis=-1)
        xbc = jax.nn.silu(dwconv1d(xbc, conv_w, conv_b)).astype(F32)
        xs, Bm, Cm = jnp.split(xbc, [SSD_DIM, SSD_DIM + SSD_GROUPS * SSD_STATE], axis=-1)
        xs = xs.reshape(b, l, SSD_HEADS, SSD_HEAD_DIM)
        Bm = Bm.reshape(b, l, SSD_GROUPS, SSD_STATE)
        Cm = Cm.reshape(b, l, SSD_GROUPS, SSD_STATE)
        dt = jax.nn.softplus(dt.astype(F32).reshape(b, l, 2, SSD_HEADS) + dtb)
        return z, xs, Bm, Cm, dt

    def run(v, h0f, h0b, need_y):
        z, xs, Bm, Cm, dt = prep(v)
        yf, sf = ssd_scan(xs, dt[:, :, 0], A[0], Bm, Cm, h0f, need_y)
        yb, sb = ssd_scan(_flip(xs), _flip(dt[:, :, 1]), A[1], _flip(Bm), _flip(Cm), h0b, need_y)
        if not need_y:
            return None, sf, sb
        y = yf + _flip(yb) + Dsk * xs
        y = y.reshape(z.shape).astype(z.dtype) * jax.nn.silu(z)
        return rms_norm(y, norm_g) @ w_out, sf, sb

    h0 = jnp.zeros((u.shape[0], SSD_HEADS, SSD_HEAD_DIM, SSD_STATE), F32)
    yc, sf, sb = run(uc, h0, h0, ctx_out)
    y, _, _ = run(u, sf, sb, True)
    return y, yc

def rwkv7_scan(r, w, k, v, kk, ka, S0, readout):
    def step(S, inp):
        r_t, w_t, k_t, v_t, kk_t, ka_t = inp
        sa = jnp.einsum('bhvk,bhk->bhv', S, -kk_t)
        S = S * w_t[:, :, None, :] + sa[..., None] * ka_t[:, :, None, :] + v_t[..., None] * k_t[:, :, None, :]
        y = jnp.einsum('bhvk,bhk->bhv', S, r_t) if readout else None
        return S, y
    seq = tuple(jnp.moveaxis(t, 1, 0) for t in (r, w, k, v, kk, ka))
    S, ys = lax.scan(step, S0, seq)
    return (jnp.moveaxis(ys, 0, 1) if readout else None), S

def rwkv_branch(u, uc, rows, ctx_out, mu, w0, w2, a0, a2, g2, k_k, k_a, r_k, ln_g, ln_b, w_out):
    def prep(v):
        b, l, _ = v.shape
        v = v + token_shift(v) * mu
        r, k, vv, wf, wb, al, gl = jnp.split(v, RWKV_OFFSETS, axis=-1)
        heads = lambda t: t.astype(F32).reshape(b, l, RWKV_HEADS, RWKV_HEAD_DIM)

        def decay(lo, d):
            wl = -jax.nn.softplus(-(w0[d] + jnp.tanh(lo) @ w2[d])) - 0.5
            return heads(jnp.exp(-jnp.exp(wl.astype(F32))))
        a = jax.nn.sigmoid(a0 + al @ a2)
        kk = heads(k * k_k)
        kk = kk * lax.rsqrt(jnp.sum(kk * kk, axis=-1, keepdims=True) + 1e-12)
        kmod = heads(k * (1 + (a - 1) * k_a))
        g = jax.nn.sigmoid(gl) @ g2
        return heads(r), decay(wf, 0), decay(wb, 1), kmod, heads(vv), kk, kk * heads(a), g

    def run(v, S0f, S0b, need_y):
        b, l, _ = v.shape
        r, wf, wb, k, vv, kk, ka, g = prep(v)
        yf, Sf = rwkv7_scan(r, wf, k, vv, kk, ka, S0f, need_y)
        yb, Sb = rwkv7_scan(*(_flip(t) for t in (r, wb, k, vv, kk, ka)), S0b, need_y)
        if not need_y:
            return None, Sf, Sb
        y = yf + _flip(yb)
        m = jnp.mean(y, axis=-1, keepdims=True)
        var = jnp.mean(jnp.square(y - m), axis=-1, keepdims=True)
        y = ((y - m) * lax.rsqrt(var + GN_EPS)).reshape(b, l, RWKV_DIM) * ln_g + ln_b
        bonus = (jnp.sum(r * k * r_k, axis=-1, keepdims=True) * vv).reshape(b, l, RWKV_DIM)
        return ((y + bonus) * g).astype(v.dtype), Sf, Sb

    S0 = jnp.zeros((u.shape[0], RWKV_HEADS, RWKV_HEAD_DIM, RWKV_HEAD_DIM), F32)
    oc, Sf, Sb = run(uc, S0, S0, ctx_out)
    o, _, _ = run(to_cols(u, rows), Sf, Sb, True)
    y = to_rows(o, rows) @ w_out
    yc = oc @ w_out if ctx_out else None
    return y, yc

def conformer_branch(u, seg, conv_w, conv_b, ln_g, ln_b, w_out):
    b, l, _ = u.shape
    val, gate = jnp.split(u, 2, axis=-1)
    v = (val * jax.nn.sigmoid(gate)).reshape(-1, seg, CONV_DIM)
    v = dwconv1d(v, conv_w, conv_b).reshape(b, l, CONV_DIM)
    v = layer_norm(v, ln_g, ln_b, LN_EPS)
    return jax.nn.silu(v) @ w_out

def fourier_branch(u, w_out):
    b, l, _ = u.shape
    uf = u.astype(F32).reshape(b, l, FOURIER_GROUPS, FOURIER_GROUP_DIM)
    y = jnp.fft.fftn(uf, axes=(1, 3), norm='ortho').real
    return y.reshape(b, l, FOURIER_DIM).astype(u.dtype) @ w_out

def gated_merge(gate_pre, branches, w_o):
    b, l, _ = gate_pre.shape
    gates = jax.nn.sigmoid(gate_pre).reshape(b, l, N_BRANCH, D_MODEL)
    m = gates[:, :, 0] * branches[0]
    for i in range(1, N_BRANCH):
        m = m + gates[:, :, i] * branches[i]
    return m @ w_o

def hybrid_mixer(h, hc, rows, ctx_out, w_in, conv_p, ssd_p, fourier_out, rwkv_p, w_o):
    u = h @ w_in
    uc = hc @ (w_in if ctx_out else w_in[:, :REC_IN])
    u_ssd, u_rwkv, u_conv, u_fft, u_gate = jnp.split(u, IN_OFFSETS, axis=-1)
    uc_ssd, uc_rwkv = uc[..., :SSD_IN], uc[..., SSD_IN:REC_IN]
    p_ssd, pc_ssd = ssd_branch(u_ssd, uc_ssd, ctx_out, *ssd_p)
    p_rwkv, pc_rwkv = rwkv_branch(u_rwkv, uc_rwkv, rows, ctx_out, *rwkv_p)
    p_conv = conformer_branch(u_conv, GRID_W, *conv_p)
    p_fft = fourier_branch(u_fft, fourier_out)
    y = gated_merge(u_gate, (p_conv, p_ssd, p_fft, p_rwkv), w_o)
    if not ctx_out:
        return y, None
    uc_conv, uc_fft, uc_gate = uc[..., IN_OFFSETS[1]:IN_OFFSETS[2]], uc[..., IN_OFFSETS[2]:IN_OFFSETS[3]], uc[..., IN_OFFSETS[3]:]
    pc_conv = conformer_branch(uc_conv, uc_conv.shape[1], *conv_p)
    pc_fft = fourier_branch(uc_fft, fourier_out)
    yc = gated_merge(uc_gate, (pc_conv, pc_ssd, pc_fft, pc_rwkv), w_o)
    return y, yc

def sq_relu_mlp(h, w_up, w_down):
    return jnp.square(jax.nn.relu(h @ w_up)) @ w_down

def first_inputs(seed: int = 0) -> dict:
    key = jax.random.key(seed)
    ks = iter(jax.random.split(key, 48))
    nrm = lambda shape, scale: jax.random.normal(next(ks), shape, F32) * scale
    L, D = DEPTH, D_MODEL
    x = nrm((BATCH, SEQ, D), 1.0)
    c = nrm((BATCH, D), 1.0)
    ctx = nrm((BATCH, CTX_LEN, D), 1.0)
    c_ctx = nrm((D,), 1.0)
    mod_w = nrm((L, D, 6 * D), 0.5 * D ** -0.5)
    mod_b = nrm((L, 6 * D), 0.02)
    norm_g = 1.0 + nrm((L, 4, D), 0.02)
    w_in = nrm((L, D, IN_DIM), D ** -0.5)
    conv_w = nrm((L, CONV_WIDTH, CONV_DIM), CONV_WIDTH ** -0.5)
    conv_b = nrm((L, CONV_DIM), 0.02)
    conv_ln_g = 1.0 + nrm((L, CONV_DIM), 0.02)
    conv_ln_b = nrm((L, CONV_DIM), 0.02)
    conv_out = nrm((L, CONV_DIM, D), CONV_DIM ** -0.5)
    ssd_conv_w = nrm((L, SSD_CONV, SSD_XBC), SSD_CONV ** -0.5)
    ssd_conv_b = nrm((L, SSD_XBC), 0.02)
    ssd_A_log = jnp.log(jax.random.uniform(next(ks), (L, 2, SSD_HEADS), F32, 1.0, 16.0))
    dt0 = jnp.exp(jax.random.uniform(next(ks), (L, 2, SSD_HEADS), F32, float(np.log(1e-3)), float(np.log(1e-1))))
    ssd_dt_bias = dt0 + jnp.log(-jnp.expm1(-dt0))
    ssd_D = 1.0 + nrm((L, SSD_HEADS), 0.1)
    ssd_norm_g = 1.0 + nrm((L, SSD_DIM), 0.02)
    ssd_out = nrm((L, SSD_DIM, D), SSD_DIM ** -0.5)
    fourier_out = nrm((L, FOURIER_DIM, D), FOURIER_DIM ** -0.5)
    rwkv_mu = jax.random.uniform(next(ks), (L, RWKV_IN), F32, 0.0, 1.0)
    rwkv_w0 = nrm((L, 2, RWKV_DIM), 0.5)
    rwkv_w2 = nrm((L, 2, DECAY_LORA, RWKV_DIM), 0.1 * DECAY_LORA ** -0.5)
    rwkv_a0 = nrm((L, RWKV_DIM), 0.1)
    rwkv_a2 = nrm((L, ICL_LORA, RWKV_DIM), 0.1 * ICL_LORA ** -0.5)
    rwkv_g2 = nrm((L, GATE_LORA, RWKV_DIM), GATE_LORA ** -0.5)
    rwkv_k_k = 0.85 + nrm((L, RWKV_DIM), 0.02)
    rwkv_k_a = 1.0 + nrm((L, RWKV_DIM), 0.02)
    rwkv_r_k = nrm((L, RWKV_HEADS, RWKV_HEAD_DIM), 0.1)
    rwkv_ln_g = 1.0 + nrm((L, RWKV_DIM), 0.02)
    rwkv_ln_b = nrm((L, RWKV_DIM), 0.02)
    rwkv_out = nrm((L, RWKV_DIM, D), RWKV_DIM ** -0.5)
    w_o = nrm((L, D, D), D ** -0.5)
    mlp_up = nrm((L, D, D_FF), D ** -0.5)
    mlp_down = nrm((L, D_FF, D), D_FF ** -0.5)
    return {'x': x, 'c': c, 'ctx': ctx, 'c_ctx': c_ctx, 'mod_w': mod_w, 'mod_b': mod_b,
            'norm_g': norm_g, 'w_in': w_in,
            'conv_w': conv_w, 'conv_b': conv_b, 'conv_ln_g': conv_ln_g, 'conv_ln_b': conv_ln_b, 'conv_out': conv_out,
            'ssd_conv_w': ssd_conv_w, 'ssd_conv_b': ssd_conv_b, 'ssd_A_log': ssd_A_log, 'ssd_dt_bias': ssd_dt_bias,
            'ssd_D': ssd_D, 'ssd_norm_g': ssd_norm_g, 'ssd_out': ssd_out,
            'fourier_out': fourier_out,
            'rwkv_mu': rwkv_mu, 'rwkv_w0': rwkv_w0, 'rwkv_w2': rwkv_w2, 'rwkv_a0': rwkv_a0, 'rwkv_a2': rwkv_a2,
            'rwkv_g2': rwkv_g2, 'rwkv_k_k': rwkv_k_k, 'rwkv_k_a': rwkv_k_a, 'rwkv_r_k': rwkv_r_k,
            'rwkv_ln_g': rwkv_ln_g, 'rwkv_ln_b': rwkv_ln_b, 'rwkv_out': rwkv_out,
            'w_o': w_o, 'mlp_up': mlp_up, 'mlp_down': mlp_down}

def first_block(x, c, ctx, c_ctx, mod_w, mod_b, norm_g, w_in,
              conv_w, conv_b, conv_ln_g, conv_ln_b, conv_out,
              ssd_conv_w, ssd_conv_b, ssd_A_log, ssd_dt_bias, ssd_D, ssd_norm_g, ssd_out,
              fourier_out,
              rwkv_mu, rwkv_w0, rwkv_w2, rwkv_a0, rwkv_a2, rwkv_g2, rwkv_k_k, rwkv_k_a, rwkv_r_k,
              rwkv_ln_g, rwkv_ln_b, rwkv_out,
              w_o, mlp_up, mlp_down):
    rows = x.shape[1] // GRID_W
    xc = ctx
    silu_c = jax.nn.silu(c)
    silu_cc = jax.nn.silu(c_ctx)
    for i in range(DEPTH):
        last = i == DEPTH - 1
        mod = silu_c @ mod_w[i] + mod_b[i]
        modc = silu_cc @ mod_w[i] + mod_b[i]
        sh1, sc1, g1, sh2, sc2, g2 = jnp.split(mod[:, None, :], 6, axis=-1)
        csh1, csc1, cg1, csh2, csc2, cg2 = jnp.split(modc, 6, axis=-1)
        conv_p = (conv_w[i], conv_b[i], conv_ln_g[i], conv_ln_b[i], conv_out[i])
        ssd_p = (ssd_conv_w[i], ssd_conv_b[i], ssd_A_log[i], ssd_dt_bias[i], ssd_D[i], ssd_norm_g[i], ssd_out[i])
        rwkv_p = (rwkv_mu[i], rwkv_w0[i], rwkv_w2[i], rwkv_a0[i], rwkv_a2[i], rwkv_g2[i], rwkv_k_k[i],
                  rwkv_k_a[i], rwkv_r_k[i], rwkv_ln_g[i], rwkv_ln_b[i], rwkv_out[i])
        h = rms_norm(x, norm_g[i, 0]) * (1 + sc1) + sh1
        hc = rms_norm(xc, norm_g[i, 0]) * (1 + csc1) + csh1
        y, yc = hybrid_mixer(h, hc, rows, not last, w_in[i], conv_p, ssd_p, fourier_out[i], rwkv_p, w_o[i])
        x = x + g1 * rms_norm(y, norm_g[i, 1])
        h = rms_norm(x, norm_g[i, 2]) * (1 + sc2) + sh2
        x = x + g2 * rms_norm(sq_relu_mlp(h, mlp_up[i], mlp_down[i]), norm_g[i, 3])
        if not last:
            xc = xc + cg1 * rms_norm(yc, norm_g[i, 1])
            hc = rms_norm(xc, norm_g[i, 2]) * (1 + csc2) + csh2
            xc = xc + cg2 * rms_norm(sq_relu_mlp(hc, mlp_up[i], mlp_down[i]), norm_g[i, 3])
    return x


_first_inputs = first_inputs


def first_inputs(seed=0):
    import zlib

    import numpy as np

    out = dict(_first_inputs(seed))
    spreads = {}
    factors = {'ctx': 4.42,
     'c_ctx': 5.607,
     'norm_g': 4.183,
     'conv_b': 64.0,
     'conv_ln_g': 64.0,
     'conv_ln_b': 64.0,
     'ssd_conv_b': 64.0,
     'ssd_D': 62.728,
     'ssd_norm_g': 64.0,
     'rwkv_w0': 2.748,
     'rwkv_w2': 35.513,
     'rwkv_a0': 8.0,
     'rwkv_a2': 8.0,
     'rwkv_k_k': 64.0,
     'rwkv_k_a': 21.424,
     'rwkv_ln_g': 64.0,
     'rwkv_ln_b': 64.0,
     'ssd_A_log': 2.685}
    for name, (base, spread) in spreads.items():
        noise = np.random.default_rng([zlib.crc32(name.encode()), seed]).standard_normal(out[name].shape)
        drawn = base * np.exp(spread * noise) if base else spread * noise
        out[name] = __import__('jax').numpy.asarray(drawn.astype(out[name].dtype))
    for name, factor in factors.items():
        out[name] = (out[name] * factor).astype(out[name].dtype)
    return out


_narrow_inputs = first_inputs


def first_inputs(seed=0):

    out = dict(_narrow_inputs(seed))
    wider = {'conv_ln_g': 12.0,
     'conv_ln_b': 12.0,
     'ssd_D': 12.0,
     'ssd_norm_g': 9.93,
     'fourier_out': 4.21,
     'rwkv_k_k': 12.0,
     'rwkv_k_a': 3.74,
     'rwkv_ln_g': 12.0,
     'rwkv_ln_b': 12.0}
    for name, times in wider.items():
        mean = out[name].mean()
        out[name] = (mean + times * (out[name] - mean)).astype(out[name].dtype)
    return out


HEAD_DIM = 128
D_MIX = D_MODEL
POOL_WIDTH = D_MIX // 4
N_POOL_GROUPS = 4
POOL_GROUP_DIM = POOL_WIDTH // N_POOL_GROUPS
POOL_WINDOWS = (2, 4, 8, 16)
ATTN_WIDTH = D_MIX // 2
N_ATTN_HEADS = ATTN_WIDTH // HEAD_DIM
LRU_WIDTH = D_MIX - POOL_WIDTH - ATTN_WIDTH
N_LRU_BLOCKS = 4
LRU_BLOCK_DIM = LRU_WIDTH // N_LRU_BLOCKS
LRU_CONV_WIDTH = 4
LRU_C = 8.0
D_FF_2 = ((8 * D_MODEL // 3 + 255) // 256) * 256
FFN_CONV_WIDTH = 3
Q_BLOCK = 128
N_IN = POOL_WIDTH + 3 * ATTN_WIDTH + N_ATTN_HEADS + 2 * LRU_WIDTH
EPS = 1e-6


def rmsnorm(x, g):
    xf = x.astype(jnp.float32)
    y = xf * lax.rsqrt(jnp.mean(xf * xf, axis=-1, keepdims=True) + EPS)
    return (y * g.astype(jnp.float32)).astype(x.dtype)

def causal_dwconv(u, w, b):
    K = w.shape[0]
    S = u.shape[1]
    up = jnp.pad(u, ((0, 0), (K - 1, 0), (0, 0)))
    out = b + up[:, 0:S] * w[0]
    for k in range(1, K):
        out = out + up[:, k:k + S] * w[k]
    return out

def pool_mixer(u, w, scale):
    B, S, _ = u.shape
    uf = u.astype(jnp.float32).reshape(B, S, N_POOL_GROUPS, POOL_GROUP_DIM)
    cs = jnp.cumsum(uf, axis=1)
    pos = jnp.arange(1, S + 1, dtype=jnp.float32)
    outs = []
    for g, win in enumerate(POOL_WINDOWS):
        csg = cs[:, :, g]
        lag = jnp.pad(csg, ((0, 0), (win, 0), (0, 0)))[:, :S]
        mean = (csg - lag) / jnp.minimum(pos, float(win))[None, :, None]
        outs.append(mean - uf[:, :, g])
    d = jnp.stack(outs, axis=2).astype(u.dtype)
    y = jnp.einsum('bsgc,gcd->bsgd', d, w).reshape(B, S, POOL_WIDTH)
    return y * scale

def forgetting_attention(q, k, v, f_logit, b_f):
    B, S, _ = q.shape
    H = N_ATTN_HEADS
    q = q.reshape(B, S, H, HEAD_DIM).transpose(0, 2, 1, 3)
    k = k.reshape(B, S, H, HEAD_DIM).transpose(0, 2, 1, 3)
    v = v.reshape(B, S, H, HEAD_DIM).transpose(0, 2, 1, 3)
    log_f = jax.nn.log_sigmoid(f_logit.astype(jnp.float32) + b_f.astype(jnp.float32))
    F = jnp.cumsum(log_f, axis=1).transpose(0, 2, 1)
    nb = S // Q_BLOCK
    qb = q.reshape(B, H, nb, Q_BLOCK, HEAD_DIM).transpose(2, 0, 1, 3, 4)
    Fb = F.reshape(B, H, nb, Q_BLOCK).transpose(2, 0, 1, 3)
    kpos = jnp.arange(S)
    scale = HEAD_DIM ** -0.5

    def block(args):
        q_blk, F_blk, i = args
        qpos = i * Q_BLOCK + jnp.arange(Q_BLOCK)
        s = (jnp.einsum('bhqd,bhkd->bhqk', q_blk, k).astype(jnp.float32) * scale
             + F_blk[..., None] - F[:, :, None, :])
        s = jnp.where(kpos[None, :] <= qpos[:, None], s, -jnp.inf)
        p = jax.nn.softmax(s, axis=-1).astype(v.dtype)
        return jnp.einsum('bhqk,bhkd->bhqd', p, v)

    o = lax.map(block, (qb, Fb, jnp.arange(nb)))
    return o.transpose(1, 0, 3, 2, 4).reshape(B, S, H * HEAD_DIM)

def rg_lru_branch(xb, yb, conv_w, conv_b, wa, ba, wi, bi, lam):
    B, S, _ = xb.shape
    xc = causal_dwconv(xb, conv_w, conv_b)
    xh = xc.reshape(B, S, N_LRU_BLOCKS, LRU_BLOCK_DIM)
    gate_r = jax.nn.sigmoid((jnp.einsum('bshc,hcd->bshd', xh, wa).reshape(B, S, LRU_WIDTH) + ba).astype(jnp.float32))
    gate_i = jax.nn.sigmoid((jnp.einsum('bshc,hcd->bshd', xh, wi).reshape(B, S, LRU_WIDTH) + bi).astype(jnp.float32))
    log_a = -LRU_C * gate_r * jax.nn.softplus(-lam.astype(jnp.float32))
    a = jnp.exp(log_a)
    inp = jnp.sqrt(-jnp.expm1(2.0 * log_a)) * (gate_i * xc.astype(jnp.float32))

    def combine(left, right):
        a1, b1 = left
        a2, b2 = right
        return a1 * a2, a2 * b1 + b2

    _, h = lax.associative_scan(combine, (a, inp), axis=1)
    return (h * jax.nn.gelu(yb.astype(jnp.float32))).astype(xb.dtype)

def hybrid_mixer_2(h, w_in, b_f, pool_w, pool_scale, lru_conv_w, lru_conv_b,
                 lru_wa, lru_ba, lru_wi, lru_bi, lru_lambda, w_out):
    z = h @ w_in
    sizes = [POOL_WIDTH, ATTN_WIDTH, ATTN_WIDTH, ATTN_WIDTH, N_ATTN_HEADS, LRU_WIDTH]
    offsets = [int(o) for o in np.cumsum(sizes)]
    zp, zq, zk, zv, zf, zx, zy = jnp.split(z, offsets, axis=-1)
    y_pool = pool_mixer(zp, pool_w, pool_scale)
    y_attn = forgetting_attention(zq, zk, zv, zf, b_f)
    y_lru = rg_lru_branch(zx, zy, lru_conv_w, lru_conv_b, lru_wa, lru_ba, lru_wi, lru_bi, lru_lambda)
    y = jnp.concatenate([y_pool, y_attn.astype(h.dtype), y_lru], axis=-1)
    return y @ w_out

def conv_glu_ffn(h, w_gate, w_up, conv_w, conv_b, w_down):
    g = causal_dwconv(h @ w_gate, conv_w, conv_b)
    return (jax.nn.silu(g) * (h @ w_up)) @ w_down

def second_inputs(seed: int = 0) -> dict:
    key = jax.random.key(seed)
    ks = jax.random.split(key, 26)
    f32 = jnp.float32

    def nrm(k, shape, s):
        return jax.random.normal(k, shape, f32) * s

    u_lam = jax.random.uniform(ks[15], (DEPTH, LRU_WIDTH), f32, 0.9, 0.999)
    s_lam = u_lam ** (1.0 / LRU_C)
    lru_lambda = jnp.log(s_lam) - jnp.log1p(-s_lam)
    return {
        "x": nrm(ks[0], (BATCH, SEQ, D_MODEL), 1.0),
        "c": nrm(ks[1], (BATCH, D_MODEL), 1.0),
        "w_ada": nrm(ks[2], (DEPTH, D_MODEL, 6 * D_MODEL), 0.5 * D_MODEL ** -0.5),
        "b_ada": nrm(ks[3], (DEPTH, 6 * D_MODEL), 0.01),
        "g_mix": 1.0 + nrm(ks[4], (DEPTH, D_MODEL), 0.05),
        "w_in": nrm(ks[5], (DEPTH, D_MODEL, N_IN), D_MODEL ** -0.5),
        "b_f": jax.random.uniform(ks[6], (DEPTH, N_ATTN_HEADS), f32, 1.0, 5.0),
        "pool_w": nrm(ks[7], (DEPTH, N_POOL_GROUPS, POOL_GROUP_DIM, POOL_GROUP_DIM), POOL_GROUP_DIM ** -0.5),
        "pool_scale": 1.0 + nrm(ks[8], (DEPTH, POOL_WIDTH), 0.1),
        "lru_conv_w": nrm(ks[9], (DEPTH, LRU_CONV_WIDTH, LRU_WIDTH), LRU_CONV_WIDTH ** -0.5),
        "lru_conv_b": nrm(ks[10], (DEPTH, LRU_WIDTH), 0.01),
        "lru_wa": nrm(ks[11], (DEPTH, N_LRU_BLOCKS, LRU_BLOCK_DIM, LRU_BLOCK_DIM), LRU_BLOCK_DIM ** -0.5),
        "lru_ba": nrm(ks[12], (DEPTH, LRU_WIDTH), 0.01),
        "lru_wi": nrm(ks[13], (DEPTH, N_LRU_BLOCKS, LRU_BLOCK_DIM, LRU_BLOCK_DIM), LRU_BLOCK_DIM ** -0.5),
        "lru_bi": nrm(ks[14], (DEPTH, LRU_WIDTH), 0.01),
        "lru_lambda": lru_lambda,
        "w_out": nrm(ks[16], (DEPTH, D_MIX, D_MODEL), D_MIX ** -0.5),
        "g_ffn": 1.0 + nrm(ks[17], (DEPTH, D_MODEL), 0.05),
        "w_ffn_gate": nrm(ks[18], (DEPTH, D_MODEL, D_FF_2), D_MODEL ** -0.5),
        "w_ffn_up": nrm(ks[19], (DEPTH, D_MODEL, D_FF_2), D_MODEL ** -0.5),
        "ffn_conv_w": nrm(ks[20], (DEPTH, FFN_CONV_WIDTH, D_FF_2), FFN_CONV_WIDTH ** -0.5),
        "ffn_conv_b": nrm(ks[21], (DEPTH, D_FF_2), 0.01),
        "w_ffn_down": nrm(ks[22], (DEPTH, D_FF_2, D_MODEL), D_FF_2 ** -0.5),
        "final_g": 1.0 + nrm(ks[23], (D_MODEL,), 0.05),
    }

def second_block(x, c, w_ada, b_ada, g_mix, w_in, b_f, pool_w, pool_scale, lru_conv_w, lru_conv_b,
              lru_wa, lru_ba, lru_wi, lru_bi, lru_lambda, w_out, g_ffn, w_ffn_gate, w_ffn_up,
              ffn_conv_w, ffn_conv_b, w_ffn_down, final_g):
    c_act = jax.nn.silu(c)
    for l in range(DEPTH):
        mod = c_act @ w_ada[l] + b_ada[l]
        sh1, sc1, gt1, sh2, sc2, gt2 = jnp.split(mod[:, None, :], 6, axis=-1)
        h = rmsnorm(x, g_mix[l]) * (1.0 + sc1) + sh1
        x = x + gt1 * hybrid_mixer_2(h, w_in[l], b_f[l], pool_w[l], pool_scale[l], lru_conv_w[l], lru_conv_b[l],
                                   lru_wa[l], lru_ba[l], lru_wi[l], lru_bi[l], lru_lambda[l], w_out[l])
        h = rmsnorm(x, g_ffn[l]) * (1.0 + sc2) + sh2
        x = x + gt2 * conv_glu_ffn(h, w_ffn_gate[l], w_ffn_up[l], ffn_conv_w[l], ffn_conv_b[l], w_ffn_down[l])
    return rmsnorm(x, final_g)


def setup_inputs(seed=0):
    out = dict(first_inputs(seed))
    for name, value in second_inputs(seed + 1).items():
        if name != "x":
            out[name + "_2"] = value
    return out


def reference(
    x, c, ctx, c_ctx, mod_w, mod_b, norm_g, w_in, conv_w, conv_b, conv_ln_g, conv_ln_b,
    conv_out, ssd_conv_w, ssd_conv_b, ssd_A_log, ssd_dt_bias, ssd_D, ssd_norm_g, ssd_out,
    fourier_out, rwkv_mu, rwkv_w0, rwkv_w2, rwkv_a0, rwkv_a2, rwkv_g2, rwkv_k_k, rwkv_k_a,
    rwkv_r_k, rwkv_ln_g, rwkv_ln_b, rwkv_out, w_o, mlp_up, mlp_down, c_2, w_ada_2, b_ada_2,
    g_mix_2, w_in_2, b_f_2, pool_w_2, pool_scale_2, lru_conv_w_2, lru_conv_b_2, lru_wa_2,
    lru_ba_2, lru_wi_2, lru_bi_2, lru_lambda_2, w_out_2, g_ffn_2, w_ffn_gate_2, w_ffn_up_2,
    ffn_conv_w_2, ffn_conv_b_2, w_ffn_down_2, final_g_2,
):
    x = first_block(
        x, c, ctx, c_ctx, mod_w, mod_b, norm_g, w_in, conv_w, conv_b, conv_ln_g, conv_ln_b,
        conv_out, ssd_conv_w, ssd_conv_b, ssd_A_log, ssd_dt_bias, ssd_D, ssd_norm_g, ssd_out,
        fourier_out, rwkv_mu, rwkv_w0, rwkv_w2, rwkv_a0, rwkv_a2, rwkv_g2, rwkv_k_k, rwkv_k_a,
        rwkv_r_k, rwkv_ln_g, rwkv_ln_b, rwkv_out, w_o, mlp_up, mlp_down,
    )
    return second_block(
        x, c_2, w_ada_2, b_ada_2, g_mix_2, w_in_2, b_f_2, pool_w_2, pool_scale_2, lru_conv_w_2,
        lru_conv_b_2, lru_wa_2, lru_ba_2, lru_wi_2, lru_bi_2, lru_lambda_2, w_out_2, g_ffn_2,
        w_ffn_gate_2, w_ffn_up_2, ffn_conv_w_2, ffn_conv_b_2, w_ffn_down_2, final_g_2,
    )


_drawn_inputs = setup_inputs


def setup_inputs(seed=0):
    import zlib

    import numpy as np

    out = dict(_drawn_inputs(seed))
    spreads = {}
    factors = {'rwkv_k_k': 3.94,
     'b_ada_2': 8.0,
     'g_mix_2': 7.969,
     'b_f_2': 3.07,
     'pool_scale_2': 8.0,
     'lru_conv_b_2': 200.0,
     'lru_wa_2': 6.148,
     'lru_ba_2': 200.0,
     'lru_bi_2': 200.0,
     'lru_lambda_2': 2.819,
     'g_ffn_2': 7.356,
     'ffn_conv_b_2': 53.02}
    for name, (base, spread) in spreads.items():
        noise = np.random.default_rng([zlib.crc32(name.encode()), seed]).standard_normal(out[name].shape)
        drawn = base * np.exp(spread * noise) if base else spread * noise
        out[name] = __import__('jax').numpy.asarray(drawn.astype(out[name].dtype))
    for name, factor in factors.items():
        out[name] = (out[name] * factor).astype(out[name].dtype)
    return out
```

```python
from contextlib import ExitStack

import numpy as np

import concourse.bass as bass
from concourse import mybir

ALU = mybir.AluOpType
ACT = mybir.ActivationFunctionType
AX = mybir.AxisListType
F32 = mybir.dt.float32

P = 128
D = 2048
T = 256
KT = D // P
TT = T // P
GRID_W = 64
ROWS = T // GRID_W
CONV, CONV_TAPS = 512, 31
SSD_H, SSD_P, SSD_G, SSD_N, SSD_TAPS = 12, 64, 4, 128, 5
SSD_DIM = SSD_H * SSD_P
SSD_XBC = SSD_DIM + 2 * SSD_G * SSD_N
SSD_IN = SSD_DIM + SSD_XBC + 2 * SSD_H
RW_H, RW_N, RW_DIM = 8, 64, 512
RW_C = 64
LORA, GATE_LORA = 64, 128
RW_IN = 3 * RW_DIM + 3 * LORA + GATE_LORA
REC_IN = SSD_IN + RW_IN
FFT = 512
D_FF = 4 * D
POOL, ATTN, LRU = 512, 1024, 512
AH = 8
POOL_WINDOWS = (2, 4, 8, 16)
LRU_TAPS = 4
D_FF2 = 5632
FFN_TAPS = 3
KF = D_FF // P
KF2 = D_FF2 // P
DECAY = float(np.exp(-0.5))
NEG = -1.0e30

CT = CONV // P
ST = SSD_DIM // P
FT = FFT // P
RT = RW_DIM // P
XT_TILES = SSD_XBC // P

SLOTS = 2
G_SLOTS = 2
UNIT = KT * 2 * P
UNIT2 = (KF2 // 4) * 2 * P
BO_K = CT + ST + FT + RT



def offsets(sizes):
    out, at = {}, 0
    for name, n in sizes:
        out[name] = (at, n)
        at += n
    return out, at


VECS, VEC_N = offsets([
    ("c", KT * 2), ("mod_b", 96), ("ada_b", 96), ("norm_g", 4 * KT),
    ("conv_w", CONV_TAPS * CT), ("conv_b", CT), ("conv_ln_g", CT), ("conv_ln_b", CT),
    ("ssd_cw", SSD_TAPS * XT_TILES), ("ssd_cb", XT_TILES), ("ssd_ng", ST),
    ("A_log", 2 * SSD_H), ("dt_bias", 2 * SSD_H), ("ssd_D", SSD_H),
    ("mu", 15), ("w0", 2 * RT), ("a0", RT), ("k_k", RT), ("k_a", RT), ("r_k", RT), ("rln_g", RT), ("rln_b", RT),
    ("g_mix", KT), ("g_ffn", KT), ("final_g", KT), ("b_f", AH), ("pool_scale", 4),
    ("lru_cw", LRU_TAPS * 4), ("lru_cb", 4), ("lru_ba", 4), ("lru_bi", 4), ("lru_lam", 4),
    ("ffn_cw", FFN_TAPS * KF2), ("ffn_cb", KF2),
])
LEVELS = (1, 2, 4, 8, 16, 32)
CONSTS, CONST_N = offsets(
    [("ident", P), ("ones", P), ("blk", P), ("upto", P), ("from", P), ("neg_f", P), ("neg_b", P)]
    + [(f"strict{d}", P) for d in range(2)] + [(f"incl{d}", P) for d in range(2)]
    + [(f"lev{s}_{d}", P) for s in LEVELS for d in range(2)]
    + [("eye64", RW_N), ("dft_c", 2 * P), ("dft_l", 2 * TT * T), ("reset0", T), ("reset1", T), ("pool_inv", 4 * 16),
       ("eps", 8)])
EPS_RMS, EPS_LN, EPS_GN, EPS_KK, ONE = range(5)
SMALLS, SMALL_N = offsets([("w_aldt", KT * 88), ("w2", RW_DIM), ("a2", RW_DIM), ("g2", RW_DIM)])
SMALLS2, SMALL2_N = offsets([("wf", KT * AH), ("pool_w", 4 * P), ("lru_wa", 4 * P), ("lru_wi", 4 * P)])


def shape_constants():
    out = np.zeros((P, CONST_N), np.float32)

    def put(name, a):
        o, n = CONSTS[name]
        out[:, o:o + n] = np.asarray(a, np.float32).reshape(P, n)

    i, t = np.arange(P)[:, None], np.arange(P)[None, :]
    put("ident", i == t)
    put("ones", np.ones((P, P)))
    put("blk", i // RW_N == t // RW_N)
    put("upto", i <= t)
    put("from", i >= t)
    put("neg_f", NEG * (i > t))
    put("neg_b", NEG * (i < t))
    same = i // RW_C == t // RW_C
    put("strict0", same & (i < t))
    put("strict1", same & (i > t))
    put("incl0", same & (i <= t))
    put("incl1", same & (i >= t))
    for s in LEVELS:
        pair = (i // (2 * s) == t // (2 * s)) & (i // s != t // s)
        sign = -1.0 if s == 1 else 1.0
        put(f"lev{s}_0", sign * (pair & (i < t)))
        put(f"lev{s}_1", sign * (pair & (i > t)))
    put("eye64", (np.arange(P) % RW_N)[:, None] == np.arange(RW_N)[None, :])
    c = 2 * np.pi * (i * t % P) / P
    put("dft_c", np.concatenate([np.cos(c), np.sin(c)], 1) / np.sqrt(P * T))
    l = np.arange(T)
    w = 2 * np.pi * (l[:, None] * l[None, :] % T) / T
    both = np.stack([np.cos(w), -np.sin(w)])
    put("dft_l", both.reshape(2, TT, P, T).transpose(2, 0, 1, 3))
    put("reset0", np.broadcast_to(np.arange(T) % RW_C != 0, (P, T)))
    put("reset1", np.broadcast_to(np.arange(T) % RW_C != RW_C - 1, (P, T)))
    put("pool_inv", np.broadcast_to(np.stack([1.0 / np.minimum(np.arange(1, 17), n) for n in POOL_WINDOWS]).reshape(1, -1), (P, 64)))
    put("eps", np.broadcast_to(np.array([1e-6, 1e-5, 64e-5, 1e-12, 1.0, 0, 0, 0])[None], (P, 8)))
    return out


class Own:

    def __init__(self, eng, sem):
        self.eng, self.sem, self.n = eng, sem, 0

    def step(self, ins):
        ins.then_inc(self.sem, 1)
        self.n += 1

    def settle(self, back=0):
        if self.n > back:
            self.eng.wait_ge(self.sem, self.n - back)


class Banks:

    def __init__(self, full, free):
        self.full, self.free, self.used = full, free, [0] * len(full)

    def take(self, bank, n=1):
        first = self.used[bank]
        self.used[bank] += n
        return bank, first


def branch_kernel(nc, x_t, ctx_t, vecs, consts, smalls, smalls2, c_rows, mod_u, mod_r, ada_r, conv_u, ssd_u, rw_u, gate_u, bo_u, wo_u,
                  up_u, down_u, in2_u, out2_u, ffn_u, down2_u, out_t):
    ctx = ExitStack()
    with ctx:
        def sb(name, shape):
            return ctx.enter_context(nc.sbuf_tensor(name, shape, F32))

        def sem(name):
            return ctx.enter_context(nc.semaphore(name))

        ring = sb("ring", [P, SLOTS, UNIT])
        hT = sb("hT", [P, KT, 2 * T])
        xT = sb("xT", [P, KT, T])
        K = sb("K", [P, CONST_N])
        V = sb("V", [P, VEC_N])
        rows_buf = sb("rows_buf", [P, G_SLOTS, D])
        c_row = sb("c_row", [P, D])
        g_acc = sb("g_acc", [P, G_SLOTS])
        csT = sb("csT", [P, KT, 2])
        modT = sb("modT", [P, 32, 2])
        modx = sb("modx", [P, 64])
        adaT = sb("adaT", [P, 96])
        coef = sb("coef", [P, 6 * KT])
        WORK = (nc.sbuf_bytes_remaining // 4) // 8 * 8 - 8
        work = sb("work", [P, WORK])
        ps = ctx.enter_context(nc.psum_tensor("ps", [P, 8, 512], F32))

        def kc(name, a=0, b=None):
            o, n = CONSTS[name]
            return K[:, o + a:o + (n if b is None else b)]

        def vec(name, a=0, b=None):
            o, n = VECS[name]
            return V[:, o + a:o + (n if b is None else b)]

        def eps(i):
            return kc("eps", i, i + 1)

        def w(at, n, **kw):
            v = work[:, at:at + n]
            assert at + n <= WORK, (at, n, WORK)
            if kw:
                names = list(kw)
                v = v.rearrange("p (" + " ".join(names) + " z) -> p " + " ".join(names) + " z", **kw)
            return v

        xflat = xT[:, :, :].rearrange("p k t -> p (k t)")

        convT = w(0, CT * T, a=CT)
        fftT = w(CT * T, FT * T, a=FT)
        ssdT = w((CT + FT) * T, ST * T, a=ST)
        rwT = w((CT + FT + ST) * T, RT * T, a=RT)
        W0 = BO_K * T

        w_ready = [sem(f"w_ready{s}") for s in range(SLOTS)]
        w_used = sem("w_used")
        bk = Banks([sem(f"bank_full{b}") for b in range(8)], [sem(f"bank_free{b}") for b in range(8)])
        pe_done = sem("pe_done")
        dve_done = sem("dve_done")
        act_done = sem("act_done")
        pool_done = sem("pool_done")
        vecs_in, x_in, consts_in, smalls_in = sem("vecs_in"), sem("x_in"), sem("consts_in"), sem("smalls_in")

        def full(eng, use):
            eng.wait_ge(bk.full[use[0]], use[1] + 1)

        def emptied(use, ins):
            ins.then_inc(bk.free[use[0]], 1)

        def evacuated(eng, use):
            eng.wait_ge(bk.free[use[0]], use[1] + 1)

        def acquire(pe, use, it=None, k=0):
            if it is not None:
                pe.wait_ge(bk.free[use[0]], it * k + use[1])
            elif use[1] > 0:
                pe.wait_ge(bk.free[use[0]], use[1])

        def unit_done(eng, u, it=0, k=0):
            eng.wait_ge(w_used, u + 1 + (it * k if k else 0))

        units = [0]

        def segment(n):
            at = units[0]
            units[0] += n
            return at

        def slot(n):
            return ring[:, n % SLOTS, :]

        def fetch(sp, src, at, n, size=UNIT):
            def one(j, it, wait):
                u = at + j
                if wait:
                    sp.wait_ge(w_used, u - SLOTS + 1 + (4 * it if it is not None else 0))
                i = j if it is None else j + 4 * it
                sp.dma_start(slot(u)[:, 0:size], src[i]).then_inc(w_ready[u % SLOTS], 16)

            first = 0
            if at < SLOTS:
                for j in range(SLOTS):
                    one(j, None, False)
                first = SLOTS
            if n - first >= 8:
                rounds = (n - first) // 4
                with sp.Fori(0, rounds) as it:
                    for j in range(4):
                        one(first + j, it, True)
                first += 4 * rounds
            for j in range(first, n):
                one(j, None, True)

        def unit_ready(pe, u, it=0):
            pe.wait_ge(w_ready[u % SLOTS], 16 * (u // SLOTS + 1) + 16 * it)

        def wtile(u, kt, o, width=2 * P):
            return slot(u)[:, kt * width + o * P:kt * width + o * P + P]

        c_sig, c_silu = sem("c_sig"), sem("c_silu")
        seg_mod0 = segment(16)
        use_mod0 = [bk.take(b, 8) for b in range(2)]
        use_turn = bk.take(2)
        mod_rows = work[0:2, W0 + (KT + 2) * T:W0 + (KT + 2) * T + 2 * KT * P]
        rows_ready = [sem(f"rows_ready{n}") for n in range(G_SLOTS)]
        row_free, col_done = sem("row_free"), sem("col_done")
        c_row_in, c2_row_in, c_row_sig, c_row_silu = (sem(n) for n in ("c_row_in", "c2_row_in", "c_row_sig", "c_row_silu"))
        ADA0 = 64

        def mod_pair(pe, it):
            for j in range(2):
                u = seg_mod0 + j
                unit_ready(pe, u, it if it is not None else 0)
                acquire(pe, use_mod0[j], it, 1)
                for kt in range(KT):
                    mm = pe.matmul(ps[0:2, j, 0:2 * P], csT[:, kt, :], slot(u)[:, kt * 2 * P:(kt + 1) * 2 * P], start=kt == 0, stop=kt == KT - 1)
                mm.then_inc(w_used, 1)

        def mod_row_pair(act, it):
            for j in range(2):
                unit_done(act, seg_mod0 + j, it if it is not None else 0, 2)
                at = (it if it is not None else 0) * 4 * P + j * 2 * P
                act.activation(mod_rows[:, bass.ds(at, 2 * P)], ps[0:2, j, 0:2 * P], ACT.Copy).then_inc(bk.free[j], 1)

        def fetch_rows(pool, src, first, n):
            with pool.Fori(0, n // G_SLOTS) as it:
                for j in range(G_SLOTS):
                    pool.wait_ge(row_free, it * G_SLOTS + (first + j + 1))
                    pool.dma_start(rows_buf[:, j, :], src[it * G_SLOTS + j]).then_inc(rows_ready[j], 16)

        def column(dve, dst, bias, tile, k, it=None, step=0):
            j = tile % G_SLOTS
            off = it * step if it is not None else 0
            dve.wait_ge(rows_ready[j], off * 16 // G_SLOTS + 16 * (tile // G_SLOTS + 1) if it is None else
                        it * (16 * step // G_SLOTS) + 16 * (tile // G_SLOTS + 1))
            dve.wait_ge(col_done, off + tile + 1)
            dve.tensor_tensor_reduce(rows_buf[:, j, :], rows_buf[:, j, :], c_row[:, :], 1.0, 0.0, ALU.mult, ALU.add,
                                     g_acc[:, j:j + 1]).then_inc(row_free, 1)
            dve.wait_ge(row_free, off + tile + G_SLOTS + 1)
            dve.tensor_tensor(dst[:, bass.ds(off + k, 1)], g_acc[:, j:j + 1], bias[:, bass.ds(off + k, 1)], ALU.add).then_inc(col_done, 1)

        class Mod:
            def sync(sp):
                fetch(sp, mod_u, seg_mod0, 16)

            def scalar(act, own):
                act.dma_start(V[:, :], vecs).then_inc(vecs_in, 16)
                act.dma_start(xT[:, :, :], x_t).then_inc(x_in, 16)
                act.dma_start(ctxT, ctx_t).then_inc(x_in, 16)
                act.dma_start(K[:, :], consts).then_inc(consts_in, 16)
                act.dma_start(smallw, smalls).then_inc(smalls_in, 16)
                act.dma_start(c_row[:, :], c_rows[0:1, :].to_broadcast([P, D])).then_inc(c_row_in, 16)
                act.wait_ge(vecs_in, 16)
                act.activation(csT[:, :, :].rearrange("p k c -> p (k c)"), vec("c"), ACT.Sigmoid).then_inc(c_sig, 1)

            def vector(dve, own):
                dve.sem_inc(row_free, G_SLOTS)
                dve.sem_inc(col_done, G_SLOTS)
                dve.wait_ge(c_sig, 1)
                flat = csT[:, :, :].rearrange("p k c -> p (k c)")
                dve.tensor_tensor(flat, flat, vec("c"), ALU.mult).then_inc(c_silu, 1)

            def tensor(pe, own):
                pe.wait_ge(c_silu, 1)
                mod_pair(pe, None)
                with pe.Fori(1, 4) as it:
                    mod_pair(pe, it)

        ctxT = w(W0, KT * T, a=KT)
        smallw = w(WORK - SMALL_N, SMALL_N)

        def small(name, rows=P):
            o, n = SMALLS[name]
            return smallw[0:rows, o:o + n]

        mods0, coef0 = sem("mods0"), sem("coef0")
        sq_done, rt_done, rs_done, h_scaled, h_ready = sem("sq_done"), sem("rt_done"), sem("rs_done"), sem("h_scaled"), sem("h_ready")
        use_ssq0 = bk.take(3)
        rtb = w(W0 + KT * T, 2 * T)
        gsc0 = coef[:, 0:2 * KT].rearrange("p (k c) -> p k c", c=2)

        class Norm0:
            def scalar(act, own):
                mod_row_pair(act, None)
                act.wait_ge(x_in, 32)
                act.activation(hT[:, :, 0:T], xT[:, :, :], ACT.Square).then_inc(sq_done, 1)
                act.activation(hT[:, :, T:], ctxT, ACT.Square).then_inc(sq_done, 1)
                with act.Fori(1, 4) as it:
                    mod_row_pair(act, it)
                full(act, use_ssq0)
                act.wait_ge(consts_in, 16)
                emptied(use_ssq0, act.activation(rtb, ps[:, 3, :], ACT.Sqrt, bias=eps(EPS_RMS), scale=1.0 / D))
                with act.Fori(4, 8) as it:
                    mod_row_pair(act, it)
                act.wait_ge(c_row_in, 16)
                act.activation(rows_buf[:, 0, :], c_row[:, :], ACT.Sigmoid).then_inc(c_row_sig, 1)
                act.wait_ge(mods0, 1)
                for n in range(2 * KT):
                    kt, c = n // 2, n % 2
                    act.wait_ge(h_scaled, n + 1)
                    act.activation(hT[:, kt, c * T:(c + 1) * T], hT[:, kt, c * T:(c + 1) * T], ACT.Identity,
                                   bias=modT[:, kt, c:c + 1]).then_inc(h_ready, 1)

            def tensor(pe, own):
                pe.wait_ge(sq_done, 2)
                pe.wait_ge(consts_in, 16)
                for kt in range(KT):
                    mm = pe.matmul(ps[:, 3, :], kc("ones"), hT[:, kt, :], start=kt == 0, stop=kt == KT - 1)
                mm.then_inc(bk.full[3], 1)
                with pe.Fori(4, 8) as it:
                    mod_pair(pe, it)
                for b in range(2):
                    pe.wait_ge(bk.free[b], 8)
                for n in range(2 * KT):
                    mm = pe.matmul(ps[:, 2, 2 * n:2 * n + 2], mod_rows[:, n * P:(n + 1) * P], kc("ident")[0:2, 0:2], start=True, stop=True)
                mm.then_inc(bk.full[2], 1)

            def vector(dve, own):
                evacuated(dve, use_ssq0)
                own.step(dve.reciprocal(rtb, rtb))
                full(dve, use_turn)
                bias = vec("mod_b", 0, 32).unsqueeze(2).to_broadcast([P, 32, 2])
                emptied(use_turn, dve.tensor_tensor(modT[:, 0:32, :], ps[:, 2, 0:64].rearrange("p (u c) -> p u c", c=2), bias, ALU.add))
                evacuated(dve, use_turn)
                dve.sem_inc(mods0, 1)
                g = vec("norm_g", 0, KT).unsqueeze(2).to_broadcast([P, KT, 2])
                own.step(dve.scalar_tensor_tensor(gsc0, modT[:, KT:2 * KT, :], 1.0, g, ALU.add, ALU.mult))
                own.settle()
                for n in range(2 * KT):
                    kt, c = n // 2, n % 2
                    src = xT[:, kt, :] if c == 0 else ctxT[:, kt, :]
                    dve.scalar_tensor_tensor(hT[:, kt, c * T:(c + 1) * T], src, gsc0[:, kt, c:c + 1],
                                             rtb[:, c * T:(c + 1) * T], ALU.mult, ALU.mult).then_inc(h_scaled, 1)
                dve.wait_ge(c_row_sig, 1)
                dve.tensor_tensor(c_row[:, :], c_row[:, :], rows_buf[:, 0, :], ALU.mult).then_inc(c_row_silu, 1)

        def gemm_unit(pe, u, rhs, outs, uses, kts=KT, start=True, stop=True, it=None, k=0, ring=0, parts=False):
            unit_ready(pe, u, it * ring if it is not None else 0)
            for o in range(2):
                if o < len(uses):
                    acquire(pe, uses[o], it, k)
                for kt in range(kts):
                    first = start and kt == 0 and not (parts and o == 1)
                    mm = pe.matmul(outs[o], wtile(u, kt, o), rhs(kt), start=first, stop=stop and kt == kts - 1, skip_group_check=parts)
            mm.then_inc(w_used, 1)

        def main_rhs(kt):
            return hT[:, kt, 0:T]

        def both_rhs(kt):
            return hT[:, kt, :]

        def pair(b):
            return [ps[:, b, 0:T], ps[:, b, T:]]

        seg_cf = segment(6)
        cf_use = [bk.take(n % 2) for n in range(6)]
        C0 = W0
        sgT = w(C0, CT * T, a=CT)
        valT = w(C0 + CT * T, CT * T, a=CT)
        SEG = GRID_W + CONV_TAPS - 1
        cbuf_flat = w(C0 + 2 * CT * T, CT * ROWS * SEG)
        cbuf = cbuf_flat.rearrange("p (a r z) -> p a r z", a=CT, r=ROWS)
        c1 = C0 + 2 * CT * T + CT * ROWS * SEG
        ufT = w(c1, FT * T, a=FT)
        z1 = w(c1 + FT * T, FT * TT * 2 * P, a=FT, l=TT)
        c2 = c1 + FT * T + FT * TT * 2 * P
        cacc = w(c2, CT * T, a=CT)
        csq = w(c2 + CT * T, CT * T, a=CT)
        cmu = w(c2 + 2 * CT * T, T)
        crs = w(c2 + 2 * CT * T + T, T)
        conv_sum, conv_cent, conv_sq, conv_norm = (sem(n) for n in ("conv_sum", "conv_cent", "conv_sq", "conv_norm"))
        conv_ready = sem("conv_ready")
        use_f1 = [bk.take(3 + g) for g in range(FT)]
        use_f2 = [bk.take(3 + g) for g in range(2)]
        use_mu = bk.take(7)
        use_var = bk.take(7)

        def bc(v, n):
            return v.unsqueeze(1).to_broadcast([P, n, v.shape[-1]])

        def flat(v):
            return v.rearrange("p a t -> p (a t)")

        class ConvFft:
            def sync(sp):
                fetch(sp, conv_u, seg_cf, 6)

            def tensor(pe, own):
                pe.wait_ge(h_ready, 2 * KT)
                for n in range(6):
                    gemm_unit(pe, seg_cf + n, main_rhs, pair(n % 2), [cf_use[n]])
                for g in range(FT):
                    evacuated(pe, cf_use[4 + g // 2])
                    acquire(pe, use_f1[g])
                    for l in range(TT):
                        mm = pe.matmul(ps[:, 3 + g, l * 2 * P:(l + 1) * 2 * P], ufT[:, g, l * P:(l + 1) * P], kc("dft_c"),
                                       start=True, stop=True)
                    mm.then_inc(bk.full[3 + g], 1)
                for g in range(FT):
                    evacuated(pe, use_f1[g])
                    b = 3 + g // 2
                    if g % 2 == 0:
                        acquire(pe, use_f2[g // 2])
                    for i in range(2):
                        for l in range(TT):
                            at = (i * TT + l) * T
                            mm = pe.matmul(ps[:, b, g % 2 * T:(g % 2 + 1) * T], z1[:, g, l, i * P:(i + 1) * P],
                                           kc("dft_l", at, at + T), start=i + l == 0, stop=i + l == TT)
                    if g % 2:
                        mm.then_inc(bk.full[b], 1)

            def tensor_norm(pe, own):
                for s, src, use in ((conv_sum, cacc, use_mu), (conv_sq, csq, use_var)):
                    pe.wait_ge(s, 1)
                    acquire(pe, use)
                    for t in range(CT):
                        mm = pe.matmul(ps[:, 7, 0:T], kc("ones"), src[:, t, :], start=t == 0, stop=t == CT - 1)
                    mm.then_inc(bk.full[7], 1)

            def scalar(act, own):
                for n in range(6):
                    unit_done(act, seg_cf + n)
                    i = n % 2 * 2
                    dst, f = ((sgT, ACT.Sigmoid), (valT, ACT.Copy), (ufT, ACT.Copy))[n // 2]
                    emptied(cf_use[n], act.activation(flat(dst[:, i:i + 2, :]), ps[:, n % 2, :], f))
                for g in range(FT):
                    full(act, use_f1[g])
                    emptied(use_f1[g], act.activation(z1[:, g, :, :].rearrange("p l n -> p (l n)"), ps[:, 3 + g, :], ACT.Copy))
                for h in range(2):
                    full(act, use_f2[h])
                    emptied(use_f2[h], act.activation(flat(fftT[:, 2 * h:2 * h + 2, :]), ps[:, 3 + h, :], ACT.Copy))

            def scalar_norm(act, own):
                full(act, use_mu)
                emptied(use_mu, act.activation(cmu, ps[:, 7, 0:T], ACT.Copy, scale=1.0 / CONV))
                act.wait_ge(conv_cent, 1)
                act.activation(flat(csq), flat(cacc), ACT.Square).then_inc(conv_sq, 1)
                full(act, use_var)
                emptied(use_var, act.activation(crs, ps[:, 7, 0:T], ACT.Sqrt, bias=eps(EPS_LN), scale=1.0 / CONV))
                act.wait_ge(conv_norm, 1)
                for t in range(CT):
                    act.activation(convT[:, t, :], cacc[:, t, :], ACT.Silu, bias=vec("conv_ln_b", t, t + 1),
                                   scale=vec("conv_ln_g", t, t + 1)).then_inc(conv_ready, 1)

            def vector(dve, own):
                dve.wait_ge(h_scaled, 2 * KT)
                own.step(dve.memset(cbuf_flat, 0.0))
                own.settle()
                evacuated(dve, cf_use[1])
                evacuated(dve, cf_use[2])
                evacuated(dve, cf_use[3])
                for t in range(CT):
                    own.step(dve.tensor_tensor(cbuf[:, t, :, CONV_TAPS // 2:CONV_TAPS // 2 + GRID_W],
                                               valT[:, t, :].rearrange("p (r z) -> p r z", r=ROWS),
                                               sgT[:, t, :].rearrange("p (r z) -> p r z", r=ROWS), ALU.mult))
                for k in range(CONV_TAPS):
                    for t in range(CT):
                        src = cbuf[:, t, :, k:k + GRID_W]
                        dst = cacc[:, t, :].rearrange("p (r z) -> p r z", r=ROWS)
                        tap = vec("conv_w", k * CT + t, k * CT + t + 1)
                        own.settle(CT - 1)
                        if k == 0:
                            ins = dve.tensor_scalar(dst, src, tap, vec("conv_b", t, t + 1), ALU.mult, ALU.add)
                        else:
                            ins = dve.scalar_tensor_tensor(dst, src, tap, dst, ALU.mult, ALU.add)
                        if k == CONV_TAPS - 1 and t == CT - 1:
                            ins.then_inc(conv_sum, 1)
                        else:
                            own.step(ins)

            def vector_norm(dve, own):
                evacuated(dve, use_mu)
                dve.wait_ge(conv_sum, 1)
                dve.tensor_tensor(cacc, cacc, bc(cmu, CT), ALU.subtract).then_inc(conv_cent, 1)
                evacuated(dve, use_var)
                own.step(dve.reciprocal(crs, crs))
                own.settle()
                dve.wait_ge(conv_sq, 1)
                dve.tensor_tensor(cacc, cacc, bc(crs, CT), ALU.mult).then_inc(conv_norm, 1)

        H2 = 2 * SSD_H
        NT = 2 * TT
        S0 = W0
        zT = w(S0, ST * T, a=ST)
        bT = w(S0 + 1536, SSD_G * 2 * T, a=SSD_G)
        b_tok = w(S0 + 3584, NT * SSD_G * SSD_N, a=NT)
        xsT = w(S0 + 5632, ST * 2 * T, a=ST)
        PADW = T + SSD_TAPS - 1
        pads = w(S0 + 8704, 2 * 2 * PADW).rearrange("p (r c t) -> p r c t", r=2, c=2)
        E0 = S0 + 8704 + 4 * PADW
        y_s = w(E0, SSD_DIM)
        dts = w(E0 + SSD_DIM, 8 * NT * H2).rearrange("p (i a h) -> p i a h", i=8, a=NT)
        dt_s, a_s, cs_s, tot_s, wdec_s, ecs_s, etot_s, ncs_s = (dts[:, n] for n in range(8))
        al_raw = work[0:LORA, E0 + SSD_DIM + 8 * NT * H2:E0 + SSD_DIM + 8 * NT * H2 + 2 * T]
        assert E0 + SSD_DIM + 8 * NT * H2 + 2 * T <= WORK - SMALL_N + KT * 88
        xs_tok = xflat[:, 0:NT * SSD_DIM].rearrange("p (a n) -> p a n", a=NT)
        cT = xflat[:, NT * SSD_DIM:].rearrange("p (a n) -> p a n", a=SSD_G)
        RW0 = (CT + FT + ST) * T
        sp_t = [w(RW0 + n * NT * H2, NT * H2, a=NT) for n in range(4)]
        w_aldt = small("w_aldt").rearrange("p (k n) -> p k n", k=KT)

        use_al, use_dt = bk.take(3), bk.take(4)
        seg_ssd = segment(10)
        ssd_uses = [[bk.take(n % 2)] for n in range(3)] + [[bk.take(0), bk.take(1)] for _ in range(5)] + \
            [[bk.take(n % 2)] for n in range(2)]
        use_cs = bk.take(4)
        use_cb = [bk.take(5 + n) for n in range(TT)]
        use_tr = [bk.take(3 + n % 5) for n in range(10)]
        pad_zero, pad_in, conv5, silu5, a_ready, sp_abs, sp_e, sp_u, sp_ln, dt_done = (sem(n) for n in (
            "pad_zero", "pad_in", "conv5", "silu5", "a_ready", "sp_abs", "sp_e", "sp_u", "sp_ln", "dt_done"))
        exps_ready, a_neg = sem("exps_ready"), sem("a_neg")

        def conv_dst(t):
            if t < ST:
                return xsT[:, t, :]
            return bT[:, t - ST, :] if t < ST + SSD_G else cT[:, t - ST - SSD_G, :]

        class SsdIn:
            def sync(sp):
                fetch(sp, ssd_u, seg_ssd, 10)

            def tensor(pe, own):
                pe.wait_ge(smalls_in, 16)
                acquire(pe, use_al)
                for kt in range(KT):
                    mm = pe.matmul(ps[0:LORA, 3, :], w_aldt[:, kt, 0:LORA], hT[:, kt, :], start=kt == 0, stop=kt == KT - 1)
                mm.then_inc(bk.full[3], 1)
                acquire(pe, use_dt)
                for a in range(NT):
                    for kt in range(KT):
                        mm = pe.matmul(ps[:, 4, a * H2:(a + 1) * H2], hT[:, kt, a * P:(a + 1) * P], w_aldt[:, kt, LORA:],
                                       start=kt == 0, stop=kt == KT - 1)
                mm.then_inc(bk.full[4], 1)
                for n in range(10):
                    both = 3 <= n < 8
                    outs = [ps[:, 0, :], ps[:, 1, :]] if both else pair(ssd_uses[n][0][0])
                    gemm_unit(pe, seg_ssd + n, both_rhs if both else main_rhs, outs, ssd_uses[n])
                pe.wait_ge(a_ready, 1)
                acquire(pe, use_cs)
                for a in range(NT):
                    at = a * 2 * H2
                    pe.matmul(ps[:, 4, at:at + SSD_H], kc("upto"), a_s[:, a, 0:SSD_H], start=True, stop=True)
                    pe.matmul(ps[:, 4, at + SSD_H:at + H2], kc("from"), a_s[:, a, SSD_H:], start=True, stop=True)
                    mm = pe.matmul(ps[:, 4, at + H2:at + 2 * H2], kc("ones"), a_s[:, a, :], start=True, stop=True)
                mm.then_inc(bk.full[4], 1)
                pe.wait_ge(silu5, XT_TILES)
                for a in range(TT):
                    acquire(pe, use_cb[a])
                    for g in range(SSD_G):
                        mm = pe.matmul(ps[:, 5 + a, g * P:(g + 1) * P], bT[:, g, a * P:(a + 1) * P], cT[:, g, a * P:(a + 1) * P],
                                       start=True, stop=True)
                    mm.then_inc(bk.full[5 + a], 1)
                for n in range(10):
                    src = conv_dst(n)
                    acquire(pe, use_tr[n])
                    b = use_tr[n][0]
                    for a in range(NT):
                        mm = pe.transpose(ps[:, b, a * P:(a + 1) * P], src[:, a * P:(a + 1) * P], kc("ident"))
                    mm.then_inc(bk.full[b], 1)

            def scalar(act, own):
                full(act, use_al)
                full(act, use_dt)
                emptied(use_al, act.activation(al_raw, ps[0:LORA, 3, :], ACT.Copy))
                act.activation(sp_t[3][:, 0, :], vec("A_log"), ACT.Exp).then_inc(a_neg, 1)
                act.wait_ge(sp_abs, 1)
                act.activation(sp_t[1], sp_t[1], ACT.Exp, scale=-1.0).then_inc(sp_e, 1)
                act.wait_ge(sp_u, 1)
                act.activation(dt_s, sp_t[2], ACT.Ln).then_inc(sp_ln, 1)
                for n in range(3):
                    unit_done(act, seg_ssd + n)
                    emptied(ssd_uses[n][0], act.activation(flat(zT[:, 2 * n:2 * n + 2, :]), ps[:, n % 2, :], ACT.Silu))
                for n in range(3, 10):
                    unit_done(act, seg_ssd + n)
                    for o in range(2):
                        t = 2 * (n - 3) + o
                        r = t % 2
                        if t == 0:
                            act.wait_ge(pad_zero, 1)
                        if t >= 2:
                            act.wait_ge(conv5, t - 1)
                        if n < 8:
                            ins = act.activation(pads[:, r, :, 2:2 + T], ps[:, o, :].rearrange("p (c t) -> p c t", c=2), ACT.Copy)
                            emptied(ssd_uses[n][o], ins)
                        else:
                            ins = act.activation(pads[:, r, 0, 2:2 + T], ps[:, n % 2, o * T:(o + 1) * T], ACT.Copy)
                            if o == 1:
                                emptied(ssd_uses[n][0], ins)
                            else:
                                ins.then_inc(pad_in, 1)
                    if n >= 3:
                        for o in range(2):
                            t = 2 * (n - 3) + o
                            act.wait_ge(conv5, t + 1)
                            act.activation(conv_dst(t), conv_dst(t), ACT.Silu).then_inc(silu5, 1)
                full(act, use_cs)
                act.activation(cs_s, ps[:, 4, 0:NT * 2 * H2].rearrange("p (a c h) -> p a c h", a=NT, c=2)[:, :, 0, :], ACT.Copy)
                emptied(use_cs, act.activation(
                    tot_s, ps[:, 4, 0:NT * 2 * H2].rearrange("p (a c h) -> p a c h", a=NT, c=2)[:, :, 1, :], ACT.Copy))
                evacuated(act, use_cs)
                act.activation(ecs_s, cs_s, ACT.Exp).then_inc(exps_ready, 1)
                act.activation(etot_s, tot_s, ACT.Exp).then_inc(exps_ready, 1)
                act.activation(ncs_s, cs_s, ACT.Copy, scale=-1.0).then_inc(exps_ready, 1)
                act.wait_ge(dt_done, 1)
                act.activation(wdec_s, wdec_s, ACT.Exp).then_inc(exps_ready, 1)
                for a in range(TT):
                    full(act, use_cb[a])
                    emptied(use_cb[a], act.activation(cb_s[:, a, :], ps[:, 5 + a, :], ACT.Copy))
                for n in range(10):
                    full(act, use_tr[n])
                    src = ps[:, use_tr[n][0], :].rearrange("p (a n) -> p a n", a=NT)
                    dst = xs_tok[:, :, n * P:(n + 1) * P] if n < ST else b_tok[:, :, (n - ST) * P:(n - ST + 1) * P]
                    emptied(use_tr[n], act.activation(dst, src, ACT.Copy))

            def vector(dve, own):
                full(dve, use_dt)
                z, e, u, t = sp_t
                dve.wait_ge(a_neg, 1)
                own.step(dve.tensor_scalar(vec("A_log"), t[:, 0, :], -1.0, None, ALU.mult))
                emptied(use_dt, dve.tensor_tensor(z, ps[:, 4, 0:NT * H2].rearrange("p (a h) -> p a h", a=NT),
                                                  bc(vec("dt_bias"), NT), ALU.add))
                evacuated(dve, use_dt)
                dve.scalar_tensor_tensor(e, z, -1.0, z, ALU.mult, ALU.max).then_inc(sp_abs, 1)
                own.step(dve.memset(pads.rearrange("p r c t -> p (r c t)"), 0.0))
                own.settle()
                dve.sem_inc(pad_zero, 1)
                dve.wait_ge(sp_e, 1)
                dve.tensor_scalar(u, e, 1.0, None, ALU.add).then_inc(sp_u, 1)
                dve.wait_ge(sp_u, 1)
                own.step(dve.scalar_tensor_tensor(e, u, -1.0, e, ALU.add, ALU.subtract))
                own.step(dve.reciprocal(t, u))
                own.settle()
                own.step(dve.tensor_tensor(e, e, t, ALU.mult))
                own.settle()
                own.step(dve.scalar_tensor_tensor(e, z, 0.0, e, ALU.max, ALU.subtract))
                own.settle()
                dve.wait_ge(sp_ln, 1)
                own.step(dve.tensor_tensor(dt_s, dt_s, e, ALU.add))
                own.settle()
                dve.tensor_tensor(a_s, dt_s, bc(vec("A_log"), NT), ALU.mult).then_inc(a_ready, 1)
                for t in range(XT_TILES):
                    n = 3 + t // 2
                    if n < 8:
                        evacuated(dve, ssd_uses[n][t % 2])
                    elif t % 2:
                        evacuated(dve, ssd_uses[n][0])
                    else:
                        dve.wait_ge(pad_in, n - 7)
                    for k in range(SSD_TAPS):
                        if n < 8:
                            src = pads[:, t % 2, :, k:k + T]
                            dst = conv_dst(t).rearrange("p (c t) -> p c t", c=2)
                        else:
                            src, dst = pads[:, t % 2, 0, k:k + T], conv_dst(t)
                        tap = vec("ssd_cw", k * XT_TILES + t, k * XT_TILES + t + 1)
                        if k == 0:
                            own.step(dve.tensor_scalar(dst, src, tap, vec("ssd_cb", t, t + 1), ALU.mult, ALU.add))
                            own.settle()
                            continue
                        ins = dve.scalar_tensor_tensor(dst, src, tap, dst, ALU.mult, ALU.add)
                        if k < SSD_TAPS - 1:
                            own.step(ins)
                            own.settle()
                        else:
                            ins.then_inc(conv5, 1)
                evacuated(dve, use_cs)
                dve.tensor_tensor(wdec_s, tot_s, cs_s, ALU.subtract).then_inc(dt_done, 1)

        cb_s = w(S0 + 8704, TT * SSD_G * P, a=TT)
        st_s = w(S0 + 5632, 4 * SSD_DIM).rearrange("p (d a n) -> p d a n", d=2, a=TT)
        xdd = w(S0 + 1536, 2 * SSD_DIM, a=2)
        lq = w(RW0, 2 * 4 * P, a=2)
        mh = w((CT + FT) * T, SSD_H * P, a=SSD_H)
        HALF = SSD_DIM // 2
        ORDER = [[(2, False), (3, True), (0, True)], [(3, False), (2, True), (1, True)]]

        def heads_bc(col, n=SSD_P):
            return col.unsqueeze(2).to_broadcast([P, col.shape[-1], n])

        use_st = [[(bk.take(3 + 2 * d), bk.take(4 + 2 * d)) for d in range(2)] for _ in range(3)]
        use_l, use_y, use_off, use_yt = {}, {}, {}, {}
        for a in range(TT):
            for q in range(3):
                for d in range(2):
                    use_l[a, q, d] = bk.take((7, 3)[d])
            use_y[a] = (bk.take(4), bk.take(5))
            for d in range(2):
                use_off[a, d] = (bk.take(6), bk.take(7))
            use_yt[a] = (bk.take(3), bk.take(4))
        use_ssdvar = bk.take(5)
        xdd_ready, xdd_used, st_ready, l_ready, m_ready, y_ready, yz_ready, ysq, ssd_ready = (sem(n) for n in (
            "xdd_ready", "xdd_used", "st_ready", "l_ready", "m_ready", "y_ready", "yz_ready", "ysq", "ssd_ready"))
        srt = w(E0, T)
        ssq = w(S0 + 5632, ST * T, a=ST)

        class SsdScan:
            def tensor(pe, own):
                for n in range(3):
                    for d in range(2):
                        a = ORDER[d][n][0]
                        pe.wait_ge(xdd_ready, 2 * n + d + 1)
                        for h in range(2):
                            use = use_st[n][d][h]
                            acquire(pe, use)
                            for g in range(2):
                                mm = pe.matmul(ps[:, use[0], g * 192:(g + 1) * 192], b_tok[:, a, (2 * h + g) * P:(2 * h + g + 1) * P],
                                               xdd[:, d, (2 * h + g) * 192:(2 * h + g + 1) * 192], start=True, stop=True)
                            mm.then_inc(bk.full[use[0]], 1)
                for a in range(TT):
                    for q in range(3):
                        for d in range(2):
                            use = use_l[a, q, d]
                            acquire(pe, use)
                            pe.matmul(ps[:, use[0], :].rearrange("p (h t) -> p h t", h=4), kc("ident"), bc(kc(("neg_f", "neg_b")[d]), 4),
                                      start=True, stop=False)
                            for h in range(4):
                                col = d * SSD_H + 4 * q + h
                                mm = pe.matmul(ps[:, use[0], h * P:(h + 1) * P], a_s[:, a, col:col + 1].to_broadcast([P, P]),
                                               kc(("upto", "from")[d]), start=False, stop=h == 3)
                            mm.then_inc(bk.full[use[0]], 1)
                    for h in range(SSD_H):
                        pe.wait_ge(m_ready, a * SSD_H + h + 1)
                        b, at = 4 + h // 8, h % 8 * SSD_P
                        if h % 8 == 0:
                            acquire(pe, use_y[a][h // 8])
                        mm = pe.matmul(ps[:, b, at:at + SSD_P], mh[:, h, :], xs_tok[:, a, h * SSD_P:(h + 1) * SSD_P], start=True, stop=True)
                        if h in (7, SSD_H - 1):
                            mm.then_inc(bk.full[b], 1)
                    for d in range(2):
                        pe.wait_ge(st_ready, 6)
                        for h in range(2):
                            use = use_off[a, d][h]
                            acquire(pe, use)
                            for g in range(2):
                                gg = 2 * h + g
                                mm = pe.matmul(ps[:, use[0], g * 192:(g + 1) * 192], cT[:, gg, a * P:(a + 1) * P],
                                               st_s[:, d, a, gg * 192:(gg + 1) * 192], start=True, stop=True)
                            mm.then_inc(bk.full[use[0]], 1)
                    pe.wait_ge(y_ready, a + 1)
                    for n in range(ST):
                        use = use_yt[a][n // 4]
                        if n % 4 == 0:
                            acquire(pe, use)
                        mm = pe.transpose(ps[:, use[0], n % 4 * P:(n % 4 + 1) * P], y_s[:, n * P:(n + 1) * P], kc("ident"))
                        if n in (3, ST - 1):
                            mm.then_inc(bk.full[use[0]], 1)
                pe.wait_ge(ysq, 1)
                acquire(pe, use_ssdvar)
                for n in range(ST):
                    mm = pe.matmul(ps[:, 5, 0:T], kc("ones"), ssq[:, n, :], start=n == 0, stop=n == ST - 1)
                mm.then_inc(bk.full[5], 1)

            def scalar(act, own):
                act.wait_ge(exps_ready, 3)
                n = 0
                for a in range(TT):
                    for q in range(3):
                        for d in range(2):
                            use = use_l[a, q, d]
                            full(act, use)
                            if n >= 2:
                                act.wait_ge(m_ready, (n // 2) * 4)
                            for h in range(4):
                                col = d * SSD_H + 4 * q + h
                                ins = act.activation(lq[:, d, h * P:(h + 1) * P], ps[:, use[0], h * P:(h + 1) * P], ACT.Exp,
                                                     bias=ncs_s[:, a, col:col + 1])
                            emptied(use, ins)
                            n += 1
                act.wait_ge(yz_ready, 2)
                act.activation(flat(ssq), flat(zT), ACT.Square).then_inc(ysq, 1)
                full(act, use_ssdvar)
                emptied(use_ssdvar, act.activation(srt, ps[:, 5, 0:T], ACT.Sqrt, bias=eps(EPS_RMS), scale=1.0 / SSD_DIM))

            def vector(dve, own):
                dve.wait_ge(exps_ready, 4)
                own.step(dve.tensor_tensor(wdec_s, wdec_s, dt_s, ALU.mult))
                own.settle()
                for n in use_tr:
                    evacuated(dve, n)
                for n in range(3):
                    for d in range(2):
                        a = ORDER[d][n][0]
                        if n:
                            for h in range(2):
                                full(dve, use_st[n - 1][d][h])
                        dve.tensor_tensor(xdd[:, d, :].rearrange("p (h c) -> p h c", c=SSD_P),
                                          xs_tok[:, a, :].rearrange("p (h c) -> p h c", c=SSD_P),
                                          heads_bc(wdec_s[:, a, d * SSD_H:(d + 1) * SSD_H]), ALU.mult).then_inc(xdd_ready, 1)
                    for d in range(2):
                        a = ORDER[d][n][0]
                        first = (0, 1)[d]
                        src = None if n == 0 else st_s[:, d, first, :]
                        dst = st_s[:, d, first if n < 2 else 1 - first, :]
                        if src is not None:
                            own.step(dve.tensor_tensor(dst.rearrange("p (h c) -> p h c", c=SSD_P), src.rearrange("p (h c) -> p h c", c=SSD_P),
                                                       heads_bc(etot_s[:, a, d * SSD_H:(d + 1) * SSD_H]), ALU.mult))
                            own.settle()
                        for h in range(2):
                            use = use_st[n][d][h]
                            full(dve, use)
                            part = dst[:, h * HALF:(h + 1) * HALF]
                            if src is None:
                                ins = dve.tensor_copy(part, ps[:, use[0], 0:HALF])
                            else:
                                ins = dve.tensor_tensor(part, part, ps[:, use[0], 0:HALF], ALU.add)
                            emptied(use, ins)
                        for h in range(2):
                            evacuated(dve, use_st[n][d][h])
                        dve.sem_inc(st_ready, 1)
                for a in range(TT):
                    for q in range(3):
                        evacuated(dve, use_l[a, q, 0])
                        evacuated(dve, use_l[a, q, 1])
                        for h in range(4):
                            hh = 4 * q + h
                            if a and hh in (0, 8):
                                full(dve, use_y[a - 1][hh // 8])
                            own.step(dve.tensor_scalar(mh[:, hh, :], lq[:, 0, h * P:(h + 1) * P], dt_s[:, a, hh:hh + 1], None, ALU.mult))
                            own.settle()
                            own.step(dve.scalar_tensor_tensor(mh[:, hh, :], lq[:, 1, h * P:(h + 1) * P],
                                                              dt_s[:, a, SSD_H + hh:SSD_H + hh + 1], mh[:, hh, :], ALU.mult, ALU.add))
                            own.settle()
                            g = hh // 3
                            dve.tensor_tensor(mh[:, hh, :], mh[:, hh, :], cb_s[:, a, g * P:(g + 1) * P], ALU.mult).then_inc(m_ready, 1)
                    if a:
                        for u in use_yt[a - 1]:
                            full(dve, u)
                    own.step(dve.tensor_tensor(y_s.rearrange("p (h c) -> p h c", c=SSD_P), xs_tok[:, a, :].rearrange("p (h c) -> p h c", c=SSD_P),
                                               heads_bc(vec("ssd_D")), ALU.mult))
                    own.settle()
                    for i, (lo, hi) in enumerate(((0, 512), (512, SSD_DIM))):
                        full(dve, use_y[a][i])
                        emptied(use_y[a][i], dve.tensor_tensor(y_s[:, lo:hi], y_s[:, lo:hi], ps[:, 4 + i, 0:hi - lo], ALU.add))
                    for i in range(2):
                        evacuated(dve, use_y[a][i])
                    for d in range(2):
                        for i in range(2):
                            use = use_off[a, d][i]
                            full(dve, use)
                            for h in range(6):
                                hh = 6 * i + h
                                part = y_s[:, hh * SSD_P:(hh + 1) * SSD_P]
                                ins = dve.scalar_tensor_tensor(part, ps[:, use[0], h * SSD_P:(h + 1) * SSD_P],
                                                               ecs_s[:, a, d * SSD_H + hh:d * SSD_H + hh + 1], part, ALU.mult, ALU.add)
                                if h < 5:
                                    own.step(ins)
                            emptied(use, ins)
                        for i in range(2):
                            evacuated(dve, use_off[a, d][i])
                    dve.sem_inc(y_ready, 1)
                    for i, (lo, hi) in enumerate(((0, 4), (4, ST))):
                        use = use_yt[a][i]
                        full(dve, use)
                        part = zT[:, lo:hi, a * P:(a + 1) * P]
                        emptied(use, dve.tensor_tensor(part, part, ps[:, use[0], 0:(hi - lo) * P].rearrange("p (n t) -> p n t", t=P), ALU.mult))
                    for u in use_yt[a]:
                        evacuated(dve, u)
                    dve.sem_inc(yz_ready, 1)
                evacuated(dve, use_ssdvar)
                own.step(dve.reciprocal(srt, srt))
                own.settle()
                for n in range(ST):
                    dve.scalar_tensor_tensor(ssdT[:, n, :], zT[:, n, :], vec("ssd_ng", n, n + 1), srt, ALU.mult, ALU.mult).then_inc(ssd_ready, 1)

        R0 = W0
        kT = w(R0, RT * 2 * T, a=RT)
        v_tok = w(R0 + 2048, NT * RW_DIM, a=NT)
        lora_t = w(R0 + 4096, 2 * T)
        G0 = R0 + 4608
        PADR = T + 2
        rpads = w(G0, 2 * 2 * PADR).rearrange("p (r c t) -> p r c t", r=2, c=2)
        vT = w(G0 + 1032, RT * 2 * T, a=RT)
        aT = w(G0 + 3080, RT * 2 * T, a=RT)
        sq_r = w(G0 + 5128, 2 * 2 * T, a=2)
        t1_r = w(G0 + 6152, 2 * T)
        assert G0 + 6152 + 2 * T <= E0 + SSD_DIM + 8 * NT * H2
        gl_r = w(RW0, T)
        rt_r = w(RW0 + T, 2 * T)
        rT = xflat[:, 0:RT * T].rearrange("p (a t) -> p a t", a=RT)
        bonusT = xflat[:, RT * T:2 * RT * T].rearrange("p (a t) -> p a t", a=RT)
        gT = xflat[:, 2 * RT * T:3 * RT * T].rearrange("p (a t) -> p a t", a=RT)
        y_tok = xflat[:, 3 * RT * T:].rearrange("p (a n) -> p a n", a=TT)

        def kkT(j):
            return hT[:, j:j + RT + 1:RT, T:]

        def kaT(j):
            return hT[:, 2 * RT + j:3 * RT + j + 1:RT, T:]

        seg_rw = segment(7)
        rw_uses = [[bk.take(n % 2)] for n in range(2)] + [[bk.take(0), bk.take(1)] for _ in range(5)]
        rot = [0]

        def aux():
            rot[0] += 1
            return bk.take(3 + rot[0] % 5)

        use_vt = [aux() for _ in range(NT)]
        use_a = [aux() for _ in range(RT)]
        use_g = [aux() for _ in range(2)]
        use_kk = [aux() for _ in range(RT)]
        use_bonus = [aux() for _ in range(2)]
        rpad_zero, rpad_in, shifted, lora_ready, al_ready, gl_ready, kk_raw, kk_sq, rt_ready, kk_ready, rk_ready, prep_ready = (sem(n) for n in (
            "rpad_zero", "rpad_in", "shifted", "lora_ready", "al_ready", "gl_ready", "kk_raw", "kk_sq", "rt_ready", "kk_ready", "rk_ready",
            "prep_ready"))
        R_TILES = 15

        def shift_dst(t):
            if t < RT:
                return rT[:, t, :]
            if t < 2 * RT:
                return kT[:, t - RT, :]
            if t < 3 * RT:
                return vT[:, t - 2 * RT, :]
            return (lora_t, gl_r, al_raw)[t - 3 * RT]

        class RwIn:
            def sync(sp):
                fetch(sp, rw_u, seg_rw, 7)

            def tensor(pe, own):
                for n in range(7):
                    both = n >= 2
                    outs = [ps[:, 0, :], ps[:, 1, :]] if both else pair(n % 2)
                    gemm_unit(pe, seg_rw + n, both_rhs if both else main_rhs, outs, rw_uses[n])
                for a in range(NT):
                    pe.wait_ge(shifted, 3 * RT)
                    acquire(pe, use_vt[a])
                    for j in range(RT):
                        mm = pe.transpose(ps[:, use_vt[a][0], j * P:(j + 1) * P], vT[:, j, a * P:(a + 1) * P], kc("ident"))
                    mm.then_inc(bk.full[use_vt[a][0]], 1)
                pe.wait_ge(al_ready, 1)
                for j in range(RT):
                    acquire(pe, use_a[j])
                    pe.matmul(ps[:, use_a[j][0], :], small("a2", LORA)[:, j * P:(j + 1) * P], al_raw, start=True, stop=True)\
                        .then_inc(bk.full[use_a[j][0]], 1)
                pe.wait_ge(gl_ready, 1)
                for j in range(RT):
                    use = use_g[j // 2]
                    if j % 2 == 0:
                        acquire(pe, use)
                    mm = pe.matmul(ps[:, use[0], j % 2 * T:(j % 2 + 1) * T], small("g2")[:, j * P:(j + 1) * P], gl_r, start=True, stop=True)
                    if j % 2:
                        mm.then_inc(bk.full[use[0]], 1)
                for j in range(RT):
                    pe.wait_ge(kk_sq, j + 1)
                    acquire(pe, use_kk[j])
                    pe.matmul(ps[:, use_kk[j][0], :], kc("blk"), sq_r[:, j % 2, :], start=True, stop=True).then_inc(bk.full[use_kk[j][0]], 1)
                for j in range(RT):
                    use = use_bonus[j // 2]
                    if j % 2 == 0:
                        acquire(pe, use)
                    pe.wait_ge(rk_ready, j + 1)
                    mm = pe.matmul(ps[:, use[0], j % 2 * T:(j % 2 + 1) * T], kc("blk"), sq_r[:, j % 2, 0:T], start=True, stop=True)
                    if j % 2:
                        mm.then_inc(bk.full[use[0]], 1)

            def scalar(act, own):
                act.wait_ge(rpad_zero, 1)
                for t in range(R_TILES):
                    n, o = t // 2, t % 2
                    rows = P if t < 14 else LORA
                    pad = rpads[0:rows, t % 2]
                    if t >= 2:
                        act.wait_ge(shifted, t - 1)
                    if t < 14:
                        unit_done(act, seg_rw + n)
                        src = ps[:, n % 2, o * T:(o + 1) * T] if n < 2 else ps[:, o, :]
                    else:
                        src = al_raw
                    ctx_too = n >= 2 and t != 13
                    ins = act.activation(pad[:, 0, 1:1 + T].rearrange("p (w r) -> p r w", r=ROWS),
                                         src[:, 0:T].rearrange("p (r w) -> p r w", r=ROWS), ACT.Copy)
                    if ctx_too:
                        ins.then_inc(rpad_in, 1)
                        ins = act.activation(pad[:, 1, 1:1 + T], src[:, T:], ACT.Copy)
                    if t < 14 and not (n < 2 and o == 0):
                        emptied(rw_uses[n][o if n >= 2 else 0], ins)
                    else:
                        ins.then_inc(rpad_in, 1)
                act.wait_ge(shifted, 13)
                act.activation(lora_t, lora_t, ACT.Tanh).then_inc(lora_ready, 1)
                act.wait_ge(shifted, 14)
                act.activation(gl_r, gl_r, ACT.Sigmoid).then_inc(gl_ready, 1)
                for a in range(NT):
                    full(act, use_vt[a])
                    emptied(use_vt[a], act.activation(v_tok[:, a, :], ps[:, use_vt[a][0], :], ACT.Copy))
                for j in range(RT):
                    full(act, use_a[j])
                    emptied(use_a[j], act.activation(aT[:, j, :], ps[:, use_a[j][0], :], ACT.Sigmoid, bias=vec("a0", j, j + 1)))
                for i in range(2):
                    full(act, use_g[i])
                    emptied(use_g[i], act.activation(flat(gT[:, 2 * i:2 * i + 2, :]), ps[:, use_g[i][0], :], ACT.Copy))
                for j in range(RT):
                    act.wait_ge(kk_raw, j + 1)
                    if j >= 2:
                        full(act, use_kk[j - 2])
                    act.activation(sq_r[:, j % 2, :].rearrange("p (c t) -> p c t", c=2), kkT(j), ACT.Square).then_inc(kk_sq, 1)
                for j in range(RT):
                    full(act, use_kk[j])
                    if j >= 1:
                        act.wait_ge(kk_ready, j)
                    emptied(use_kk[j], act.activation(rt_r, ps[:, use_kk[j][0], :], ACT.Sqrt, bias=eps(EPS_KK)))

            def vector(dve, own):
                dve.wait_ge(ssd_ready, ST)
                own.step(dve.memset(rpads.rearrange("p r c t -> p (r c t)"), 0.0))
                own.settle()
                dve.sem_inc(rpad_zero, 1)
                pads_in = 0
                for t in range(R_TILES):
                    n, o = t // 2, t % 2
                    rows = P if t < 14 else LORA
                    ctx_too = n >= 2 and t != 13
                    pads_in += ctx_too
                    if t < 14 and not (n < 2 and o == 0):
                        evacuated(dve, rw_uses[n][o if n >= 2 else 0])
                    else:
                        pads_in += 1
                    if pads_in:
                        dve.wait_ge(rpad_in, pads_in)
                    c = 2 if ctx_too else 1
                    pad = rpads[0:rows, t % 2, 0:c]
                    mid = pad[:, :, 1:1 + T]
                    tmp = t1_r[0:rows, 0:c * T].rearrange("p (c t) -> p c t", c=c)
                    dst = shift_dst(t).rearrange("p (c t) -> p c t", c=c)
                    own.settle()
                    if t:
                        dve.wait_ge(shifted, t)
                    own.step(dve.tensor_tensor(tmp, pad[:, :, 0:T], pad[:, :, 2:2 + T], ALU.add))
                    own.settle()
                    own.step(dve.scalar_tensor_tensor(tmp, tmp, 0.5, mid, ALU.mult, ALU.subtract))
                    own.settle()
                    dve.scalar_tensor_tensor(dst, tmp, vec("mu", t, t + 1)[0:rows], mid, ALU.mult, ALU.add).then_inc(shifted, 1)
                dve.wait_ge(shifted, R_TILES)
                dve.sem_inc(al_ready, 1)
                for j in range(RT):
                    own.step(dve.tensor_scalar(kkT(j), kT[:, j, :].rearrange("p (c t) -> p c t", c=2), vec("k_k", j, j + 1), None, ALU.mult))
                    own.settle()
                    dve.sem_inc(kk_raw, 1)
                for j in range(RT):
                    evacuated(dve, use_kk[j])
                    own.step(dve.reciprocal(rt_r, rt_r))
                    own.settle()
                    dve.tensor_tensor(kkT(j), kkT(j), rt_r.rearrange("p (c t) -> p c t", c=2), ALU.mult).then_inc(kk_ready, 1)
                dve.wait_ge(kk_ready, RT)
                for j in range(RT):
                    evacuated(dve, use_a[j])
                    a2 = aT[:, j, :].rearrange("p (c t) -> p c t", c=2)
                    own.step(dve.tensor_tensor(kaT(j), kkT(j), a2, ALU.mult))
                    own.settle()
                    own.step(dve.tensor_scalar(aT[:, j, :], aT[:, j, :], 1.0, vec("k_a", j, j + 1), ALU.subtract, ALU.mult))
                    own.settle()
                    own.step(dve.scalar_tensor_tensor(kT[:, j, :], aT[:, j, :], 1.0, kT[:, j, :], ALU.add, ALU.mult))
                    own.settle()
                    if j >= 2:
                        full(dve, use_bonus[0])
                    dve.scalar_tensor_tensor(sq_r[:, j % 2, 0:T], rT[:, j, :], vec("r_k", j, j + 1), kT[:, j, 0:T], ALU.mult, ALU.mult)\
                        .then_inc(rk_ready, 1)
                for i in range(2):
                    full(dve, use_bonus[i])
                    emptied(use_bonus[i], dve.tensor_tensor(bonusT[:, 2 * i:2 * i + 2, :],
                                                            ps[:, use_bonus[i][0], :].rearrange("p (a t) -> p a t", a=2),
                                                            vT[:, 2 * i:2 * i + 2, 0:T], ALU.mult))
                    evacuated(dve, use_bonus[i])
                dve.sem_inc(prep_ready, 1)

        CH = T // RW_C
        UN = 4 * P

        def d_mem(d):
            if d == 0:
                at = G0
                e = [w(at + n * T, T) for n in range(5)]
                return e, [w(at + 1280 + n * T, TT * P, a=TT) for n in range(2)], w(at + 1792, CH * RW_N, a=CH)
            free = WORK - SMALL_N + SMALLS["a2"][0]
            e = [w(RW0 + n * T, T) for n in range(4)] + [w(free, T)]
            return e, [w(free + T + n * T, TT * P, a=TT) for n in range(2)], w(G0 + 2048, CH * RW_N, a=CH)

        assert G0 + 2304 + 10 * UN <= WORK - SMALL_N + SMALLS["w2"][0]
        MEM = [d_mem(d) for d in range(2)]
        BIG = [[w(G0 + 2304 + (5 * h + n) * UN, UN) for n in range(5)] for h in range(2)]
        ROUNDS = [(j, half) for j in range(RT) for half in (1, 0)]
        rsem = {n: [sem(f"{n}{d}") for d in range(2)] for n in ("dec_sum", "dec_exp", "abkr", "t_init", "q_ready", "s_zero")}
        rounds = []
        for r, (j, half) in enumerate(ROUNDS):
            u = dict(z=[aux() for _ in range(2)], m=[], mt=[])
            for h in range(2):
                u["mt"].append(aux())
                u["m"].append(aux())
            u["bt"] = [aux() for _ in range(2)]
            u["lev"] = []
            for s in LEVELS[1:]:
                x = [aux() for _ in range(2)]
                tx, xt = [], []
                for h in range(2):
                    tx.append(aux() if s != LEVELS[-1] else None)
                    xt.append(aux())
                u["lev"].append((x, tx, xt))
            u["at"] = aux()
            u["nt"] = [[aux() for _ in range(1 if half else 3)] for _ in range(2)]
            u["nv"] = [aux() for _ in range(2)]
            u["tav"] = [aux() for _ in range(2)]
            u["du"] = [aux() for _ in range(2)]
            u["rh"] = [aux() for _ in range(2)] if not half else None
            u["s"] = [[aux() for _ in range(2)] for _ in range(CH if half else CH - 1)]
            u["y"] = [aux() for _ in range(2)] if not half else None
            rounds.append(u)

        def chunks(d):
            return list(range(CH)) if d == 0 else list(range(CH - 1, -1, -1))

        def blk4(i):
            return slice(i * P, (i + 1) * P)

        def hrows(i):
            return slice(i * RW_N, (i + 1) * RW_N)

        def da(v):
            return v.rearrange("p (d a t) -> p d a t", d=2, a=TT)

        def mask_da(name, swap=False):
            o = CONSTS[name + "0"][0]
            m = K[:, o:o + 2 * P].rearrange("p (d t) -> p d t", d=2)
            if swap:
                m = m[:, ::-1, :]
            return m.unsqueeze(2).to_broadcast([P, 2, TT, P])

        def ident_da():
            return kc("ident").unsqueeze(1).unsqueeze(1).to_broadcast([P, 2, TT, P])

        UNITS = [(d, a) for d in range(2) for a in range(TT)]

        class RwScan:
            def tensor(pe, own):
                pe.wait_ge(prep_ready, 1)
                pe.wait_ge(lora_ready, 1)
                for r, (j, half) in enumerate(ROUNDS):
                    u = rounds[r]

                    def v_of(h, a, rows=slice(0, P)):
                        return v_tok[rows, half * TT + a, j * P + h * RW_N:j * P + (h + 1) * RW_N]

                    def products(use, h, left, right):
                        acquire(pe, use)
                        for i, (d, a) in enumerate(UNITS):
                            mm = pe.matmul(ps[:, use[0], blk4(i)], MEM[d][0][left][hrows(h), blk4(a)], MEM[d][0][right][hrows(h), blk4(a)],
                                           start=True, stop=True)
                        mm.then_inc(bk.full[use[0]], 1)

                    def squares(use, left, right):
                        acquire(pe, use)
                        for i in range(4):
                            mm = pe.matmul(ps[:, use[0], blk4(i)], left[:, blk4(i)], right[:, blk4(i)], start=True, stop=True)
                        mm.then_inc(bk.full[use[0]], 1)

                    for d in range(2):
                        acquire(pe, u["z"][d])
                        pe.matmul(ps[:, u["z"][d][0], 0:T], small("w2")[d * LORA:(d + 1) * LORA, j * P:(j + 1) * P],
                                  lora_t[d * LORA:(d + 1) * LORA, half * T:(half + 1) * T], start=True, stop=True)\
                            .then_inc(bk.full[u["z"][d][0]], 1)
                    for d in range(2):
                        pe.wait_ge(rsem["abkr"][d], r + 1)
                    for h in range(2):
                        products(u["mt"][h], h, 1, 0)
                        products(u["m"][h], h, 0, 1)
                    for d in range(2):
                        A, B, E, Kd, R = MEM[d][0]
                        use = u["bt"][d]
                        acquire(pe, use)
                        for a in range(TT):
                            pe.transpose(ps[:, use[0], blk4(a)], B[:, blk4(a)], kc("ident"))
                            mm = pe.transpose(ps[:, use[0], blk4(2 + a)], Kd[:, blk4(a)], kc("ident"))
                        mm.then_inc(bk.full[use[0]], 1)
                    for n, (x, tx, xt) in enumerate(u["lev"]):
                        for h in range(2):
                            MT, Tm, Tt, X, Q = BIG[h]
                            pe.wait_ge(rsem["q_ready"][h], 5 * r + n + 1)
                            if n == 0:
                                pe.wait_ge(rsem["t_init"][h], 2 * r + 2)
                            else:
                                evacuated(pe, u["lev"][n - 1][1][h])
                                evacuated(pe, u["lev"][n - 1][2][h])
                            squares(x[h], Q, Tm)
                        for h in range(2):
                            MT, Tm, Tt, X, Q = BIG[h]
                            evacuated(pe, x[h])
                            if tx[h] is not None:
                                squares(tx[h], Tt, X)
                            squares(xt[h], X, Tt)
                    use = u["at"]
                    acquire(pe, use)
                    for i, (d, a) in enumerate(UNITS):
                        mm = pe.transpose(ps[:, use[0], blk4(i)], MEM[d][0][0][:, blk4(a)], kc("ident"))
                    mm.then_inc(bk.full[use[0]], 1)
                    for h in range(2):
                        for use, (left, right) in zip(u["nt"][h], ((3, 0), (1, 4), (3, 4))):
                            products(use, h, left, right)
                    for h in range(2):
                        use = u["nv"][h]
                        evacuated(pe, u["nt"][h][0])
                        acquire(pe, use)
                        for i, (d, a) in enumerate(UNITS):
                            mm = pe.matmul(ps[:, use[0], i * RW_N:(i + 1) * RW_N], BIG[h][0][:, blk4(i)], v_of(h, a), start=True, stop=True)
                        mm.then_inc(bk.full[use[0]], 1)
                    evacuated(pe, u["at"])
                    for h in range(2):
                        evacuated(pe, u["nv"][h])
                        evacuated(pe, u["lev"][-1][2][h])
                        squares(u["tav"][h], BIG[h][2], BIG[h][4])
                    for n in range(2):
                        evacuated(pe, u["tav"][n])
                        evacuated(pe, u["bt"][n])
                    for odd in range(2):
                        use = u["du"][odd]
                        acquire(pe, use)
                        rows = hrows(odd)
                        for h in range(2):
                            nta = BIG[h][0]
                            for i, (d, a) in enumerate(UNITS):
                                b_t, k_t = MEM[d][1]
                                to = slice(i * RW_N, (i + 1) * RW_N)
                                pe.matmul(ps[hrows(h), use[0], to], nta[rows, i * P:i * P + RW_N], b_t[rows, a, hrows(h)], start=True, stop=True)
                                to = slice((4 + i) * RW_N, (5 + i) * RW_N)
                                pe.matmul(ps[hrows(h), use[0], to], k_t[rows, a, hrows(h)], v_of(h, a, rows), start=True, stop=False)
                                mm = pe.matmul(ps[hrows(h), use[0], to], b_t[rows, a, hrows(h)], nta[rows, i * P + RW_N:(i + 1) * P],
                                               start=False, stop=True)
                        mm.then_inc(bk.full[use[0]], 1)
                    if not half:
                        for h in range(2):
                            evacuated(pe, u["nt"][h][1])
                        for d in range(2):
                            use = u["rh"][d]
                            acquire(pe, use)
                            for h in range(2):
                                for a in range(TT):
                                    i = TT * d + a
                                    mm = pe.matmul(ps[hrows(h), use[0], blk4(a)], BIG[h][0][:, i * P:i * P + RW_N], BIG[h][1][:, blk4(i)],
                                                   start=True, stop=True)
                            mm.then_inc(bk.full[use[0]], 1)
                    for odd in range(2):
                        evacuated(pe, u["du"][odd])
                    for n in range(len(u["s"])):
                        for d in range(2):
                            st = MEM[d][2]
                            c = chunks(d)[n]
                            i = TT * d + c // 2
                            use = u["s"][n][d]
                            if n:
                                evacuated(pe, u["s"][n - 1][d])
                            elif half:
                                pe.wait_ge(rsem["s_zero"][d], j + 1)
                            else:
                                evacuated(pe, rounds[r - 1]["s"][CH - 1][d])
                            acquire(pe, use)
                            for h in range(2):
                                mm = pe.matmul(ps[hrows(h), use[0], 0:RW_N], BIG[c % 2][4][hrows(h), i * RW_N:(i + 1) * RW_N], st[hrows(h), n, :],
                                               start=True, stop=True)
                            mm.then_inc(bk.full[use[0]], 1)
                    if not half:
                        for d in range(2):
                            evacuated(pe, u["rh"][d])
                            evacuated(pe, u["s"][CH - 2][d])
                        for h in range(2):
                            nta, rb, _, rk, _ = BIG[h]
                            use = u["y"][h]
                            evacuated(pe, u["nt"][h][2])
                            acquire(pe, use)
                            for a in range(TT):
                                to = slice(a * RW_N, (a + 1) * RW_N)
                                for d in range(2):
                                    i = TT * d + a
                                    pe.matmul(ps[:, use[0], to], rk[:, blk4(i)], v_of(h, a), start=d == 0, stop=False)
                                    pe.matmul(ps[:, use[0], to], rb[:, blk4(i)], nta[:, i * P + RW_N:(i + 1) * P], start=False, stop=False)
                                for d in range(2):
                                    for odd in range(2):
                                        c = 2 * a + odd
                                        mm = pe.matmul(ps[hrows(odd), use[0], to], MEM[d][0][1][hrows(h), c * RW_C:(c + 1) * RW_C],
                                                       MEM[d][2][hrows(h), chunks(d).index(c), :], start=False, stop=d == 1)
                            mm.then_inc(bk.full[use[0]], 1)

            def scalar(act, own):
                act.wait_ge(prep_ready, 1)
                for r, (j, half) in enumerate(ROUNDS):
                    u = rounds[r]
                    if r:
                        last = rounds[r - 1]
                        for n in range(2):
                            full(act, last["du"][n])
                            if last["y"]:
                                full(act, last["y"][n])
                    for d in range(2):
                        full(act, u["z"][d])
                        emptied(u["z"][d], act.activation(MEM[d][0][0], ps[:, u["z"][d][0], 0:T], ACT.Sigmoid,
                                                          bias=vec("w0", d * RT + j, d * RT + j + 1)))
                    for d in range(2):
                        A, B, E, Kd, R = MEM[d][0]
                        act.wait_ge(rsem["dec_sum"][d], r + 1)
                        act.activation(A, A, ACT.Exp, scale=-DECAY).then_inc(rsem["dec_exp"][d], 1)
                        act.activation(Kd, B, ACT.Exp, scale=DECAY).then_inc(rsem["dec_exp"][d], 1)
                        act.activation(E, B, ACT.Exp, scale=-DECAY).then_inc(rsem["dec_exp"][d], 1)
                    for h in range(2):
                        full(act, u["mt"][h])
                        emptied(u["mt"][h], act.activation(BIG[h][0], ps[:, u["mt"][h][0], :], ACT.Copy))
                    for d in range(2):
                        b_t, k_t = MEM[d][1]
                        use = u["bt"][d]
                        full(act, use)
                        own.step(act.activation(b_t, ps[:, use[0], 0:2 * P].rearrange("p (a n) -> p a n", a=TT), ACT.Copy))
                        emptied(use, act.activation(k_t, ps[:, use[0], 2 * P:].rearrange("p (a n) -> p a n", a=TT), ACT.Copy))
                    for n, (x, tx, xt) in enumerate(u["lev"]):
                        for h in range(2):
                            full(act, x[h])
                            emptied(x[h], act.activation(BIG[h][3], ps[:, x[h][0], :], ACT.Copy))
                    for h in range(2):
                        use = u["nv"][h]
                        full(act, use)
                        rhs = BIG[h][4].rearrange("p (u n) -> p u n", u=4)
                        emptied(use, act.activation(rhs[:, :, RW_N:], ps[:, use[0], 0:4 * RW_N].rearrange("p (u n) -> p u n", u=4), ACT.Copy))
                    for h in range(2):
                        use = u["tav"][h]
                        full(act, use)
                        emptied(use, act.activation(BIG[h][0], ps[:, use[0], :], ACT.Copy, scale=-1.0))

            def vector(dve, own):
                for r, (j, half) in enumerate(ROUNDS):
                    u = rounds[r]
                    if half:
                        for d in range(2):
                            own.step(dve.memset(MEM[d][2][:, 0, :], 0.0))
                            own.settle()
                            dve.sem_inc(rsem["s_zero"][d], 1)
                    for d in range(2):
                        A, B, E, Kd, R = MEM[d][0]
                        evacuated(dve, u["z"][d])
                        step = 1 if d == 0 else -1
                        own.step(dve.tensor_tensor_scan(B[:, ::step], kc(f"reset{d}")[:, ::step], A[:, ::step], 0.0, ALU.mult, ALU.add))
                        own.settle()
                        dve.tensor_tensor(A, B, A, ALU.subtract).then_inc(rsem["dec_sum"][d], 1)
                    for d in range(2):
                        A, B, E, Kd, R = MEM[d][0]
                        dve.wait_ge(rsem["dec_exp"][d], 3 * r + 3)
                        own.step(dve.tensor_tensor(A, A, kkT(j)[:, half, :], ALU.mult))
                        own.step(dve.tensor_tensor(B, Kd, kaT(j)[:, half, :], ALU.mult))
                        if not half:
                            own.step(dve.tensor_tensor(R, E, rT[:, j, :], ALU.mult))
                        own.settle()
                        dve.tensor_tensor(Kd, Kd, kT[:, j, half * T:(half + 1) * T], ALU.mult).then_inc(rsem["abkr"][d], 1)
                    for h in range(2):
                        Tm = da(BIG[h][1])
                        use = u["m"][h]
                        full(dve, use)
                        emptied(use, dve.tensor_tensor(Tm, da(ps[:, use[0], :]), mask_da("lev1_", swap=True), ALU.mult))
                        evacuated(dve, use)
                        dve.tensor_tensor(Tm, Tm, ident_da(), ALU.add).then_inc(rsem["t_init"][h], 1)
                    for n, (x, tx, xt) in enumerate(u["lev"]):
                        for h in range(2):
                            full(dve, xt[h])
                            for use, m in ((tx[h], BIG[h][1]), (xt[h], BIG[h][2])):
                                if use is not None:
                                    full(dve, use)
                                    emptied(use, dve.tensor_tensor(m, m, ps[:, use[0], :], ALU.subtract))
                    use = u["at"]
                    full(dve, use)
                    for h in range(2):
                        rhs = BIG[h][4].rearrange("p (u n) -> p u n", u=4)
                        ins = dve.tensor_copy(rhs[:, :, 0:RW_N], ps[:, use[0], :].rearrange("p (u n) -> p u n", u=4)[:, :, hrows(h)])
                        if h == 0:
                            own.step(ins)
                    emptied(use, ins)
                    for h in range(2):
                        for use, m, mask in zip(u["nt"][h], (BIG[h][0], BIG[h][1], BIG[h][3]), ("strict", "incl", "incl")):
                            full(dve, use)
                            emptied(use, dve.tensor_tensor(da(m), da(ps[:, use[0], :]), mask_da(mask), ALU.mult))
                    for odd in range(2):
                        use = u["du"][odd]
                        full(dve, use)
                        dt_m, u_m = (BIG[odd][4][:, n * 4 * RW_N:(n + 1) * 4 * RW_N].rearrange("p (u n) -> p u n", u=4) for n in range(2))
                        src = ps[:, use[0], :].rearrange("p (u n) -> p u n", n=RW_N)
                        own.step(dve.tensor_tensor(dt_m, src[:, 0:4, :], bc(kc("eye64"), 4), ALU.add))
                        for d in range(2):
                            end = odd * RW_C + (RW_C - 1 if d == 0 else 0)
                            ins = dve.tensor_tensor(u_m[:, TT * d:TT * d + TT, :], src[:, 4 + TT * d:4 + TT * d + TT, :],
                                                    heads_bc(MEM[d][0][2][:, end:end + P + 1:P], RW_N), ALU.mult)
                            if d == 0:
                                own.step(ins)
                        emptied(use, ins)
                    if not half:
                        for d in range(2):
                            use = u["rh"][d]
                            full(dve, use)
                            emptied(use, dve.tensor_tensor(MEM[d][0][1], ps[:, use[0], 0:T], MEM[d][0][4], ALU.add))
                    for odd in range(2):
                        evacuated(dve, u["du"][odd])
                    for n in range(len(u["s"])):
                        for d in range(2):
                            c = chunks(d)[n]
                            use = u["s"][n][d]
                            E, st = MEM[d][0][2], MEM[d][2]
                            at = c * RW_C + (RW_C - 1 if d == 0 else 0)
                            i = 4 + TT * d + c // 2
                            full(dve, use)
                            emptied(use, dve.scalar_tensor_tensor(st[:, (n + 1) % CH, :], ps[:, use[0], 0:RW_N], E[:, at:at + 1],
                                                                  BIG[c % 2][4][:, i * RW_N:(i + 1) * RW_N], ALU.mult, ALU.add))
                    if not half:
                        for h in range(2):
                            use = u["y"][h]
                            full(dve, use)
                            emptied(use, dve.tensor_copy(y_tok[:, :, j * P + h * RW_N:j * P + (h + 1) * RW_N],
                                                         ps[:, use[0], 0:P].rearrange("p (a n) -> p a n", a=TT)))

            def gpsimd(pool, own):
                pool.wait_ge(consts_in, 16)
                for r, (j, half) in enumerate(ROUNDS):
                    u = rounds[r]
                    if r:
                        for d in range(2):
                            evacuated(pool, rounds[r - 1]["s"][-1][d])
                    for h in range(2):
                        MT, _, Tt, _, Q = (da(v) for v in BIG[h])
                        evacuated(pool, u["mt"][h])
                        own.step(pool.tensor_tensor(Tt, MT, mask_da("lev1_"), ALU.mult))
                        pool.tensor_tensor(Q, MT, mask_da("lev2_"), ALU.mult).then_inc(rsem["q_ready"][h], 1)
                        own.settle()
                        pool.tensor_tensor(Tt, Tt, ident_da(), ALU.add).then_inc(rsem["t_init"][h], 1)
                    for n, s in enumerate(LEVELS[2:]):
                        for h in range(2):
                            full(pool, u["lev"][n][0][h])
                            pool.tensor_tensor(da(BIG[h][4]), da(BIG[h][0]), mask_da(f"lev{s}_"), ALU.mult).then_inc(rsem["q_ready"][h], 1)

        use_gt = [aux() for _ in range(2 * TT)]
        gn = w(G0, 4 * TT * RW_H).rearrange("p (i a h) -> p i a h", i=4, a=TT)
        gsq = w(G0 + 64, TT * RW_DIM, a=TT)
        yT = w(G0 + 64 + TT * RW_DIM, RT * T, a=RT)
        gn_sq, gn_rt, gn_y, yt_aff, rw_ready = (sem(n) for n in ("gn_sq", "gn_rt", "gn_y", "yt_aff", "rw_ready"))

        class RwOut:
            def tensor(pe, own):
                pe.wait_ge(gn_y, 1)
                for n in range(2 * TT):
                    a, q = n // 2, n % 2
                    use = use_gt[n]
                    acquire(pe, use)
                    for i in range(2):
                        mm = pe.transpose(ps[:, use[0], blk4(i)], y_tok[:, a, blk4(2 * q + i)], kc("ident"))
                    mm.then_inc(bk.full[use[0]], 1)

            def vector(dve, own):
                for h in range(2):
                    for u in rounds:
                        if u["y"]:
                            evacuated(dve, u["y"][h])
                y3 = y_tok.rearrange("p a (h n) -> p (a h) n", n=RW_N)
                sq3 = gsq.rearrange("p a (h n) -> p (a h) n", n=RW_N)
                s, m, v, rt = (gn[:, i].rearrange("p a h -> p (a h)") for i in range(4))
                own.step(dve.tensor_reduce(s, y3, AX.X, ALU.add))
                own.settle()
                own.step(dve.tensor_scalar(m, s, 1.0 / RW_N, None, ALU.mult))
                own.settle()
                own.step(dve.tensor_tensor(y3, y3, heads_bc(m, RW_N), ALU.subtract))
                own.settle()
                own.step(dve.tensor_tensor(sq3, y3, y3, ALU.mult))
                own.settle()
                dve.tensor_reduce(v, sq3, AX.X, ALU.add).then_inc(gn_sq, 1)
                dve.wait_ge(gn_rt, 1)
                own.step(dve.reciprocal(rt, rt))
                own.settle()
                dve.tensor_tensor(y3, y3, heads_bc(rt, RW_N), ALU.mult).then_inc(gn_y, 1)
                for j in range(RT):
                    dve.wait_ge(yt_aff, j + 1)
                    own.step(dve.tensor_tensor(yT[:, j, :], yT[:, j, :], bonusT[:, j, :], ALU.add))
                    own.settle()
                    dve.tensor_tensor(rwT[:, j, :].rearrange("p (r w) -> p w r", r=ROWS), yT[:, j, :].rearrange("p (w r) -> p w r", r=ROWS),
                                      gT[:, j, :].rearrange("p (w r) -> p w r", r=ROWS), ALU.mult).then_inc(rw_ready, 1)

            def scalar(act, own):
                v, rt = (gn[:, i].rearrange("p a h -> p (a h)") for i in (2, 3))
                act.wait_ge(gn_sq, 1)
                act.activation(rt, v, ACT.Sqrt, bias=eps(EPS_GN), scale=1.0 / RW_N).then_inc(gn_rt, 1)
                for n in range(2 * TT):
                    a, q = n // 2, n % 2
                    full(act, use_gt[n])
                    emptied(use_gt[n], act.activation(yT[:, 2 * q:2 * q + 2, blk4(a)],
                                                      ps[:, use_gt[n][0], 0:2 * P].rearrange("p (i t) -> p i t", i=2), ACT.Copy))
                for n in range(2 * TT):
                    evacuated(act, use_gt[n])
                for j in range(RT):
                    act.activation(yT[:, j, :], yT[:, j, :], ACT.Identity, bias=vec("rln_b", j, j + 1), scale=vec("rln_g", j, j + 1))\
                        .then_inc(yt_aff, 1)

        PAIRS2 = KT // 2
        seg_merge = segment(4 * PAIRS2)
        bo_buf = [w(W0 + n * BO_K * 2 * P, BO_K * 2 * P, k=BO_K) for n in range(2)]
        gates = [w(W0 + 2 * BO_K * 2 * P + n * 8 * T, 8 * T, b=4) for n in range(2)]
        use_gate = [bk.take(b, 2 * PAIRS2) for b in range(2)]
        use_bo = [bk.take(3 + b, PAIRS2) for b in range(4)]
        bo_ready = [sem(f"bo_ready{n}") for n in range(2)]
        merged = sem("merged")
        BRANCHES = ((convT, CT), (ssdT, ST), (fftT, FT), (rwT, RT))

        class Merge:
            def sync(sp):
                def a_pair(jj, it, first):
                    for b in range(4):
                        u = seg_merge + 4 * jj + b
                        sp.wait_ge(w_used, it * 8 + (u - SLOTS + 1))
                        sp.dma_start(slot(u), gate_u[it * 8 + (4 * jj + b)]).then_inc(w_ready[u % SLOTS], 16)
                        if b == 1:
                            if first:
                                sp.wait_ge(rw_ready, RT)
                                if jj == 0:
                                    sp.dma_start(xT[:, :, :], x_t).then_inc(x_in, 16)
                            else:
                                sp.wait_ge(bk.full[6], it * 2 + (use_bo[3][1] + jj - 1))
                            sp.dma_start(bo_buf[jj].rearrange("p k n -> p (k n)"), bo_u[it * 2 + jj]).then_inc(bo_ready[jj], 16)
                a_pair(0, 0, True)
                a_pair(1, 0, True)
                with sp.Fori(1, PAIRS2 // 2) as it:
                    for jj in range(2):
                        a_pair(jj, it, False)

            def tensor(pe, own):
                with pe.Fori(0, PAIRS2 // 2) as it:
                    for jj in range(2):
                        for b in range(4):
                            n = 4 * jj + b
                            gemm_unit(pe, seg_merge + n, main_rhs, pair(n % 2), [(n % 2, use_gate[n % 2][1] + n // 2)], it=it, k=4, ring=8 // SLOTS)
                        if jj == 0:
                            pe.wait_ge(conv_ready, CT)
                            evacuated(pe, use_f2[1])
                            pe.wait_ge(ssd_ready, ST)
                            pe.wait_ge(rw_ready, RT)
                        pe.wait_ge(bo_ready[jj], it * 16 + 16)
                        at = 0
                        for b, (src, kts) in enumerate(BRANCHES):
                            acquire(pe, (3 + b, use_bo[b][1] + jj), it, 2)
                            for o in range(2):
                                for kt in range(kts):
                                    mm = pe.matmul(ps[:, 3 + b, o * T:(o + 1) * T], bo_buf[jj][:, at + kt, o * P:(o + 1) * P], src[:, kt, :],
                                                   start=kt == 0, stop=kt == kts - 1)
                            mm.then_inc(bk.full[3 + b], 1)
                            at += kts

            def scalar(act, own):
                act.wait_ge(rw_ready, RT)
                with act.Fori(0, PAIRS2 // 2) as it:
                    for jj in range(2):
                        act.wait_ge(merged, it * 2 + (jj + 1))
                        for b in range(4):
                            n = 4 * jj + b
                            unit_done(act, seg_merge + n, it, 8)
                            act.activation(gates[jj][:, b, :], ps[:, n % 2, :], ACT.Sigmoid).then_inc(bk.free[n % 2], 1)

            def gpsimd(pool, own):
                pool.wait_ge(c_row_silu, 1)
                fetch_rows(pool, mod_r, 0, 64)

            def vector(dve, own):
                dve.sem_inc(merged, 2)
                dve.wait_ge(c_row_silu, 1)
                with dve.Fori(0, PAIRS2 // 2) as it:
                    for jj in range(2):
                        for n in range(8):
                            column(dve, modx, vec("mod_b", 32, 96), 8 * jj + n, 8 * jj + n, it, 16)
                        for b in range(2):
                            dve.wait_ge(bk.free[b], it * 4 + (use_gate[b][1] + 2 * jj + 2))
                        for b in range(4):
                            dve.wait_ge(bk.full[3 + b], it * 2 + (use_bo[b][1] + jj + 1))
                            g = gates[jj][:, b, :]
                            dve.tensor_tensor(g, g, ps[:, 3 + b, :], ALU.mult).then_inc(bk.free[3 + b], 1)
                        for b in range(4):
                            dve.wait_ge(bk.free[3 + b], it * 2 + (use_bo[b][1] + jj + 1))
                        g = gates[jj].rearrange("p b (o t) -> p b o t", o=2)
                        dve.tensor_tensor(g[:, 0], g[:, 0], g[:, 1], ALU.add).then_inc(merge_sum, 1)
                        dve.wait_ge(merge_sum, it * 4 + (2 * jj + 1))
                        dve.tensor_tensor(g[:, 0], g[:, 0], g[:, 2], ALU.add).then_inc(merge_sum, 1)
                        dve.wait_ge(merge_sum, it * 4 + (2 * jj + 2))
                        dve.tensor_tensor(m_pairs[:, it * 2 + jj], g[:, 0], g[:, 3], ALU.add).then_inc(merged, 1)
                dve.wait_ge(col_done, G_SLOTS + ADA0)
                own.step(dve.tensor_tensor(gn1, modx[:, 0:KT], vec("norm_g", KT, 2 * KT), ALU.mult))
                own.step(dve.scalar_tensor_tensor(gsc2, modx[:, 2 * KT:3 * KT], 1.0, vec("norm_g", 2 * KT, 3 * KT), ALU.add, ALU.mult))
                own.step(dve.tensor_tensor(gn3, modx[:, 3 * KT:4 * KT], vec("norm_g", 3 * KT, 4 * KT), ALU.mult))
                own.settle()
        m_pairs = hT[:, :, T:].rearrange("p (j o) t -> p j o t", o=2)
        merge_sum = sem("merge_sum")
        gn1, gsc2, gn3 = coef[:, 2 * KT:3 * KT], coef[:, 3 * KT:4 * KT], coef[:, 4 * KT:5 * KT]

        rtn = w(WORK - T, T)
        nsq, nrs, nadd, hsc, hrd = (sem(n) for n in ("norm_squares", "norm_root", "x_added", "h2_scaled", "h2_ready"))
        norms = [0]

        class Rms:

            def __init__(self, src, ready):
                self.src, self.ready = src, ready
                norms[0] += 1
                self.k = norms[0]
                self.use = aux()

            def tensor(self, pe):
                pe.wait_ge(nsq, self.k)
                acquire(pe, self.use)
                for kt in range(KT):
                    mm = pe.matmul(ps[:, self.use[0], 0:T], kc("ones"), hT[:, kt, 0:T], start=kt == 0, stop=kt == KT - 1)
                mm.then_inc(bk.full[self.use[0]], 1)

            def scalar(self, act):
                self.ready(act)
                act.activation(hT[:, :, 0:T], self.src, ACT.Square).then_inc(nsq, 1)
                full(act, self.use)
                emptied(self.use, act.activation(rtn, ps[:, self.use[0], 0:T], ACT.Sqrt, bias=eps(EPS_RMS), scale=1.0 / D))

            def vector(self, dve):
                evacuated(dve, self.use)
                dve.reciprocal(rtn, rtn).then_inc(nrs, 1)
                dve.wait_ge(nrs, self.k)

        adds = [0]

        def add_scaled(dve, own, src, col):
            own.step(dve.tensor_tensor(src, src, bc(rtn, KT), ALU.mult))
            own.settle()
            for kt in range(KT):
                dve.scalar_tensor_tensor(xT[:, kt, :], src[:, kt, :], col[:, kt:kt + 1], xT[:, kt, :], ALU.mult, ALU.add).then_inc(nadd, 1)

        hs = [0]

        def scale_h(dve, col):
            for kt in range(KT):
                dve.scalar_tensor_tensor(hT[:, kt, 0:T], xT[:, kt, :], col[:, kt:kt + 1], rtn, ALU.mult, ALU.mult).then_inc(hsc, 1)

        def shift_h(act, k, col):
            for kt in range(KT):
                act.wait_ge(hsc, k * KT + kt + 1)
                act.activation(hT[:, kt, 0:T], hT[:, kt, 0:T], ACT.Identity, bias=col[:, kt:kt + 1]).then_inc(hrd, 1)

        def to_width(pe, seg, use, rhs, kts=KT):
            with pe.Fori(0, PAIRS2 // 4) as it:
                for j in range(4):
                    gemm_unit(pe, seg + j, rhs, pair(j % 2), [(j % 2, use[j % 2][1] + j // 2)], kts=kts, it=it, k=2, ring=4 // SLOTS)

        def from_width(act, seg, use, dst):
            with act.Fori(0, PAIRS2 // 4) as it:
                for j in range(4):
                    unit_done(act, seg + j, it, 4)
                    act.activation(dst[:, it * 4 + j], ps[:, j % 2, :].rearrange("p (o t) -> p o t", o=2), ACT.Copy).then_inc(bk.free[j % 2], 1)

        def width_done(eng, use):
            for b in range(2):
                eng.wait_ge(bk.free[b], use[b][1] + PAIRS2 // 2)

        seg_wo = segment(PAIRS2)
        use_wo = [bk.take(b, PAIRS2 // 2) for b in range(2)]
        yT1 = w(W0, KT * T, a=KT)
        y1_pairs = yT1.rearrange("p (j o) t -> p j o t", o=2)
        rms_y1 = Rms(yT1, lambda e: width_done(e, use_wo))
        rms_x1 = Rms(xT[:, :, :], lambda e: e.wait_ge(nadd, KT))
        smallw2 = w(WORK - T - SMALL2_N, SMALL2_N)
        smalls2_in = sem("smalls2_in")

        class Mix:
            def sync(sp):
                fetch(sp, wo_u, seg_wo, PAIRS2)
                sp.wait_ge(merged, 2 + PAIRS2)
                sp.dma_start(smallw2, smalls2).then_inc(smalls2_in, 16)

            def tensor(pe, own):
                pe.wait_ge(merged, 2 + PAIRS2)
                to_width(pe, seg_wo, use_wo, lambda kt: hT[:, kt, T:])
                rms_y1.tensor(pe)
                rms_x1.tensor(pe)

            def gpsimd(pool, own):
                pool.wait_ge(row_free, G_SLOTS + ADA0)
                pool.dma_start(c_row[:, :], c_rows[1:2, :].to_broadcast([P, D])).then_inc(c2_row_in, 16)

            def scalar(act, own):
                act.wait_ge(c2_row_in, 16)
                act.activation(rows_buf[:, 0, :], c_row[:, :], ACT.Sigmoid).then_inc(c_row_sig, 1)
                from_width(act, seg_wo, use_wo, y1_pairs)
                rms_y1.scalar(act)
                rms_x1.scalar(act)
                shift_h(act, 0, modx[:, KT:2 * KT])

            def vector(dve, own):
                dve.wait_ge(c_row_sig, 2)
                dve.tensor_tensor(c_row[:, :], c_row[:, :], rows_buf[:, 0, :], ALU.mult).then_inc(c_row_silu, 1)
                rms_y1.vector(dve)
                dve.wait_ge(x_in, 48)
                add_scaled(dve, own, yT1, gn1)
                rms_x1.vector(dve)
                scale_h(dve, gsc2)

        seg_up = segment(D_FF // (2 * P))
        use_up = [bk.take(b, D_FF // (4 * P)) for b in range(2)]
        seg_down = segment(4 * PAIRS2)
        use_down = [bk.take(b, PAIRS2 // 2) for b in range(2)]
        actT = w(0, KF * T, a=KF)
        act_pairs = w(0, KF * T, j=KF // 2)
        y2_pairs = m_pairs
        yT2 = hT[:, :, T:]
        relu_done, sqr_done = sem("relu_done"), sem("sqr_done")
        rms_y2 = Rms(yT2, lambda e: width_done(e, use_down))

        class Mlp:
            def sync(sp):
                fetch(sp, up_u, seg_up, D_FF // (2 * P))
                fetch(sp, down_u, seg_down, 4 * PAIRS2)

            def tensor(pe, own):
                pe.wait_ge(hrd, KT)
                with pe.Fori(0, D_FF // (8 * P)) as it:
                    for j in range(4):
                        gemm_unit(pe, seg_up + j, main_rhs, pair(j % 2), [(j % 2, use_up[j % 2][1] + j // 2)], it=it, k=2, ring=4 // SLOTS)
                pe.wait_ge(sqr_done, D_FF // (2 * P))
                with pe.Fori(0, PAIRS2 // 2) as it:
                    for j in range(2):
                        for q in range(4):
                            gemm_unit(pe, seg_down + 4 * j + q, lambda kt, q=q: actT[:, q * KT + kt, :], pair(j),
                                      [(j, use_down[j][1])] if q == 0 else [], start=q == 0, stop=q == 3, it=it, k=1, ring=8 // SLOTS, parts=True)
                rms_y2.tensor(pe)

            def scalar(act, own):
                act.wait_ge(nadd, KT)
                with act.Fori(0, D_FF // (8 * P)) as it:
                    for j in range(4):
                        unit_done(act, seg_up + j, it, 4)
                        act.activation(act_pairs[:, it * 4 + j], ps[:, j % 2, :], ACT.Relu).then_inc(bk.free[j % 2], 1)
                with act.Fori(0, PAIRS2 // 2) as it:
                    for j in range(2):
                        unit_done(act, seg_down + 4 * j + 3, it, 8)
                        act.activation(y2_pairs[:, it * 2 + j], ps[:, j, :].rearrange("p (o t) -> p o t", o=2), ACT.Copy).then_inc(bk.free[j], 1)
                rms_y2.scalar(act)

            def gpsimd(pool, own):
                pool.wait_ge(c_row_silu, 2)
                fetch_rows(pool, ada_r, ADA0, 96)

            def vector(dve, own):
                dve.wait_ge(c_row_silu, 2)
                with dve.Fori(0, D_FF // (8 * P)) as it:
                    for n in range(6):
                        column(dve, adaT, vec("ada_b"), ADA0 + n, n, it, 6)
                    for j in range(4):
                        dve.wait_ge(bk.free[j % 2], it * 2 + (use_up[j % 2][1] + j // 2 + 1))
                        a = act_pairs[:, it * 4 + j]
                        dve.tensor_tensor(a, a, a, ALU.mult).then_inc(sqr_done, 1)
                with dve.Fori(0, 8) as it:
                    for n in range(6):
                        column(dve, adaT, vec("ada_b"), ADA0 + 48 + n, 48 + n, it, 6)
                dve.wait_ge(col_done, G_SLOTS + ADA0 + 96)
                rms_y2.vector(dve)
                add_scaled(dve, own, yT2, gn3)

        gmix, gffn = coef[:, 0:KT], coef[:, KT:2 * KT]
        mods_b2 = sem("mods_b2")
        seg_in2 = segment(18)
        use_in2 = [bk.take(b, 9) for b in range(2)]
        u2_pairs = w(0, 36 * T, j=18)
        u2 = w(0, 36 * T, a=36)
        zp, zq, zk, zv, zx, zy = (u2[:, a:b, :] for a, b in ((0, 4), (4, 12), (12, 20), (20, 28), (28, 32), (32, 36)))
        use_f = aux()
        rms_x2 = Rms(xT[:, :, :], lambda e: e.wait_ge(nadd, 2 * KT))

        def small2(name):
            o, n = SMALLS2[name]
            return smallw2[:, o:o + n]

        class In2:
            def sync(sp):
                fetch(sp, in2_u, seg_in2, 18)

            def tensor(pe, own):
                rms_x2.tensor(pe)
                pe.wait_ge(hrd, 2 * KT)
                with pe.Fori(0, 4) as it:
                    for j in range(4):
                        gemm_unit(pe, seg_in2 + j, main_rhs, pair(j % 2), [(j % 2, use_in2[j % 2][1] + j // 2)], it=it, k=2, ring=4 // SLOTS)
                for j in range(16, 18):
                    gemm_unit(pe, seg_in2 + j, main_rhs, pair(j % 2), [(j % 2, use_in2[j % 2][1] + j // 2)])
                pe.wait_ge(smalls2_in, 16)
                acquire(pe, use_f)
                wf = small2("wf").rearrange("p (k n) -> p k n", k=KT)
                for a in range(TT):
                    for kt in range(KT):
                        mm = pe.matmul(ps[:, use_f[0], a * AH:(a + 1) * AH], hT[:, kt, a * P:(a + 1) * P], wf[:, kt, :], start=kt == 0, stop=kt == KT - 1)
                mm.then_inc(bk.full[use_f[0]], 1)

            def scalar(act, own):
                rms_x2.scalar(act)
                shift_h(act, 1, adaT[:, 0:KT])
                with act.Fori(0, 4) as it:
                    for j in range(4):
                        unit_done(act, seg_in2 + j, it, 4)
                        act.activation(u2_pairs[:, it * 4 + j], ps[:, j % 2, :], ACT.Copy).then_inc(bk.free[j % 2], 1)
                for j in range(16, 18):
                    unit_done(act, seg_in2 + j)
                    act.activation(u2_pairs[:, j], ps[:, j % 2, :], ACT.Copy).then_inc(bk.free[j % 2], 1)

            def vector(dve, own):
                own.step(dve.scalar_tensor_tensor(gmix, adaT[:, KT:2 * KT], 1.0, vec("g_mix"), ALU.add, ALU.mult))
                own.step(dve.scalar_tensor_tensor(gffn, adaT[:, 4 * KT:5 * KT], 1.0, vec("g_ffn"), ALU.add, ALU.mult))
                own.settle()
                rms_x2.vector(dve)
                scale_h(dve, gmix)

        mixT = hT[:, :, T:]
        B0 = 36 * T
        PW = T + 16
        pool_in = w(B0, 2 * 4 * PW).rearrange("p (i a t) -> p i a t", i=2, a=4)
        pool_d = w(B0 + 8 * PW, 4 * T, a=4)
        L0 = B0 + 8 * PW + 4 * T
        LW = T + LRU_TAPS - 1
        lru_pad = w(L0, 4 * LW, a=4)
        xc = w(L0 + 4 * LW, 4 * T, a=4)
        A0 = L0 + 4 * LW + 4 * T
        gr, gi = zx, w(A0, 4 * T, a=4)
        vt2 = hT[:, :, 0:T]
        F0 = A0 + 4 * T
        fz = [w(F0 + n * TT * AH, TT * AH, a=TT) for n in range(4)]
        sp_l = [w(F0 + 64 + n * 4, 4) for n in range(4)]
        mx = w(F0 + 80, 2 * 8).rearrange("p (i n) -> p i n", i=2)
        F1 = F0 + 96
        assert F1 <= WORK - T - SMALL2_N
        prob = w(B0, 2 * TT * T).rearrange("p (r a s) -> p r a s", r=2, a=TT)
        probT = w(B0 + 2 * TT * T, 2 * TT * T).rearrange("p (r s t) -> p r s t", r=2, s=TT)
        use_pool = [aux() for _ in range(2)]
        use_lr = [aux() for _ in range(4)]
        use_v2 = [aux() for _ in range(4)]
        ATT = []
        for h in range(AH):
            ATT.append(dict(l=aux(), t=aux(), o=aux()))
        (pool_ready, xc_ready, lf_abs, lf_e, lf_u, lf_ln, lf_ready, lam_e, lam_ln, pmax, pexp, pnorm, mix_ready, lru_tanh, lru_sq, lru_a, gelu_in, gelu_t,
         lru_h, lru_done, lam_abs, lam_u) = (sem(n) for n in (
             "pool_ready", "xc_ready", "lf_abs", "lf_e", "lf_u", "lf_ln", "lf_ready", "lam_e", "lam_ln", "pmax", "pexp", "pnorm", "mix_ready",
             "lru_tanh", "lru_sq", "lru_a", "gelu_in", "gelu_t", "lru_h", "lru_done", "lam_abs", "lam_u"))
        SCALE = float(P) ** -0.5

        def v_head(a, h):
            return vt2[:, 4 * a + h // 2, h % 2 * P:(h % 2 + 1) * P]

        GELU_C = float(np.sqrt(2.0 / np.pi))

        class Mix2:
            def tensor(pe, own):
                wp, wa, wi = (small2(n).rearrange("p (b n) -> p b n", b=4) for n in ("pool_w", "lru_wa", "lru_wi"))
                pe.wait_ge(pool_ready, 4)
                for g in range(4):
                    use = use_pool[g // 2]
                    if g % 2 == 0:
                        acquire(pe, use)
                    mm = pe.matmul(ps[:, use[0], g % 2 * T:(g % 2 + 1) * T], wp[:, g, :], pool_d[:, g, :], start=True, stop=True)
                    if g % 2:
                        mm.then_inc(bk.full[use[0]], 1)
                for i in range(4):
                    use = use_lr[i]
                    wm = (wa, wi)[i // 2]
                    acquire(pe, use)
                    for o in range(2):
                        b = i % 2 * 2 + o
                        pe.wait_ge(xc_ready, b + 1)
                        mm = pe.matmul(ps[:, use[0], o * T:(o + 1) * T], wm[:, b, :], xc[:, b, :], start=True, stop=True)
                    mm.then_inc(bk.full[use[0]], 1)
                for n in range(4):
                    a, q = n // 2, n % 2
                    use = use_v2[n]
                    acquire(pe, use)
                    for i in range(4):
                        mm = pe.transpose(ps[:, use[0], blk4(i)], zv[:, 4 * q + i, a * P:(a + 1) * P], kc("ident"))
                    mm.then_inc(bk.full[use[0]], 1)
                pe.wait_ge(lf_ready, 1)
                lf = fz[3]

                def logits(h):
                    use = ATT[h]["l"]
                    acquire(pe, use)
                    for a in range(TT):
                        s1 = (a + 1) * P
                        out = ps[:, use[0], a * T:a * T + s1]
                        pe.matmul(out, zq[:, h, a * P:(a + 1) * P], zk[:, h, 0:s1], start=True, stop=False)
                        for s in range(a + 1):
                            o = ps[:, use[0], a * T + s * P:a * T + (s + 1) * P]
                            for i in range(s + 1):
                                pe.matmul(o, lf[:, i, h:h + 1].to_broadcast([P, P]), kc("upto") if i == s else kc("ones"), start=False, stop=False)
                        mm = pe.matmul(ps[:, use[0], a * T + a * P:a * T + s1], kc("ident"), kc("neg_b"), start=False, stop=True)
                    mm.then_inc(bk.full[use[0]], 1)

                def turn(h):
                    use = ATT[h]["t"]
                    pe.wait_ge(pnorm, h + 1)
                    acquire(pe, use)
                    for s in range(TT):
                        for a in range(s, TT):
                            mm = pe.transpose(ps[:, use[0], s * T + a * P:s * T + (a + 1) * P], prob[:, h % 2, a, s * P:(s + 1) * P], kc("ident"))
                    mm.then_inc(bk.full[use[0]], 1)

                def weigh(h):
                    evacuated(pe, ATT[h]["t"])
                    for n in range(4):
                        evacuated(pe, use_v2[n])
                    use = ATT[h]["o"]
                    acquire(pe, use)
                    pe.matmul(ps[:, use[0], 0:T], v_head(0, h), probT[:, h % 2, 0, :], start=True, stop=False)
                    pe.matmul(ps[:, use[0], P:T], v_head(1, h), probT[:, h % 2, 1, P:], start=False, stop=True).then_inc(bk.full[use[0]], 1)

                logits(0)
                for h in range(AH):
                    if h + 1 < AH:
                        logits(h + 1)
                    turn(h)
                    weigh(h)

            def scalar(act, own):
                act.wait_ge(lf_abs, 1)
                act.activation(fz[1], fz[1], ACT.Exp, scale=-1.0).then_inc(lf_e, 1)
                act.activation(sp_l[1], sp_l[1], ACT.Exp, scale=-1.0).then_inc(lam_e, 1)
                act.wait_ge(lf_u, 1)
                act.activation(fz[3], fz[2], ACT.Ln).then_inc(lf_ln, 1)
                act.activation(sp_l[3], sp_l[2], ACT.Ln).then_inc(lam_ln, 1)
                for i in range(2):
                    use = use_pool[i]
                    full(act, use)
                    for o in range(2):
                        ins = act.activation(mixT[:, 2 * i + o, :], ps[:, use[0], o * T:(o + 1) * T], ACT.Copy, scale=vec("pool_scale", 2 * i + o, 2 * i + o + 1))
                        if o == 0:
                            own.step(ins)
                    emptied(use, ins)
                act.wait_ge(xc_ready, 4)
                for i in range(4):
                    use = use_lr[i]
                    full(act, use)
                    for o in range(2):
                        b = i % 2 * 2 + o
                        dst, bias = ((gr, "lru_ba"), (gi, "lru_bi"))[i // 2]
                        ins = act.activation(dst[:, b, :], ps[:, use[0], o * T:(o + 1) * T], ACT.Sigmoid, bias=vec(bias, b, b + 1))
                        if o == 0:
                            own.step(ins)
                    emptied(use, ins)
                for n in range(4):
                    a, q = n // 2, n % 2
                    full(act, use_v2[n])
                    emptied(use_v2[n], act.activation(vt2[:, 4 * a + 2 * q:4 * a + 2 * q + 2, :],
                                                               ps[:, use_v2[n][0], :].rearrange("p (o t) -> p o t", o=2), ACT.Copy))
                act.wait_ge(lru_a, 1)
                act.activation(lru_t, gr, ACT.Tanh).then_inc(lru_tanh, 1)
                act.wait_ge(gelu_in, 1)
                act.activation(gel, gel, ACT.Tanh, scale=GELU_C).then_inc(gelu_t, 1)
                act.wait_ge(lru_tanh, 1)
                act.activation(gr, gr, ACT.Exp).then_inc(lru_tanh, 1)
                act.wait_ge(lru_sq, 1)
                act.activation(lru_t, lru_t, ACT.Sqrt).then_inc(lru_h, 1)
                for h in range(AH):
                    d = ATT[h]
                    act.wait_ge(pmax, h + 1)
                    if h >= 2:
                        full(act, ATT[h - 2]["t"])
                    full(act, d["l"])
                    for a in range(TT):
                        ins = act.activation(prob[:, h % 2, a, 0:(a + 1) * P], ps[:, d["l"][0], a * T:a * T + (a + 1) * P], ACT.Exp, scale=SCALE,
                                             bias=mx[:, 0, a + 2 * (h % 2):a + 2 * (h % 2) + 1], accum_out=mx[:, 1, a + 2 * (h % 2):a + 2 * (h % 2) + 1])
                        if a == 0:
                            own.step(ins)
                    emptied(d["l"], ins)
                    full(act, d["t"])
                    own.step(act.activation(probT[:, h % 2, 0, :], ps[:, d["t"][0], 0:T], ACT.Copy))
                    emptied(d["t"], act.activation(probT[:, h % 2, 1, P:], ps[:, d["t"][0], T + P:], ACT.Copy))
                    full(act, d["o"])
                    emptied(d["o"], act.activation(mixT[:, 4 + h, :], ps[:, d["o"][0], 0:T], ACT.Copy))

            def vector(dve, own):
                for b in range(2):
                    dve.wait_ge(bk.free[b], use_in2[b][1] + 9)
                own.step(dve.memset(lru_pad.rearrange("p a t -> p (a t)"), 0.0))
                own.step(dve.memset(pool_in.rearrange("p i a t -> p (i a t)"), 0.0))
                own.settle()
                own.step(dve.tensor_copy(lru_pad[:, :, LRU_TAPS - 1:], zx))
                own.step(dve.tensor_copy(pool_in[:, 0, :, 16:], zp))
                own.settle()
                for k in range(LRU_TAPS):
                    for b in range(4):
                        own.settle(3 if k < LRU_TAPS - 1 else 3 - b)
                        tap = vec("lru_cw", k * 4 + b, k * 4 + b + 1)
                        src = lru_pad[:, b, k:k + T]
                        if k == 0:
                            ins = dve.tensor_scalar(xc[:, b, :], src, tap, vec("lru_cb", b, b + 1), ALU.mult, ALU.add)
                        else:
                            ins = dve.scalar_tensor_tensor(xc[:, b, :], src, tap, xc[:, b, :], ALU.mult, ALU.add)
                        if k == LRU_TAPS - 1:
                            ins.then_inc(xc_ready, 1)
                        else:
                            own.step(ins)
                own.settle()
                for n in range(4):
                    src, dst = pool_in[:, n % 2], pool_in[:, (n + 1) % 2]
                    s = 1 << n
                    own.settle()
                    own.step(dve.tensor_tensor(dst[:, :, s:], src[:, :, s:], src[:, :, 0:PW - s], ALU.add))
                    own.settle()
                    o = CONSTS["pool_inv"][0] + 16 * n
                    own.step(dve.tensor_tensor(pool_d[:, n, 0:16], dst[:, n, 16:32], K[:, o:o + 16], ALU.mult))
                    own.step(dve.tensor_scalar(pool_d[:, n, 16:], dst[:, n, 32:], 1.0 / POOL_WINDOWS[n], None, ALU.mult))
                    own.settle()
                    dve.tensor_tensor(pool_d[:, n, :], pool_d[:, n, :], zp[:, n, :], ALU.subtract).then_inc(pool_ready, 1)
                full(dve, use_f)
                z, e, u, l = fz
                emptied(use_f, dve.tensor_tensor(z, ps[:, use_f[0], 0:TT * AH].rearrange("p (a h) -> p a h", a=TT), bc(vec("b_f"), TT), ALU.add))
                evacuated(dve, use_f)
                own.step(dve.tensor_scalar(sp_l[0], vec("lru_lam"), -1.0, None, ALU.mult))
                own.settle()
                own.step(dve.scalar_tensor_tensor(sp_l[1], sp_l[0], -1.0, sp_l[0], ALU.mult, ALU.max))
                own.settle()
                dve.scalar_tensor_tensor(e, z, -1.0, z, ALU.mult, ALU.max).then_inc(lf_abs, 1)
                dve.wait_ge(lf_e, 1)
                dve.wait_ge(lam_e, 1)
                own.step(dve.tensor_scalar(sp_l[2], sp_l[1], 1.0, None, ALU.add))
                own.settle()
                dve.tensor_scalar(u, e, 1.0, None, ALU.add).then_inc(lf_u, 1)
                dve.wait_ge(lf_u, 1)
                dve.wait_ge(lf_ln, 1)
                dve.wait_ge(lam_ln, 1)
                for zz, ee, uu, ll in ((z, e, u, l), (sp_l[0], sp_l[1], sp_l[2], sp_l[3])):
                    own.step(dve.scalar_tensor_tensor(ee, uu, -1.0, ee, ALU.add, ALU.subtract))
                    own.settle()
                    own.step(dve.reciprocal(uu, uu))
                    own.settle()
                    own.step(dve.tensor_tensor(ee, ee, uu, ALU.mult))
                    own.settle()
                    own.step(dve.tensor_tensor(ll, ll, ee, ALU.subtract))
                    own.settle()
                own.step(dve.scalar_tensor_tensor(l, z, 0.0, l, ALU.min, ALU.subtract))
                own.step(dve.scalar_tensor_tensor(sp_l[3], sp_l[0], 0.0, sp_l[3], ALU.max, ALU.add))
                own.settle()
                own.step(dve.tensor_scalar(sp_l[3], sp_l[3], -8.0, None, ALU.mult))
                dve.tensor_scalar(l, l, -1.0 / SCALE, None, ALU.mult).then_inc(lf_ready, 1)
                own.settle()
                for n in use_lr:
                    evacuated(dve, n)
                for b in range(4):
                    ins = dve.tensor_scalar(gr[:, b, :], gr[:, b, :], sp_l[3][:, b:b + 1], None, ALU.mult)
                    if b < 3:
                        own.step(ins)
                    else:
                        ins.then_inc(lru_a, 1)
                own.step(dve.tensor_tensor(gi, gi, xc, ALU.mult))
                own.step(dve.tensor_tensor(gel, zy, zy, ALU.mult))
                own.settle()
                own.step(dve.tensor_tensor(gel, gel, zy, ALU.mult))
                own.settle()
                dve.scalar_tensor_tensor(gel, gel, 0.044715, zy, ALU.mult, ALU.add).then_inc(gelu_in, 1)
                dve.wait_ge(lru_tanh, 1)
                own.step(dve.tensor_scalar(lru_u, lru_t, -1.0, 1.0, ALU.mult, ALU.add))
                own.settle()
                own.step(dve.reciprocal(lru_u, lru_u))
                own.settle()
                dve.scalar_tensor_tensor(lru_t, lru_t, -2.0, lru_u, ALU.mult, ALU.mult).then_inc(lru_sq, 1)
                dve.wait_ge(lru_h, 1)
                own.step(dve.tensor_tensor(gi, gi, lru_t, ALU.mult))
                own.settle()
                dve.wait_ge(gelu_t, 1)
                own.step(dve.scalar_tensor_tensor(gel, gel, 1.0, zy, ALU.add, ALU.mult))
                dve.wait_ge(lru_tanh, 2)
                for b in range(4):
                    own.step(dve.tensor_tensor_scan(xc[:, b, :], gr[:, b, :], gi[:, b, :], 0.0, ALU.mult, ALU.add))
                own.settle()
                dve.scalar_tensor_tensor(mixT[:, 12:16, :], gel, 0.5, xc, ALU.mult, ALU.mult).then_inc(lru_done, 1)
                dve.wait_ge(pool_ready, 4)
                for h in range(AH):
                    d = ATT[h]
                    full(dve, d["l"])
                    m = 2 * (h % 2)
                    for a in range(TT):
                        own.step(dve.tensor_reduce(mx[:, 0, m + a:m + a + 1], ps[:, d["l"][0], a * T:a * T + (a + 1) * P], AX.X, ALU.max))
                    own.settle()
                    dve.tensor_scalar(mx[:, 0, m:m + 2], mx[:, 0, m:m + 2], -SCALE, None, ALU.mult).then_inc(pmax, 1)
                    evacuated(dve, d["l"])
                    own.step(dve.reciprocal(mx[:, 1, m:m + 2], mx[:, 1, m:m + 2]))
                    own.settle()
                    own.step(dve.tensor_scalar(prob[:, h % 2, 0, 0:P], prob[:, h % 2, 0, 0:P], mx[:, 1, m:m + 1], None, ALU.mult))
                    dve.tensor_scalar(prob[:, h % 2, 1, :], prob[:, h % 2, 1, :], mx[:, 1, m + 1:m + 2], None, ALU.mult).then_inc(pnorm, 1)
        lru_t = zv[:, 0:4, :]
        lru_u = zv[:, 4:8, :]
        gel = zp

        seg_out2 = segment(PAIRS2)
        use_out2 = [bk.take(b, PAIRS2 // 2) for b in range(2)]
        y3 = w(0, KT * T, a=KT)
        y3_pairs = y3.rearrange("p (j o) t -> p j o t", o=2)
        rms_x3 = Rms(xT[:, :, :], lambda e: e.wait_ge(nadd, 3 * KT))
        seg_ffn = segment(KF2)
        use_ffn = [bk.take(b, KF2 // 2) for b in range(2)]
        seg_down2 = segment(4 * PAIRS2)
        use_down2 = [bk.take(b, PAIRS2 // 2) for b in range(2)]
        act2 = w(0, KF2 * T, a=KF2)
        FW = T + FFN_TAPS - 1
        gpad = w(KF2 * T, 2 * 2 * FW).rearrange("p (r o t) -> p r o t", r=2, o=2)
        upb = w(KF2 * T + 4 * FW, 2 * 2 * T).rearrange("p (r o t) -> p r o t", r=2, o=2)
        gcv = w(KF2 * T + 4 * FW + 4 * T, 2 * 2 * T).rearrange("p (r o t) -> p r o t", r=2, o=2)
        gpad_zero, gconv, gsilu, gact, gtap, out_done = (sem(n) for n in ("gpad_zero", "gconv", "gsilu", "gact", "gtap", "out_done"))
        y4 = hT[:, :, T:]
        y4_pairs = m_pairs
        rms_x4 = Rms(xT[:, :, :], lambda e: e.wait_ge(nadd, 4 * KT))
        taps2 = vec("ffn_cw").rearrange("p (a k) -> p a k", k=FFN_TAPS)

        class Ffn2:
            def sync(sp):
                fetch(sp, out2_u, seg_out2, PAIRS2)
                fetch(sp, ffn_u, seg_ffn, KF2)
                fetch(sp, down2_u, seg_down2, 4 * PAIRS2, size=UNIT2)
                sp.wait_ge(out_done, KT)
                sp.dma_start(out_t, yT1).then_inc(x_in, 16)
                sp.wait_ge(x_in, 64)

            def tensor(pe, own):
                pe.wait_ge(lru_done, 1)
                evacuated(pe, use_pool[1])
                for h in range(AH):
                    evacuated(pe, ATT[h]["o"])
                to_width(pe, seg_out2, use_out2, lambda kt: mixT[:, kt, :])
                rms_x3.tensor(pe)
                pe.wait_ge(hrd, 3 * KT)
                with pe.Fori(0, KF2 // 4) as it:
                    for j in range(4):
                        gemm_unit(pe, seg_ffn + j, main_rhs, pair(j % 2), [(j % 2, use_ffn[j % 2][1] + j // 2)], it=it, k=2, ring=4 // SLOTS)
                pe.wait_ge(gact, 4 + KF2)
                kq = KF2 // 4
                with pe.Fori(0, PAIRS2 // 2) as it:
                    for j in range(2):
                        for q in range(4):
                            gemm_unit(pe, seg_down2 + 4 * j + q, lambda kt, q=q: act2[:, q * kq + kt, :], pair(j),
                                      [(j, use_down2[j][1])] if q == 0 else [], kts=kq, start=q == 0, stop=q == 3, it=it, k=1, ring=8 // SLOTS, parts=True)
                rms_x4.tensor(pe)

            def scalar(act, own):
                from_width(act, seg_out2, use_out2, y3_pairs)
                rms_x3.scalar(act)
                shift_h(act, 2, adaT[:, 3 * KT:4 * KT])
                act.wait_ge(gpad_zero, 1)
                with act.Fori(0, KF2 // 4) as it:
                    for r in range(2):
                        act.wait_ge(gact, it * 4 + (2 * r + 2))
                        unit_done(act, seg_ffn + 2 * r, it, 4)
                        act.activation(gpad[:, r, :, FFN_TAPS - 1:], ps[:, 0, :].rearrange("p (o t) -> p o t", o=2), ACT.Copy).then_inc(bk.free[0], 1)
                        unit_done(act, seg_ffn + 2 * r + 1, it, 4)
                        act.activation(upb[:, r], ps[:, 1, :].rearrange("p (o t) -> p o t", o=2), ACT.Copy).then_inc(bk.free[1], 1)
                        for o in range(2):
                            act.wait_ge(gconv, it * 4 + (2 * r + o + 1))
                            act.activation(gcv[:, r, o, :], gcv[:, r, o, :], ACT.Silu).then_inc(gsilu, 1)
                with act.Fori(0, PAIRS2 // 2) as it:
                    for j in range(2):
                        unit_done(act, seg_down2 + 4 * j + 3, it, 8)
                        act.activation(y4_pairs[:, it * 2 + j], ps[:, j, :].rearrange("p (o t) -> p o t", o=2), ACT.Copy).then_inc(bk.free[j], 1)
                rms_x4.scalar(act)

            def vector(dve, own):
                width_done(dve, use_out2)
                for kt in range(KT):
                    dve.scalar_tensor_tensor(xT[:, kt, :], y3[:, kt, :], adaT[:, 2 * KT + kt:2 * KT + kt + 1], xT[:, kt, :], ALU.mult, ALU.add).then_inc(nadd, 1)
                own.step(dve.memset(gpad.rearrange("p r o t -> p (r o t)"), 0.0))
                own.settle()
                dve.sem_inc(gpad_zero, 1)
                rms_x3.vector(dve)
                scale_h(dve, gffn)
                dve.sem_inc(gact, 4)
                dve.wait_ge(nadd, 3 * KT)
                with dve.Fori(0, KF2 // 4) as it:
                    for r in range(2):
                        dve.wait_ge(bk.free[0], it * 2 + (use_ffn[0][1] + r + 1))
                        for k in range(FFN_TAPS):
                            for o in range(2):
                                tile = it * 4 + (2 * r + o)
                                if k == 0:
                                    ins = dve.tensor_scalar(gcv[:, r, o, :], gpad[:, r, o, 0:T], taps2[:, tile, 0:1], vec("ffn_cb").unsqueeze(2)[:, tile, 0:1],
                                                            ALU.mult, ALU.add)
                                else:
                                    dve.wait_ge(gtap, it * 8 + (4 * r + 2 * (k - 1) + o + 1))
                                    ins = dve.scalar_tensor_tensor(gcv[:, r, o, :], gpad[:, r, o, k:k + T], taps2[:, tile, k:k + 1], gcv[:, r, o, :],
                                                                   ALU.mult, ALU.add)
                                ins.then_inc(gconv if k == FFN_TAPS - 1 else gtap, 1)
                        dve.wait_ge(bk.free[1], it * 2 + (use_ffn[1][1] + r + 1))
                        for o in range(2):
                            dve.wait_ge(gsilu, it * 4 + (2 * r + o + 1))
                            dve.tensor_tensor(act2[:, it * 4 + (2 * r + o), :], gcv[:, r, o, :], upb[:, r, o, :], ALU.mult).then_inc(gact, 1)
                width_done(dve, use_down2)
                for kt in range(KT):
                    dve.scalar_tensor_tensor(xT[:, kt, :], y4[:, kt, :], adaT[:, 5 * KT + kt:5 * KT + kt + 1], xT[:, kt, :], ALU.mult, ALU.add).then_inc(nadd, 1)
                rms_x4.vector(dve)
                for kt in range(KT):
                    dve.scalar_tensor_tensor(yT1[:, kt, :], xT[:, kt, :], vec("final_g", kt, kt + 1), rtn, ALU.mult, ALU.mult).then_inc(out_done, 1)

        with nc.Block() as block:
            @block.sync
            def _(sp):
                Mod.sync(sp)
                ConvFft.sync(sp)
                SsdIn.sync(sp)
                RwIn.sync(sp)
                Merge.sync(sp)
                Mix.sync(sp)
                Mlp.sync(sp)
                In2.sync(sp)
                Ffn2.sync(sp)

            @block.tensor
            def _(pe):
                own = Own(pe, pe_done)
                Mod.tensor(pe, own)
                Norm0.tensor(pe, own)
                ConvFft.tensor(pe, own)
                ConvFft.tensor_norm(pe, own)
                SsdIn.tensor(pe, own)
                SsdScan.tensor(pe, own)
                RwIn.tensor(pe, own)
                RwScan.tensor(pe, own)
                RwOut.tensor(pe, own)
                Merge.tensor(pe, own)
                Mix.tensor(pe, own)
                Mlp.tensor(pe, own)
                In2.tensor(pe, own)
                Mix2.tensor(pe, own)
                Ffn2.tensor(pe, own)

            @block.scalar
            def _(act):
                own = Own(act, act_done)
                Mod.scalar(act, own)
                Norm0.scalar(act, own)
                ConvFft.scalar(act, own)
                ConvFft.scalar_norm(act, own)
                SsdIn.scalar(act, own)
                SsdScan.scalar(act, own)
                RwIn.scalar(act, own)
                RwScan.scalar(act, own)
                RwOut.scalar(act, own)
                Merge.scalar(act, own)
                Mix.scalar(act, own)
                Mlp.scalar(act, own)
                In2.scalar(act, own)
                Mix2.scalar(act, own)
                Ffn2.scalar(act, own)

            @block.vector
            def _(dve):
                own = Own(dve, dve_done)
                Mod.vector(dve, own)
                Norm0.vector(dve, own)
                ConvFft.vector(dve, own)
                ConvFft.vector_norm(dve, own)
                SsdIn.vector(dve, own)
                SsdScan.vector(dve, own)
                RwIn.vector(dve, own)
                RwScan.vector(dve, own)
                RwOut.vector(dve, own)
                Merge.vector(dve, own)
                Mix.vector(dve, own)
                Mlp.vector(dve, own)
                In2.vector(dve, own)
                Mix2.vector(dve, own)
                Ffn2.vector(dve, own)

            @block.gpsimd
            def _(pool):
                own = Own(pool, pool_done)
                RwScan.gpsimd(pool, own)
                Merge.gpsimd(pool, own)
                Mix.gpsimd(pool, own)
                Mlp.gpsimd(pool, own)



def cols(a):
    return np.ascontiguousarray(np.asarray(a).reshape(-1, P).T)


def by_units(wm, kts=KT):
    k, c = wm.shape
    n_k, n_c = k // (kts * P), c // (2 * P)
    v = wm.reshape(n_k, kts, P, n_c, 2 * P).transpose(3, 0, 2, 1, 4)
    return np.ascontiguousarray(v.reshape(n_c * n_k, P, kts * 2 * P))


def by_rows(wm):
    return np.ascontiguousarray(wm.T).reshape(-1, P, wm.shape[0])


def k_major(wm):
    k, c = wm.shape
    return np.ascontiguousarray(wm.reshape(k // P, P, c).transpose(1, 0, 2).reshape(P, -1))


def tokens_last(x):
    return np.ascontiguousarray(np.asarray(x)[0].reshape(T, KT, P).transpose(2, 1, 0))


def lay_out(i):
    i = {k: np.asarray(v) for k, v in i.items()}
    vecs = np.zeros((P, VEC_N), np.float32)

    def put(name, a, rows=P):
        o, n = VECS[name]
        vecs[0:rows, o:o + n] = a

    def rows(a):
        return np.broadcast_to(a.reshape(1, -1), (P, a.size))

    def taps(a):
        return a.reshape(a.shape[0], -1, P).transpose(2, 0, 1).reshape(P, -1)

    put("c", np.stack([cols(i["c"]), cols(i["c_ctx"])], 2).reshape(P, -1))
    put("mod_b", cols(i["mod_b"]))
    put("ada_b", cols(i["b_ada_2"]))
    put("norm_g", cols(i["norm_g"]))
    put("conv_w", taps(i["conv_w"][0]))
    for name, key in (("conv_b", "conv_b"), ("conv_ln_g", "conv_ln_g"), ("conv_ln_b", "conv_ln_b"), ("ssd_cb", "ssd_conv_b"),
                      ("ssd_ng", "ssd_norm_g"), ("w0", "rwkv_w0"), ("a0", "rwkv_a0"), ("k_k", "rwkv_k_k"), ("k_a", "rwkv_k_a"),
                      ("r_k", "rwkv_r_k"), ("rln_g", "rwkv_ln_g"), ("rln_b", "rwkv_ln_b"), ("g_mix", "g_mix_2"),
                      ("g_ffn", "g_ffn_2"), ("final_g", "final_g_2"), ("pool_scale", "pool_scale_2"), ("lru_cb", "lru_conv_b_2"),
                      ("lru_ba", "lru_ba_2"), ("lru_bi", "lru_bi_2"), ("lru_lam", "lru_lambda_2"), ("ffn_cb", "ffn_conv_b_2")):
        put(name, cols(i[key]))
    put("ssd_cw", taps(i["ssd_conv_w"][0]))
    put("lru_cw", taps(i["lru_conv_w_2"][0]))
    put("ffn_cw", i["ffn_conv_w_2"][0].reshape(FFN_TAPS, KF2, P).transpose(2, 1, 0).reshape(P, -1))
    put("A_log", rows(i["ssd_A_log"]))
    put("dt_bias", rows(i["ssd_dt_bias"]))
    put("ssd_D", rows(i["ssd_D"]))
    put("b_f", rows(i["b_f_2"]))
    mu = i["rwkv_mu"][0]
    put("mu", np.pad(cols(mu[0:3 * RW_DIM]), ((0, 0), (0, 3))))
    o = VECS["mu"][0]
    lo = 3 * RW_DIM
    vecs[:, o + 12] = mu[lo:lo + 2 * LORA]
    vecs[:, o + 13] = mu[lo + 3 * LORA:]
    vecs[0:LORA, o + 14] = mu[lo + 2 * LORA:lo + 3 * LORA]

    w_in = i["w_in"][0]
    rw = SSD_IN
    cv = REC_IN
    ff = REC_IN + 2 * CONV
    gt = ff + FFT
    smalls = np.zeros((P, SMALL_N), np.float32)
    smalls[:, 0:KT * 88] = k_major(np.concatenate([w_in[:, rw + lo + 2 * LORA:rw + lo + 3 * LORA], w_in[:, SSD_IN - 2 * SSD_H:SSD_IN]], 1))
    for name, a in (("w2", i["rwkv_w2"].reshape(2 * LORA, RW_DIM)), ("a2", i["rwkv_a2"][0]), ("g2", i["rwkv_g2"][0])):
        at, n = SMALLS[name]
        smalls[0:a.shape[0], at:at + n] = a
    w_in2 = i["w_in_2"][0]
    fcol = POOL + 3 * ATTN
    smalls2 = np.concatenate([k_major(w_in2[:, fcol:fcol + AH])] + [
        np.ascontiguousarray(i[k][0].transpose(1, 0, 2).reshape(P, -1)) for k in ("pool_w_2", "lru_wa_2", "lru_wi_2")], 1)

    bo = np.concatenate([i[k][0] for k in ("conv_out", "ssd_out", "fourier_out", "rwkv_out")], 0)
    gates = w_in[:, gt:].reshape(D, 4, KT // 2, 2 * P).transpose(0, 2, 1, 3).reshape(D, -1)
    ffn = np.stack([i["w_ffn_gate_2"][0].reshape(D, KF2 // 2, 2 * P), i["w_ffn_up_2"][0].reshape(D, KF2 // 2, 2 * P)], 2).reshape(D, -1)
    return dict(
        x_t=tokens_last(i["x"]), ctx_t=tokens_last(i["ctx"]), vecs=vecs, consts=shape_constants(), smalls=smalls, smalls2=smalls2,
        c_rows=np.concatenate([i["c"], i["c_2"]], 0), mod_u=by_units(i["mod_w"][0][:, 0:2 * D]), mod_r=by_rows(i["mod_w"][0][:, 2 * D:]),
        ada_r=by_rows(i["w_ada_2"][0]),
        conv_u=by_units(np.concatenate([w_in[:, cv + CONV:ff], w_in[:, cv:cv + CONV], w_in[:, ff:gt]], 1)),
        ssd_u=by_units(w_in[:, 0:SSD_IN - 2 * SSD_H]),
        rw_u=by_units(np.concatenate([w_in[:, rw:rw + lo + 2 * LORA], w_in[:, rw + lo + 3 * LORA:rw + RW_IN]], 1)),
        gate_u=by_units(gates), bo_u=by_units(bo, BO_K), wo_u=by_units(i["w_o"][0]), up_u=by_units(i["mlp_up"][0]),
        down_u=by_units(i["mlp_down"][0]),
        in2_u=by_units(np.concatenate([w_in2[:, 0:fcol], w_in2[:, fcol + AH:]], 1)),
        out2_u=by_units(i["w_out_2"][0]), ffn_u=by_units(ffn), down2_u=by_units(i["w_ffn_down_2"][0], KF2 // 4))


def kernel(**inputs):
    import concourse.bacc as bacc
    from concourse.bass_utils import run_bass_kernel_spmd

    arrays = lay_out(inputs)
    nc = bacc.Bacc("TRN2", target_bir_lowering=False, num_devices=1)
    args = {n: nc.dram_tensor(f"in_{n}", a.shape, mybir.dt.from_np(a.dtype), kind="ExternalInput").ap() for n, a in arrays.items()}
    out = nc.dram_tensor("out_t", (P, KT, T), F32, kind="ExternalOutput").ap()
    branch_kernel(nc, out_t=out, **args)
    r = run_bass_kernel_spmd(nc, [{f"in_{n}": a for n, a in arrays.items()}], core_ids=[0])
    y = r.results[0]["out_t"]
    return np.ascontiguousarray(y.transpose(2, 1, 0)).reshape(1, T, D)
```

```python
from contextlib import ExitStack

import numpy as np

import concourse.bass as bass
from concourse import mybir

ALU = mybir.AluOpType
ACT = mybir.ActivationFunctionType
AX = mybir.AxisListType
F32 = mybir.dt.float32
F32R = mybir.dt.float32r

P = 128
D = 2048
T = 256
KT = D // P
TT = T // P
GRID_W = 64
ROWS = T // GRID_W
CONV, CONV_TAPS = 512, 31
SSD_H, SSD_P, SSD_G, SSD_N, SSD_TAPS = 12, 64, 4, 128, 5
SSD_DIM = SSD_H * SSD_P
SSD_XBC = SSD_DIM + 2 * SSD_G * SSD_N
SSD_IN = SSD_DIM + SSD_XBC + 2 * SSD_H
RW_H, RW_N, RW_DIM = 8, 64, 512
RW_C = 64
LORA, GATE_LORA = 64, 128
RW_IN = 3 * RW_DIM + 3 * LORA + GATE_LORA
REC_IN = SSD_IN + RW_IN
FFT = 512
D_FF = 4 * D
POOL, ATTN, LRU = 512, 1024, 512
AH = 8
POOL_WINDOWS = (2, 4, 8, 16)
LRU_TAPS = 4
D_FF2 = 5632
FFN_TAPS = 3
KF = D_FF // P
KF2 = D_FF2 // P
DECAY = float(np.exp(-0.5))
NEG = -1.0e30

CT = CONV // P
ST = SSD_DIM // P
FT = FFT // P
RT = RW_DIM // P
XT_TILES = SSD_XBC // P

SLOTS = 4
G_SLOTS = 2
UNIT = KT * P
PARTS2 = (16, 16, 12)
BO_K = CT + ST + FT + RT



def offsets(sizes):
    out, at = {}, 0
    for name, n in sizes:
        out[name] = (at, n)
        at += n
    return out, at


VECS, VEC_N = offsets([
    ("c", KT * 2), ("mod_b", 96), ("ada_b", 96), ("norm_g", 4 * KT),
    ("conv_w", CONV_TAPS * CT), ("conv_b", CT), ("conv_ln_g", CT), ("conv_ln_b", CT),
    ("ssd_cw", SSD_TAPS * XT_TILES), ("ssd_cb", XT_TILES), ("ssd_ng", ST),
    ("A_log", 2 * SSD_H), ("dt_bias", 2 * SSD_H), ("ssd_D", SSD_H),
    ("mu", 15), ("w0", 2 * RT), ("a0", RT), ("k_k", RT), ("k_a", RT), ("r_k", RT), ("rln_g", RT), ("rln_b", RT),
    ("g_mix", KT), ("g_ffn", KT), ("final_g", KT), ("b_f", AH), ("pool_scale", 4),
    ("lru_cw", LRU_TAPS * 4), ("lru_cb", 4), ("lru_ba", 4), ("lru_bi", 4), ("lru_lam", 4),
    ("ffn_cw", FFN_TAPS * KF2), ("ffn_cb", KF2),
])
LEVELS = (1, 2, 4, 8, 16, 32)
CONSTS, CONST_N = offsets(
    [("ident", P), ("ones", P), ("blk", P), ("upto", P), ("from", P), ("neg_f", P), ("neg_b", P)]
    + [(f"strict{d}", P) for d in range(2)] + [(f"incl{d}", P) for d in range(2)]
    + [(f"lev{s}_{d}", P) for s in LEVELS for d in range(2)]
    + [("eye64", RW_N), ("dft_c", 2 * P), ("dft_l", 2 * TT * T), ("reset0", T), ("reset1", T), ("pool_inv", 4 * 16),
       ("eps", 8)])
EPS_RMS, EPS_LN, EPS_GN, EPS_KK, ONE = range(5)
SMALLS, SMALL_N = offsets([("w_aldt", KT * 88), ("w2", RW_DIM), ("a2", RW_DIM), ("g2", RW_DIM)])
SMALLS2, SMALL2_N = offsets([("wf", KT * AH), ("pool_w", 4 * P), ("lru_wa", 4 * P), ("lru_wi", 4 * P)])


def shape_constants():
    out = np.zeros((P, CONST_N), np.float32)

    def put(name, a):
        o, n = CONSTS[name]
        out[:, o:o + n] = np.asarray(a, np.float32).reshape(P, n)

    i, t = np.arange(P)[:, None], np.arange(P)[None, :]
    put("ident", i == t)
    put("ones", np.ones((P, P)))
    put("blk", i // RW_N == t // RW_N)
    put("upto", i <= t)
    put("from", i >= t)
    put("neg_f", NEG * (i > t))
    put("neg_b", NEG * (i < t))
    same = i // RW_C == t // RW_C
    put("strict0", same & (i < t))
    put("strict1", same & (i > t))
    put("incl0", same & (i <= t))
    put("incl1", same & (i >= t))
    for s in LEVELS:
        pair = (i // (2 * s) == t // (2 * s)) & (i // s != t // s)
        sign = -1.0 if s == 1 else 1.0
        put(f"lev{s}_0", sign * (pair & (i < t)))
        put(f"lev{s}_1", sign * (pair & (i > t)))
    put("eye64", (np.arange(P) % RW_N)[:, None] == np.arange(RW_N)[None, :])
    c = 2 * np.pi * (i * t % P) / P
    put("dft_c", np.concatenate([np.cos(c), np.sin(c)], 1) / np.sqrt(P * T))
    l = np.arange(T)
    w = 2 * np.pi * (l[:, None] * l[None, :] % T) / T
    both = np.stack([np.cos(w), -np.sin(w)])
    put("dft_l", both.reshape(2, TT, P, T).transpose(2, 0, 1, 3))
    put("reset0", np.broadcast_to(np.arange(T) % RW_C != 0, (P, T)))
    put("reset1", np.broadcast_to(np.arange(T) % RW_C != RW_C - 1, (P, T)))
    put("pool_inv", np.broadcast_to(np.stack([1.0 / np.minimum(np.arange(1, 17), n) for n in POOL_WINDOWS]).reshape(1, -1), (P, 64)))
    put("eps", np.broadcast_to(np.array([1e-6, 1e-5, 64e-5, 1e-12, 1.0, 0, 0, 0])[None], (P, 8)))
    return out


class Own:

    def __init__(self, eng, sem):
        self.eng, self.sem, self.n = eng, sem, 0

    def step(self, ins):
        ins.then_inc(self.sem, 1)
        self.n += 1

    def settle(self, back=0):
        if self.n > back:
            self.eng.wait_ge(self.sem, self.n - back)


class Banks:

    def __init__(self, full, free):
        self.full, self.free, self.used = full, free, [0] * len(full)

    def take(self, bank, n=1):
        first = self.used[bank]
        self.used[bank] += n
        return bank, first


def branch_kernel(nc, x_t, ctx_t, vecs, consts, smalls, smalls2, c_rows, mod_u, mod_r, ada_r, conv_u, ssd_u, rw_u, gate_u, bo_u, wo_u,
                  mlp_u, in2_u, out2_u, ffn_u, down2_u, out_t):
    ctx = ExitStack()
    with ctx:
        def sb(name, shape):
            return ctx.enter_context(nc.sbuf_tensor(name, shape, F32))

        def sem(name):
            return ctx.enter_context(nc.semaphore(name))

        def sb_and_parts(name, shape):
            with nc.sbuf_tensor(name, shape, F32) as plain:
                pass
            return plain, ctx.enter_context(nc.sbuf_tensor(name + "_parts", shape, F32R))

        ring, ring_parts = sb_and_parts("ring", [P, SLOTS, UNIT])
        hT, hT_parts = sb_and_parts("hT", [P, KT, 2 * T])
        xT = sb("xT", [P, KT, T])
        K = sb("K", [P, CONST_N])
        V = sb("V", [P, VEC_N])
        rows_buf, w_high = sb_and_parts("rows_buf", [P, G_SLOTS, D])
        c_row = sb("c_row", [P, 2, D])
        g_acc = sb("g_acc", [P, G_SLOTS])
        csT = sb("csT", [P, KT, 2])
        modT = sb("modT", [P, 32, 2])
        modx = sb("modx", [P, 64])
        adaT = sb("adaT", [P, 96])
        coef = sb("coef", [P, 6 * KT])
        WORK = (nc.sbuf_bytes_remaining // 4) // 8 * 8 - 8
        work, work_parts = sb_and_parts("work", [P, WORK])
        ps = ctx.enter_context(nc.psum_tensor("ps", [P, 8, 512], F32))

        def kc(name, a=0, b=None):
            o, n = CONSTS[name]
            return K[:, o + a:o + (n if b is None else b)]

        def vec(name, a=0, b=None):
            o, n = VECS[name]
            return V[:, o + a:o + (n if b is None else b)]

        def eps(i):
            return kc("eps", i, i + 1)

        def w(at, n, **kw):
            v = work[:, at:at + n]
            assert at + n <= WORK, (at, n, WORK)
            if kw:
                names = list(kw)
                v = v.rearrange("p (" + " ".join(names) + " z) -> p " + " ".join(names) + " z", **kw)
            return v

        xflat = xT[:, :, :].rearrange("p k t -> p (k t)")

        convT = w(0, CT * T, a=CT)
        fftT = w(CT * T, FT * T, a=FT)
        ssdT = w((CT + FT) * T, ST * T, a=ST)
        rwT = w((CT + FT + ST) * T, RT * T, a=RT)
        W0 = BO_K * T

        w_ready = [sem(f"w_ready{s}") for s in range(SLOTS)]
        w_used = sem("w_used")
        bk = Banks([sem(f"bank_full{b}") for b in range(8)], [sem(f"bank_free{b}") for b in range(8)])
        pe_done = sem("pe_done")
        dve_done = sem("dve_done")
        act_done = sem("act_done")
        pool_done = sem("pool_done")
        vecs_in, x_in, consts_in, smalls_in = sem("vecs_in"), sem("x_in"), sem("consts_in"), sem("smalls_in")

        def full(eng, use):
            eng.wait_ge(bk.full[use[0]], use[1] + 1)

        def emptied(use, ins):
            ins.then_inc(bk.free[use[0]], 1)

        def evacuated(eng, use):
            eng.wait_ge(bk.free[use[0]], use[1] + 1)

        def acquire(pe, use, it=None, k=0):
            if it is not None:
                pe.wait_ge(bk.free[use[0]], it * k + use[1])
            elif use[1] > 0:
                pe.wait_ge(bk.free[use[0]], use[1])

        def unit_done(eng, u, it=0, k=0):
            eng.wait_ge(w_used, u + 1 + (it * k if k else 0))

        units = [0]

        def segment(n):
            at = units[0]
            units[0] += n
            return at

        def slot(n):
            return ring[:, n % SLOTS, :]

        def fetch(sp, src, at, n, size=UNIT):
            def one(j, it, wait):
                u = at + j
                if wait:
                    sp.wait_ge(w_used, u - SLOTS + 1 + (4 * it if it is not None else 0))
                i = j if it is None else j + 4 * it
                sp.dma_start(slot(u)[:, 0:size], src[i][:, 0:size]).then_inc(w_ready[u % SLOTS], 16)

            first = 0
            if at < SLOTS:
                for j in range(SLOTS):
                    one(j, None, False)
                first = SLOTS
            if n - first >= 8:
                rounds = (n - first) // 4
                with sp.Fori(0, rounds) as it:
                    for j in range(4):
                        one(first + j, it, True)
                first += 4 * rounds
            for j in range(first, n):
                one(j, None, True)

        def unit_ready(pe, u, it=0):
            pe.wait_ge(w_ready[u % SLOTS], 16 * (u // SLOTS + 1) + 16 * it)

        def wtile(u, kt):
            return slot(u)[:, kt * P:(kt + 1) * P]

        c_sig, c_silu = sem("c_sig"), sem("c_silu")
        seg_mod0 = segment(32)
        use_mod0 = [bk.take(b, 8) for b in range(2)]
        use_turn = bk.take(2)
        mod_rows = work[0:2, W0 + (KT + 2) * T:W0 + (KT + 2) * T + 2 * KT * P]
        rows_ready = [sem(f"rows_ready{n}") for n in range(G_SLOTS)]
        row_free, col_done = sem("row_free"), sem("col_done")
        c_row_in, c_row_sig, c_row_silu = (sem(n) for n in ("c_row_in", "c_row_sig", "c_row_silu"))
        ADA0 = 64

        def mod_pair(pe, it):
            for j in range(2):
                for o in range(2):
                    u = seg_mod0 + 2 * j + o
                    unit_ready(pe, u, it if it is not None else 0)
                    if o == 0:
                        acquire(pe, use_mod0[j], it, 1)
                    for kt in range(KT):
                        mm = pe.matmul(ps[0:2, j, o * P:(o + 1) * P], csT[:, kt, :], wtile(u, kt), start=kt == 0, stop=kt == KT - 1)
                    mm.then_inc(w_used, 1)

        def mod_row_pair(act, it):
            for j in range(2):
                unit_done(act, seg_mod0 + 2 * j + 1, it if it is not None else 0, 4)
                at = (it if it is not None else 0) * 4 * P + j * 2 * P
                act.activation(mod_rows[:, bass.ds(at, 2 * P)], ps[0:2, j, 0:2 * P], ACT.Copy).then_inc(bk.free[j], 1)

        def fetch_rows(pool, src, first, n):
            with pool.Fori(0, n // G_SLOTS) as it:
                for j in range(G_SLOTS):
                    pool.wait_ge(row_free, it * G_SLOTS + (first + j + 1))
                    pool.dma_start(rows_buf[:, j, :], src[it * G_SLOTS + j]).then_inc(rows_ready[j], 16)

        def column(dve, dst, bias, row, tile, k, it=None, step=0):
            j = tile % G_SLOTS
            off = it * step if it is not None else 0
            dve.wait_ge(rows_ready[j], off * 16 // G_SLOTS + 16 * (tile // G_SLOTS + 1) if it is None else
                        it * (16 * step // G_SLOTS) + 16 * (tile // G_SLOTS + 1))
            dve.wait_ge(col_done, off + tile + 1)
            dve.tensor_tensor_reduce(rows_buf[:, j, :], rows_buf[:, j, :], c_row[:, row, :], 1.0, 0.0, ALU.mult, ALU.add,
                                     g_acc[:, j:j + 1]).then_inc(row_free, 1)
            dve.wait_ge(row_free, off + tile + G_SLOTS + 1)
            dve.tensor_tensor(dst[:, bass.ds(off + k, 1)], g_acc[:, j:j + 1], bias[:, bass.ds(off + k, 1)], ALU.add).then_inc(col_done, 1)

        columns_done = [0]

        def first_columns(dve, n):
            for i in range(columns_done[0], min(columns_done[0] + n, ADA0)):
                column(dve, modx, vec("mod_b", 32, 96), 0, i, i)
            columns_done[0] = min(columns_done[0] + n, ADA0)

        class Mod:
            def sync(sp):
                fetch(sp, mod_u, seg_mod0, 32)

            def scalar(act, own):
                act.dma_start(V[:, :], vecs).then_inc(vecs_in, 16)
                act.dma_start(xT[:, :, :], x_t).then_inc(x_in, 16)
                act.dma_start(ctxT, ctx_t).then_inc(x_in, 16)
                act.dma_start(K[:, :], consts).then_inc(consts_in, 16)
                act.wait_ge(vecs_in, 16)
                act.activation(csT[:, :, :].rearrange("p k c -> p (k c)"), vec("c"), ACT.Sigmoid).then_inc(c_sig, 1)

            def vector(dve, own):
                dve.sem_inc(row_free, G_SLOTS)
                dve.sem_inc(col_done, G_SLOTS)
                dve.wait_ge(c_sig, 1)
                flat = csT[:, :, :].rearrange("p k c -> p (k c)")
                dve.tensor_tensor(flat, flat, vec("c"), ALU.mult).then_inc(c_silu, 1)

            def tensor(pe, own):
                pe.wait_ge(c_silu, 1)
                mod_pair(pe, None)
                with pe.Fori(1, 4) as it:
                    mod_pair(pe, it)

        ctxT = w(W0, KT * T, a=KT)
        smallw = w(WORK - SMALL_N, SMALL_N)

        def small(name, rows=P):
            o, n = SMALLS[name]
            return smallw[0:rows, o:o + n]

        mods0, coef0 = sem("mods0"), sem("coef0")
        sq_done, h_scaled, h_ready = sem("sq_done"), sem("h_scaled"), sem("h_ready")
        use_ssq0 = bk.take(3)
        rtb = w(W0 + KT * T, 2 * T)
        gsc0 = coef[:, 0:2 * KT].rearrange("p (k c) -> p k c", c=2)

        class Norm0:
            def scalar(act, own):
                mod_row_pair(act, None)
                act.wait_ge(x_in, 32)
                act.activation(hT[:, :, 0:T], xT[:, :, :], ACT.Square).then_inc(sq_done, 1)
                act.activation(hT[:, :, T:], ctxT, ACT.Square).then_inc(sq_done, 1)
                with act.Fori(1, 4) as it:
                    mod_row_pair(act, it)
                act.dma_start(smallw, smalls).then_inc(smalls_in, 16)
                for n in range(2):
                    act.dma_start(c_row[:, n, :], c_rows[n:n + 1, :].to_broadcast([P, D])).then_inc(c_row_in, 16)
                full(act, use_ssq0)
                act.wait_ge(consts_in, 16)
                emptied(use_ssq0, act.activation(rtb, ps[:, 3, :], ACT.Sqrt, bias=eps(EPS_RMS), scale=1.0 / D))
                with act.Fori(4, 8) as it:
                    mod_row_pair(act, it)
                act.wait_ge(c_row_in, 32)
                act.activation(rows_buf[:, :, :], c_row[:, :, :], ACT.Sigmoid).then_inc(c_row_sig, 1)
                act.wait_ge(mods0, 1)
                for n in range(2 * KT):
                    kt, c = n % KT, n // KT
                    act.wait_ge(h_scaled, n + 1)
                    act.activation(hT[:, kt, c * T:(c + 1) * T], hT[:, kt, c * T:(c + 1) * T], ACT.Identity,
                                   bias=modT[:, kt, c:c + 1]).then_inc(h_ready, 1)

            def tensor(pe, own):
                pe.wait_ge(sq_done, 2)
                pe.wait_ge(consts_in, 16)
                for kt in range(KT):
                    mm = pe.matmul(ps[:, 3, :], kc("ones"), hT[:, kt, :], start=kt == 0, stop=kt == KT - 1)
                mm.then_inc(bk.full[3], 1)
                with pe.Fori(4, 8) as it:
                    mod_pair(pe, it)
                for b in range(2):
                    pe.wait_ge(bk.free[b], 8)
                for n in range(2 * KT):
                    mm = pe.matmul(ps[:, 2, 2 * n:2 * n + 2], mod_rows[:, n * P:(n + 1) * P], kc("ident")[0:2, 0:2], start=True, stop=True)
                mm.then_inc(bk.full[2], 1)

            def vector(dve, own):
                evacuated(dve, use_ssq0)
                own.step(dve.reciprocal(rtb, rtb))
                full(dve, use_turn)
                bias = vec("mod_b", 0, 32).unsqueeze(2).to_broadcast([P, 32, 2])
                emptied(use_turn, dve.tensor_tensor(modT[:, 0:32, :], ps[:, 2, 0:64].rearrange("p (u c) -> p u c", c=2), bias, ALU.add))
                evacuated(dve, use_turn)
                dve.sem_inc(mods0, 1)
                g = vec("norm_g", 0, KT).unsqueeze(2).to_broadcast([P, KT, 2])
                own.step(dve.scalar_tensor_tensor(gsc0, modT[:, KT:2 * KT, :], 1.0, g, ALU.add, ALU.mult))
                own.settle()
                for n in range(2 * KT):
                    kt, c = n % KT, n // KT
                    src = xT[:, kt, :] if c == 0 else ctxT[:, kt, :]
                    dve.scalar_tensor_tensor(hT[:, kt, c * T:(c + 1) * T], src, gsc0[:, kt, c:c + 1],
                                             rtb[:, c * T:(c + 1) * T], ALU.mult, ALU.mult).then_inc(h_scaled, 1)
                dve.wait_ge(c_row_sig, 1)
                dve.tensor_tensor(c_row[:, :, :], c_row[:, :, :], rows_buf[:, :, :], ALU.mult).then_inc(c_row_silu, 1)

        def gemm_pair(pe, u, rhs, outs, uses, it=None, k=0, step=0):
            for o in range(2):
                unit_ready(pe, u + o, it * (step // SLOTS) if it is not None else 0)
                if o < len(uses):
                    acquire(pe, uses[o], it, k)
                for kt in range(KT):
                    mm = pe.matmul(outs[o], wtile(u + o, kt), rhs(kt), start=kt == 0, stop=kt == KT - 1)
                mm.then_inc(w_used, 1)

        def main_rhs(kt):
            return hT[:, kt, 0:T]

        def both_rhs(kt):
            return hT[:, kt, :]

        def pair(b):
            return [ps[:, b, 0:T], ps[:, b, T:]]

        seg_cf = segment(12)
        cf_use = [bk.take(n % 2) for n in range(6)]
        C0 = W0
        sgT = w(C0, CT * T, a=CT)
        valT = w(C0 + CT * T, CT * T, a=CT)
        SEG = GRID_W + CONV_TAPS - 1
        cbuf_flat = w(C0 + 2 * CT * T, CT * ROWS * SEG)
        cbuf = cbuf_flat.rearrange("p (a r z) -> p a r z", a=CT, r=ROWS)
        c1 = C0 + 2 * CT * T + CT * ROWS * SEG
        ufT = w(c1, FT * T, a=FT)
        z1 = w(c1 + FT * T, FT * TT * 2 * P, a=FT, l=TT)
        c2 = c1 + FT * T + FT * TT * 2 * P
        cacc = w(c2, CT * T, a=CT)
        csq = w(c2 + CT * T, CT * T, a=CT)
        cmu = w(c2 + 2 * CT * T, T)
        crs = w(c2 + 2 * CT * T + T, T)
        conv_sum, conv_cent, conv_sq, conv_norm = (sem(n) for n in ("conv_sum", "conv_cent", "conv_sq", "conv_norm"))
        conv_ready = sem("conv_ready")
        use_f1 = [bk.take(3 + g) for g in range(FT)]
        use_f2 = [bk.take(3 + g) for g in range(2)]
        use_mu = bk.take(7)
        use_var = bk.take(7)

        def bc(v, n):
            return v.unsqueeze(1).to_broadcast([P, n, v.shape[-1]])

        def flat(v):
            return v.rearrange("p a t -> p (a t)")

        class ConvFft:
            def sync(sp):
                fetch(sp, conv_u, seg_cf, 12)

            def tensor(pe, own):
                pe.wait_ge(h_ready, KT)
                for n in range(6):
                    gemm_pair(pe, seg_cf + 2 * n, main_rhs, pair(n % 2), [cf_use[n]])
                for g in range(FT):
                    evacuated(pe, cf_use[4 + g // 2])
                    acquire(pe, use_f1[g])
                    for l in range(TT):
                        mm = pe.matmul(ps[:, 3 + g, l * 2 * P:(l + 1) * 2 * P], ufT[:, g, l * P:(l + 1) * P], kc("dft_c"),
                                       start=True, stop=True)
                    mm.then_inc(bk.full[3 + g], 1)
                for g in range(FT):
                    evacuated(pe, use_f1[g])
                    b = 3 + g // 2
                    if g % 2 == 0:
                        acquire(pe, use_f2[g // 2])
                    for i in range(2):
                        for l in range(TT):
                            at = (i * TT + l) * T
                            mm = pe.matmul(ps[:, b, g % 2 * T:(g % 2 + 1) * T], z1[:, g, l, i * P:(i + 1) * P],
                                           kc("dft_l", at, at + T), start=i + l == 0, stop=i + l == TT)
                    if g % 2:
                        mm.then_inc(bk.full[b], 1)

            def tensor_norm(pe, n):
                s, src, use = ((conv_sum, cacc, use_mu), (conv_sq, csq, use_var))[n]
                pe.wait_ge(s, 1)
                acquire(pe, use)
                for t in range(CT):
                    mm = pe.matmul(ps[:, 7, 0:T], kc("ones"), src[:, t, :], start=t == 0, stop=t == CT - 1)
                mm.then_inc(bk.full[7], 1)

            def scalar(act, own):
                for n in range(6):
                    unit_done(act, seg_cf + 2 * n + 1)
                    i = n % 2 * 2
                    dst, f = ((sgT, ACT.Sigmoid), (valT, ACT.Copy), (ufT, ACT.Copy))[n // 2]
                    emptied(cf_use[n], act.activation(flat(dst[:, i:i + 2, :]), ps[:, n % 2, :], f))
                for g in range(FT):
                    full(act, use_f1[g])
                    emptied(use_f1[g], act.activation(z1[:, g, :, :].rearrange("p l n -> p (l n)"), ps[:, 3 + g, :], ACT.Copy))
                for h in range(2):
                    full(act, use_f2[h])
                    emptied(use_f2[h], act.activation(flat(fftT[:, 2 * h:2 * h + 2, :]), ps[:, 3 + h, :], ACT.Copy))

            def scalar_norm(act, own):
                full(act, use_mu)
                emptied(use_mu, act.activation(cmu, ps[:, 7, 0:T], ACT.Copy, scale=1.0 / CONV))
                act.wait_ge(conv_cent, 1)
                act.activation(flat(csq), flat(cacc), ACT.Square).then_inc(conv_sq, 1)
                full(act, use_var)
                emptied(use_var, act.activation(crs, ps[:, 7, 0:T], ACT.Sqrt, bias=eps(EPS_LN), scale=1.0 / CONV))
                act.wait_ge(conv_norm, 1)
                for t in range(CT):
                    act.activation(convT[:, t, :], cacc[:, t, :], ACT.Silu, bias=vec("conv_ln_b", t, t + 1),
                                   scale=vec("conv_ln_g", t, t + 1)).then_inc(conv_ready, 1)

            def vector(dve, own):
                dve.wait_ge(h_scaled, 2 * KT)
                own.step(dve.memset(cbuf_flat, 0.0))
                own.settle()
                evacuated(dve, cf_use[1])
                evacuated(dve, cf_use[2])
                evacuated(dve, cf_use[3])
                for t in range(CT):
                    own.step(dve.tensor_tensor(cbuf[:, t, :, CONV_TAPS // 2:CONV_TAPS // 2 + GRID_W],
                                               valT[:, t, :].rearrange("p (r z) -> p r z", r=ROWS),
                                               sgT[:, t, :].rearrange("p (r z) -> p r z", r=ROWS), ALU.mult))
                for k in range(CONV_TAPS):
                    for t in range(CT):
                        src = cbuf[:, t, :, k:k + GRID_W]
                        dst = cacc[:, t, :].rearrange("p (r z) -> p r z", r=ROWS)
                        tap = vec("conv_w", k * CT + t, k * CT + t + 1)
                        own.settle(CT - 1)
                        if k == 0:
                            ins = dve.tensor_scalar(dst, src, tap, vec("conv_b", t, t + 1), ALU.mult, ALU.add)
                        else:
                            ins = dve.scalar_tensor_tensor(dst, src, tap, dst, ALU.mult, ALU.add)
                        if k == CONV_TAPS - 1 and t == CT - 1:
                            ins.then_inc(conv_sum, 1)
                        else:
                            own.step(ins)
                    if k % 3 == 2:
                        first_columns(dve, 1)

            def vector_norm(dve, own):
                evacuated(dve, use_mu)
                dve.wait_ge(conv_sum, 1)
                dve.tensor_tensor(cacc, cacc, bc(cmu, CT), ALU.subtract).then_inc(conv_cent, 1)
                evacuated(dve, use_var)
                own.step(dve.reciprocal(crs, crs))
                own.settle()
                dve.wait_ge(conv_sq, 1)
                dve.tensor_tensor(cacc, cacc, bc(crs, CT), ALU.mult).then_inc(conv_norm, 1)

        H2 = 2 * SSD_H
        NT = 2 * TT
        S0 = W0
        zT = w(S0, ST * T, a=ST)
        bT = w(S0 + 1536, SSD_G * 2 * T, a=SSD_G)
        b_tok = w(S0 + 3584, NT * SSD_G * SSD_N, a=NT)
        xsT = w(S0 + 5632, ST * 2 * T, a=ST)
        PADW = T + SSD_TAPS - 1
        pads = w(S0 + 8704, 2 * 2 * PADW).rearrange("p (r c t) -> p r c t", r=2, c=2)
        E0 = S0 + 8704 + 4 * PADW
        y_s = w(E0, SSD_DIM)
        dts = w(E0 + SSD_DIM, 8 * NT * H2).rearrange("p (i a h) -> p i a h", i=8, a=NT)
        dt_s, a_s, cs_s, tot_s, wdec_s, ecs_s, etot_s, ncs_s = (dts[:, n] for n in range(8))
        al_raw = work[0:LORA, E0 + SSD_DIM + 8 * NT * H2:E0 + SSD_DIM + 8 * NT * H2 + 2 * T]
        assert E0 + SSD_DIM + 8 * NT * H2 + 2 * T <= WORK - SMALL_N + KT * 88
        xs_tok = xflat[:, 0:NT * SSD_DIM].rearrange("p (a n) -> p a n", a=NT)
        cT = xflat[:, NT * SSD_DIM:].rearrange("p (a n) -> p a n", a=SSD_G)
        RW0 = (CT + FT + ST) * T
        sp_t = [w(RW0 + n * NT * H2, NT * H2, a=NT) for n in range(4)]
        w_aldt = small("w_aldt").rearrange("p (k n) -> p k n", k=KT)

        use_al, use_dt = bk.take(3), bk.take(4)
        seg_ssd = segment(20)
        ssd_uses = [[bk.take(n % 2)] for n in range(3)] + [[bk.take(0), bk.take(1)] for _ in range(5)] + \
            [[bk.take(n % 2)] for n in range(2)]
        use_cs = bk.take(4)
        use_cb = [bk.take(5 + n) for n in range(TT)]
        use_tr = [bk.take(3 + n % 5) for n in range(10)]
        pad_zero, pad_in, conv5, silu5, a_ready, sp_abs, sp_e, sp_u, sp_ln, dt_done = (sem(n) for n in (
            "pad_zero", "pad_in", "conv5", "silu5", "a_ready", "sp_abs", "sp_e", "sp_u", "sp_ln", "dt_done"))
        exps_ready, a_neg = sem("exps_ready"), sem("a_neg")

        def conv_dst(t):
            if t < ST:
                return xsT[:, t, :]
            return bT[:, t - ST, :] if t < ST + SSD_G else cT[:, t - ST - SSD_G, :]

        class SsdIn:
            def sync(sp):
                fetch(sp, ssd_u, seg_ssd, 20)

            def gpsimd(pool, own):
                pool.wait_ge(c_row_silu, 1)
                fetch_rows(pool, mod_r, 0, ADA0)

            def tensor(pe, own):
                pe.wait_ge(smalls_in, 16)
                pe.wait_ge(h_ready, 2 * KT)
                acquire(pe, use_al)
                for kt in range(KT):
                    mm = pe.matmul(ps[0:LORA, 3, :], w_aldt[:, kt, 0:LORA], hT[:, kt, :], start=kt == 0, stop=kt == KT - 1)
                mm.then_inc(bk.full[3], 1)
                acquire(pe, use_dt)
                for a in range(NT):
                    for kt in range(KT):
                        mm = pe.matmul(ps[:, 4, a * H2:(a + 1) * H2], hT[:, kt, a * P:(a + 1) * P], w_aldt[:, kt, LORA:],
                                       start=kt == 0, stop=kt == KT - 1)
                mm.then_inc(bk.full[4], 1)
                for n in range(10):
                    both = 3 <= n < 8
                    outs = [ps[:, 0, :], ps[:, 1, :]] if both else pair(ssd_uses[n][0][0])
                    gemm_pair(pe, seg_ssd + 2 * n, both_rhs if both else main_rhs, outs, ssd_uses[n])
                    if n < 2:
                        ConvFft.tensor_norm(pe, n)
                pe.wait_ge(a_ready, 1)
                acquire(pe, use_cs)
                for a in range(NT):
                    at = a * 2 * H2
                    pe.matmul(ps[:, 4, at:at + SSD_H], kc("upto"), a_s[:, a, 0:SSD_H], start=True, stop=True)
                    pe.matmul(ps[:, 4, at + SSD_H:at + H2], kc("from"), a_s[:, a, SSD_H:], start=True, stop=True)
                    mm = pe.matmul(ps[:, 4, at + H2:at + 2 * H2], kc("ones"), a_s[:, a, :], start=True, stop=True)
                mm.then_inc(bk.full[4], 1)
                pe.wait_ge(silu5, XT_TILES)
                for a in range(TT):
                    acquire(pe, use_cb[a])
                    for g in range(SSD_G):
                        mm = pe.matmul(ps[:, 5 + a, g * P:(g + 1) * P], bT[:, g, a * P:(a + 1) * P], cT[:, g, a * P:(a + 1) * P],
                                       start=True, stop=True)
                    mm.then_inc(bk.full[5 + a], 1)
                for n in range(10):
                    src = conv_dst(n)
                    acquire(pe, use_tr[n])
                    b = use_tr[n][0]
                    for a in range(NT):
                        mm = pe.transpose(ps[:, b, a * P:(a + 1) * P], src[:, a * P:(a + 1) * P], kc("ident"))
                    mm.then_inc(bk.full[b], 1)

            def scalar(act, own):
                full(act, use_al)
                full(act, use_dt)
                emptied(use_al, act.activation(al_raw, ps[0:LORA, 3, :], ACT.Copy))
                act.activation(sp_t[3][:, 0, :], vec("A_log"), ACT.Exp).then_inc(a_neg, 1)
                for n in range(3):
                    unit_done(act, seg_ssd + 2 * n + 1)
                    emptied(ssd_uses[n][0], act.activation(flat(zT[:, 2 * n:2 * n + 2, :]), ps[:, n % 2, :], ACT.Silu))
                act.wait_ge(sp_abs, 1)
                act.activation(sp_t[1], sp_t[1], ACT.Exp, scale=-1.0).then_inc(sp_e, 1)
                act.wait_ge(sp_u, 1)
                act.activation(dt_s, sp_t[2], ACT.Ln).then_inc(sp_ln, 1)
                for n in range(3, 10):
                    unit_done(act, seg_ssd + 2 * n + 1)
                    for o in range(2):
                        t = 2 * (n - 3) + o
                        r = t % 2
                        if t == 0:
                            act.wait_ge(pad_zero, 1)
                        if t >= 2:
                            act.wait_ge(conv5, t - 1)
                        if n < 8:
                            ins = act.activation(pads[:, r, :, 2:2 + T], ps[:, o, :].rearrange("p (c t) -> p c t", c=2), ACT.Copy)
                            emptied(ssd_uses[n][o], ins)
                        else:
                            ins = act.activation(pads[:, r, 0, 2:2 + T], ps[:, n % 2, o * T:(o + 1) * T], ACT.Copy)
                            if o == 1:
                                emptied(ssd_uses[n][0], ins)
                            else:
                                ins.then_inc(pad_in, 1)
                    if n >= 3:
                        for o in range(2):
                            t = 2 * (n - 3) + o
                            act.wait_ge(conv5, t + 1)
                            act.activation(conv_dst(t), conv_dst(t), ACT.Silu).then_inc(silu5, 1)
                full(act, use_cs)
                act.activation(cs_s, ps[:, 4, 0:NT * 2 * H2].rearrange("p (a c h) -> p a c h", a=NT, c=2)[:, :, 0, :], ACT.Copy)
                emptied(use_cs, act.activation(
                    tot_s, ps[:, 4, 0:NT * 2 * H2].rearrange("p (a c h) -> p a c h", a=NT, c=2)[:, :, 1, :], ACT.Copy))
                evacuated(act, use_cs)
                act.activation(ecs_s, cs_s, ACT.Exp).then_inc(exps_ready, 1)
                act.activation(etot_s, tot_s, ACT.Exp).then_inc(exps_ready, 1)
                act.activation(ncs_s, cs_s, ACT.Copy, scale=-1.0).then_inc(exps_ready, 1)
                act.wait_ge(dt_done, 1)
                act.activation(wdec_s, wdec_s, ACT.Exp).then_inc(exps_ready, 1)
                for a in range(TT):
                    full(act, use_cb[a])
                    emptied(use_cb[a], act.activation(cb_s[:, a, :], ps[:, 5 + a, :], ACT.Copy))
                for n in range(10):
                    full(act, use_tr[n])
                    src = ps[:, use_tr[n][0], :].rearrange("p (a n) -> p a n", a=NT)
                    dst = xs_tok[:, :, n * P:(n + 1) * P] if n < ST else b_tok[:, :, (n - ST) * P:(n - ST + 1) * P]
                    emptied(use_tr[n], act.activation(dst, src, ACT.Copy))

            def vector(dve, own):
                full(dve, use_dt)
                z, e, u, t = sp_t
                dve.wait_ge(a_neg, 1)
                own.step(dve.tensor_scalar(vec("A_log"), t[:, 0, :], -1.0, None, ALU.mult))
                emptied(use_dt, dve.tensor_tensor(z, ps[:, 4, 0:NT * H2].rearrange("p (a h) -> p a h", a=NT),
                                                  bc(vec("dt_bias"), NT), ALU.add))
                evacuated(dve, use_dt)
                dve.scalar_tensor_tensor(e, z, -1.0, z, ALU.mult, ALU.max).then_inc(sp_abs, 1)
                own.step(dve.memset(pads.rearrange("p r c t -> p (r c t)"), 0.0))
                own.settle()
                dve.sem_inc(pad_zero, 1)
                dve.wait_ge(sp_e, 1)
                dve.tensor_scalar(u, e, 1.0, None, ALU.add).then_inc(sp_u, 1)
                dve.wait_ge(sp_u, 1)
                own.step(dve.scalar_tensor_tensor(e, u, -1.0, e, ALU.add, ALU.subtract))
                own.step(dve.reciprocal(t, u))
                own.settle()
                own.step(dve.tensor_tensor(e, e, t, ALU.mult))
                own.settle()
                own.step(dve.scalar_tensor_tensor(e, z, 0.0, e, ALU.max, ALU.subtract))
                own.settle()
                dve.wait_ge(sp_ln, 1)
                own.step(dve.tensor_tensor(dt_s, dt_s, e, ALU.add))
                own.settle()
                dve.tensor_tensor(a_s, dt_s, bc(vec("A_log"), NT), ALU.mult).then_inc(a_ready, 1)
                for t in range(XT_TILES):
                    n = 3 + t // 2
                    if n < 8:
                        evacuated(dve, ssd_uses[n][t % 2])
                    elif t % 2:
                        evacuated(dve, ssd_uses[n][0])
                    else:
                        dve.wait_ge(pad_in, n - 7)
                    for k in range(SSD_TAPS):
                        if n < 8:
                            src = pads[:, t % 2, :, k:k + T]
                            dst = conv_dst(t).rearrange("p (c t) -> p c t", c=2)
                        else:
                            src, dst = pads[:, t % 2, 0, k:k + T], conv_dst(t)
                        tap = vec("ssd_cw", k * XT_TILES + t, k * XT_TILES + t + 1)
                        if k == 0:
                            own.step(dve.tensor_scalar(dst, src, tap, vec("ssd_cb", t, t + 1), ALU.mult, ALU.add))
                            own.settle()
                            continue
                        ins = dve.scalar_tensor_tensor(dst, src, tap, dst, ALU.mult, ALU.add)
                        if k < SSD_TAPS - 1:
                            own.step(ins)
                            own.settle()
                        else:
                            ins.then_inc(conv5, 1)
                    first_columns(dve, 2 if n < 8 else 1)
                    if t == XT_TILES - 1:
                        first_columns(dve, 2)
                evacuated(dve, use_cs)
                dve.tensor_tensor(wdec_s, tot_s, cs_s, ALU.subtract).then_inc(dt_done, 1)

        cb_s = w(S0 + 8704, TT * SSD_G * P, a=TT)
        st_s = w(S0 + 5632, 4 * SSD_DIM).rearrange("p (d a n) -> p d a n", d=2, a=TT)
        xdd = w(S0 + 1536, 2 * SSD_DIM, a=2)
        lq = w(RW0, 2 * 4 * P, a=2)
        mh = w((CT + FT) * T, SSD_H * P, a=SSD_H)
        HALF = SSD_DIM // 2
        ORDER = [[(2, False), (3, True), (0, True)], [(3, False), (2, True), (1, True)]]

        def heads_bc(col, n=SSD_P):
            return col.unsqueeze(2).to_broadcast([P, col.shape[-1], n])

        use_st = [[(bk.take(3 + 2 * d), bk.take(4 + 2 * d)) for d in range(2)] for _ in range(3)]
        use_l, use_y, use_off, use_yt = {}, {}, {}, {}
        for a in range(TT):
            for q in range(3):
                for d in range(2):
                    use_l[a, q, d] = bk.take((7, 3)[d])
            use_y[a] = (bk.take(4), bk.take(5))
            for d in range(2):
                use_off[a, d] = (bk.take(6), bk.take(7))
            use_yt[a] = (bk.take(3), bk.take(4))
        use_ssdvar = bk.take(5)
        xdd_ready, st_ready, m_ready, y_ready, yz_ready, ysq, ssd_ready = (sem(n) for n in (
            "xdd_ready", "st_ready", "m_ready", "y_ready", "yz_ready", "ysq", "ssd_ready"))
        srt = w(E0, T)
        ssq = w(S0 + 5632, ST * T, a=ST)

        class SsdScan:
            def tensor(pe, own):
                for n in range(3):
                    for d in range(2):
                        a = ORDER[d][n][0]
                        pe.wait_ge(xdd_ready, 2 * n + d + 1)
                        for h in range(2):
                            use = use_st[n][d][h]
                            acquire(pe, use)
                            for g in range(2):
                                mm = pe.matmul(ps[:, use[0], g * 192:(g + 1) * 192], b_tok[:, a, (2 * h + g) * P:(2 * h + g + 1) * P],
                                               xdd[:, d, (2 * h + g) * 192:(2 * h + g + 1) * 192], start=True, stop=True)
                            mm.then_inc(bk.full[use[0]], 1)
                for a in range(TT):
                    for q in range(3):
                        for d in range(2):
                            use = use_l[a, q, d]
                            acquire(pe, use)
                            pe.matmul(ps[:, use[0], :].rearrange("p (h t) -> p h t", h=4), kc("ident"), bc(kc(("neg_f", "neg_b")[d]), 4),
                                      start=True, stop=False)
                            for h in range(4):
                                col = d * SSD_H + 4 * q + h
                                mm = pe.matmul(ps[:, use[0], h * P:(h + 1) * P], a_s[:, a, col:col + 1].to_broadcast([P, P]),
                                               kc(("upto", "from")[d]), start=False, stop=h == 3)
                            mm.then_inc(bk.full[use[0]], 1)
                    for h in range(SSD_H):
                        pe.wait_ge(m_ready, a * SSD_H + h + 1)
                        b, at = 4 + h // 8, h % 8 * SSD_P
                        if h % 8 == 0:
                            acquire(pe, use_y[a][h // 8])
                        mm = pe.matmul(ps[:, b, at:at + SSD_P], mh[:, h, :], xs_tok[:, a, h * SSD_P:(h + 1) * SSD_P], start=True, stop=True)
                        if h in (7, SSD_H - 1):
                            mm.then_inc(bk.full[b], 1)
                    for d in range(2):
                        pe.wait_ge(st_ready, 6)
                        for h in range(2):
                            use = use_off[a, d][h]
                            acquire(pe, use)
                            for g in range(2):
                                gg = 2 * h + g
                                mm = pe.matmul(ps[:, use[0], g * 192:(g + 1) * 192], cT[:, gg, a * P:(a + 1) * P],
                                               st_s[:, d, a, gg * 192:(gg + 1) * 192], start=True, stop=True)
                            mm.then_inc(bk.full[use[0]], 1)
                    pe.wait_ge(y_ready, a + 1)
                    for n in range(ST):
                        use = use_yt[a][n // 4]
                        if n % 4 == 0:
                            acquire(pe, use)
                        mm = pe.transpose(ps[:, use[0], n % 4 * P:(n % 4 + 1) * P], y_s[:, n * P:(n + 1) * P], kc("ident"))
                        if n in (3, ST - 1):
                            mm.then_inc(bk.full[use[0]], 1)
                pe.wait_ge(ysq, 1)
                acquire(pe, use_ssdvar)
                for n in range(ST):
                    mm = pe.matmul(ps[:, 5, 0:T], kc("ones"), ssq[:, n, :], start=n == 0, stop=n == ST - 1)
                mm.then_inc(bk.full[5], 1)

            def scalar(act, own):
                act.wait_ge(exps_ready, 3)
                n = 0
                for a in range(TT):
                    for q in range(3):
                        for d in range(2):
                            use = use_l[a, q, d]
                            full(act, use)
                            if n >= 2:
                                act.wait_ge(m_ready, (n // 2) * 4)
                            for h in range(4):
                                col = d * SSD_H + 4 * q + h
                                ins = act.activation(lq[:, d, h * P:(h + 1) * P], ps[:, use[0], h * P:(h + 1) * P], ACT.Exp,
                                                     bias=ncs_s[:, a, col:col + 1])
                            emptied(use, ins)
                            n += 1
                act.wait_ge(yz_ready, 2)
                act.activation(flat(ssq), flat(zT), ACT.Square).then_inc(ysq, 1)
                full(act, use_ssdvar)
                emptied(use_ssdvar, act.activation(srt, ps[:, 5, 0:T], ACT.Sqrt, bias=eps(EPS_RMS), scale=1.0 / SSD_DIM))

            def vector(dve, own):
                dve.wait_ge(exps_ready, 4)
                own.step(dve.tensor_tensor(wdec_s, wdec_s, dt_s, ALU.mult))
                own.settle()
                for n in use_tr:
                    evacuated(dve, n)
                for n in range(3):
                    for d in range(2):
                        a = ORDER[d][n][0]
                        if n:
                            for h in range(2):
                                full(dve, use_st[n - 1][d][h])
                        dve.tensor_tensor(xdd[:, d, :].rearrange("p (h c) -> p h c", c=SSD_P),
                                          xs_tok[:, a, :].rearrange("p (h c) -> p h c", c=SSD_P),
                                          heads_bc(wdec_s[:, a, d * SSD_H:(d + 1) * SSD_H]), ALU.mult).then_inc(xdd_ready, 1)
                    for d in range(2):
                        a = ORDER[d][n][0]
                        first = (0, 1)[d]
                        src = None if n == 0 else st_s[:, d, first, :]
                        dst = st_s[:, d, first if n < 2 else 1 - first, :]
                        if src is not None:
                            own.step(dve.tensor_tensor(dst.rearrange("p (h c) -> p h c", c=SSD_P), src.rearrange("p (h c) -> p h c", c=SSD_P),
                                                       heads_bc(etot_s[:, a, d * SSD_H:(d + 1) * SSD_H]), ALU.mult))
                            own.settle()
                        for h in range(2):
                            use = use_st[n][d][h]
                            full(dve, use)
                            part = dst[:, h * HALF:(h + 1) * HALF]
                            if src is None:
                                ins = dve.tensor_copy(part, ps[:, use[0], 0:HALF])
                            else:
                                ins = dve.tensor_tensor(part, part, ps[:, use[0], 0:HALF], ALU.add)
                            emptied(use, ins)
                        for h in range(2):
                            evacuated(dve, use_st[n][d][h])
                        dve.sem_inc(st_ready, 1)
                for a in range(TT):
                    for q in range(3):
                        evacuated(dve, use_l[a, q, 0])
                        evacuated(dve, use_l[a, q, 1])
                        for h in range(4):
                            hh = 4 * q + h
                            if a and hh in (0, 8):
                                full(dve, use_y[a - 1][hh // 8])
                            own.step(dve.tensor_scalar(mh[:, hh, :], lq[:, 0, h * P:(h + 1) * P], dt_s[:, a, hh:hh + 1], None, ALU.mult))
                            own.settle()
                            own.step(dve.scalar_tensor_tensor(mh[:, hh, :], lq[:, 1, h * P:(h + 1) * P],
                                                              dt_s[:, a, SSD_H + hh:SSD_H + hh + 1], mh[:, hh, :], ALU.mult, ALU.add))
                            own.settle()
                            g = hh // 3
                            dve.tensor_tensor(mh[:, hh, :], mh[:, hh, :], cb_s[:, a, g * P:(g + 1) * P], ALU.mult).then_inc(m_ready, 1)
                    if a:
                        for u in use_yt[a - 1]:
                            full(dve, u)
                    own.step(dve.tensor_tensor(y_s.rearrange("p (h c) -> p h c", c=SSD_P), xs_tok[:, a, :].rearrange("p (h c) -> p h c", c=SSD_P),
                                               heads_bc(vec("ssd_D")), ALU.mult))
                    own.settle()
                    for i, (lo, hi) in enumerate(((0, 512), (512, SSD_DIM))):
                        full(dve, use_y[a][i])
                        emptied(use_y[a][i], dve.tensor_tensor(y_s[:, lo:hi], y_s[:, lo:hi], ps[:, 4 + i, 0:hi - lo], ALU.add))
                    for i in range(2):
                        evacuated(dve, use_y[a][i])
                    for d in range(2):
                        for i in range(2):
                            use = use_off[a, d][i]
                            full(dve, use)
                            for h in range(6):
                                hh = 6 * i + h
                                part = y_s[:, hh * SSD_P:(hh + 1) * SSD_P]
                                ins = dve.scalar_tensor_tensor(part, ps[:, use[0], h * SSD_P:(h + 1) * SSD_P],
                                                               ecs_s[:, a, d * SSD_H + hh:d * SSD_H + hh + 1], part, ALU.mult, ALU.add)
                                if h < 5:
                                    own.step(ins)
                            emptied(use, ins)
                        for i in range(2):
                            evacuated(dve, use_off[a, d][i])
                    dve.sem_inc(y_ready, 1)
                    for i, (lo, hi) in enumerate(((0, 4), (4, ST))):
                        use = use_yt[a][i]
                        full(dve, use)
                        part = zT[:, lo:hi, a * P:(a + 1) * P]
                        emptied(use, dve.tensor_tensor(part, part, ps[:, use[0], 0:(hi - lo) * P].rearrange("p (n t) -> p n t", t=P), ALU.mult))
                    for u in use_yt[a]:
                        evacuated(dve, u)
                    dve.sem_inc(yz_ready, 1)
                evacuated(dve, use_ssdvar)
                own.step(dve.reciprocal(srt, srt))
                own.settle()
                for n in range(ST):
                    dve.scalar_tensor_tensor(ssdT[:, n, :], zT[:, n, :], vec("ssd_ng", n, n + 1), srt, ALU.mult, ALU.mult).then_inc(ssd_ready, 1)

        R0 = W0
        kT = w(R0, RT * 2 * T, a=RT)
        v_tok = w(R0 + 2048, NT * RW_DIM, a=NT)
        lora_t = w(R0 + 4096, 2 * T)
        G0 = R0 + 4608
        PADR = T + 2
        rpads = w(G0, 2 * 2 * PADR).rearrange("p (r c t) -> p r c t", r=2, c=2)
        vT = w(G0 + 1032, RT * 2 * T, a=RT)
        aT = w(G0 + 3080, RT * 2 * T, a=RT)
        sq_r = w(G0 + 5128, 2 * 2 * T, a=2)
        t1_r = w(G0 + 6152, 2 * T)
        assert G0 + 6152 + 2 * T <= E0 + SSD_DIM + 8 * NT * H2
        rk_t = w(G0, RT * T, a=RT)
        gl_r = w(RW0, T)
        rt_r = w(RW0 + T, 2 * T)
        rT = xflat[:, 0:RT * T].rearrange("p (a t) -> p a t", a=RT)
        bonusT = xflat[:, RT * T:2 * RT * T].rearrange("p (a t) -> p a t", a=RT)
        gT = xflat[:, 2 * RT * T:3 * RT * T].rearrange("p (a t) -> p a t", a=RT)
        y_tok = xflat[:, 3 * RT * T:].rearrange("p (a n) -> p a n", a=TT)

        def kkT(j):
            return hT[:, j:j + RT + 1:RT, T:]

        def kaT(j):
            return hT[:, 2 * RT + j:3 * RT + j + 1:RT, T:]

        seg_rw = segment(14)
        rw_uses = [[bk.take(n % 2)] for n in range(2)] + [[bk.take(0), bk.take(1)] for _ in range(5)]
        rot = [0]

        def aux():
            rot[0] += 1
            return bk.take(3 + rot[0] % 5)

        use_vt = [aux() for _ in range(NT)]
        use_a = [aux() for _ in range(RT)]
        use_g = [aux() for _ in range(2)]
        use_kk = [aux() for _ in range(RT)]
        use_bonus = [aux() for _ in range(2)]
        rpad_zero, rpad_in, shifted, lora_ready, al_ready, gl_ready, kk_raw, kk_sq, kk_ready, rk_ready, prep_ready = (sem(n) for n in (
            "rpad_zero", "rpad_in", "shifted", "lora_ready", "al_ready", "gl_ready", "kk_raw", "kk_sq", "kk_ready", "rk_ready",
            "prep_ready"))
        R_TILES = 15

        def shift_dst(t):
            if t < RT:
                return rT[:, t, :]
            if t < 2 * RT:
                return kT[:, t - RT, :]
            if t < 3 * RT:
                return vT[:, t - 2 * RT, :]
            return (lora_t, gl_r, al_raw)[t - 3 * RT]

        class RwIn:
            def sync(sp):
                fetch(sp, rw_u, seg_rw, 14)

            def tensor(pe, own):
                for n in range(7):
                    both = n >= 2
                    outs = [ps[:, 0, :], ps[:, 1, :]] if both else pair(n % 2)
                    gemm_pair(pe, seg_rw + 2 * n, both_rhs if both else main_rhs, outs, rw_uses[n])
                for a in range(NT):
                    pe.wait_ge(shifted, 3 * RT)
                    acquire(pe, use_vt[a])
                    for j in range(RT):
                        mm = pe.transpose(ps[:, use_vt[a][0], j * P:(j + 1) * P], vT[:, j, a * P:(a + 1) * P], kc("ident"))
                    mm.then_inc(bk.full[use_vt[a][0]], 1)
                pe.wait_ge(al_ready, 1)
                for j in range(RT):
                    acquire(pe, use_a[j])
                    pe.matmul(ps[:, use_a[j][0], :], small("a2", LORA)[:, j * P:(j + 1) * P], al_raw, start=True, stop=True)\
                        .then_inc(bk.full[use_a[j][0]], 1)
                pe.wait_ge(gl_ready, 1)
                for j in range(RT):
                    use = use_g[j // 2]
                    if j % 2 == 0:
                        acquire(pe, use)
                    mm = pe.matmul(ps[:, use[0], j % 2 * T:(j % 2 + 1) * T], small("g2")[:, j * P:(j + 1) * P], gl_r, start=True, stop=True)
                    if j % 2:
                        mm.then_inc(bk.full[use[0]], 1)
                for j in range(RT):
                    pe.wait_ge(kk_sq, j + 1)
                    acquire(pe, use_kk[j])
                    pe.matmul(ps[:, use_kk[j][0], :], kc("blk"), sq_r[:, j % 2, :], start=True, stop=True).then_inc(bk.full[use_kk[j][0]], 1)
                for j in range(RT):
                    use = use_bonus[j // 2]
                    if j % 2 == 0:
                        acquire(pe, use)
                    pe.wait_ge(rk_ready, j + 1)
                    mm = pe.matmul(ps[:, use[0], j % 2 * T:(j % 2 + 1) * T], kc("blk"), rk_t[:, j, :], start=True, stop=True)
                    if j % 2:
                        mm.then_inc(bk.full[use[0]], 1)

            def scalar(act, own):
                act.wait_ge(rpad_zero, 1)
                for t in range(R_TILES):
                    n, o = t // 2, t % 2
                    rows = P if t < 14 else LORA
                    pad = rpads[0:rows, t % 2]
                    if t >= 2:
                        act.wait_ge(shifted, t - 1)
                    if t < 14:
                        unit_done(act, seg_rw + 2 * n + 1)
                        src = ps[:, n % 2, o * T:(o + 1) * T] if n < 2 else ps[:, o, :]
                    else:
                        src = al_raw
                    ctx_too = n >= 2 and t != 13
                    ins = act.activation(pad[:, 0, 1:1 + T].rearrange("p (w r) -> p r w", r=ROWS),
                                         src[:, 0:T].rearrange("p (r w) -> p r w", r=ROWS), ACT.Copy)
                    if ctx_too:
                        ins.then_inc(rpad_in, 1)
                        ins = act.activation(pad[:, 1, 1:1 + T], src[:, T:], ACT.Copy)
                    if t < 14 and not (n < 2 and o == 0):
                        emptied(rw_uses[n][o if n >= 2 else 0], ins)
                    else:
                        ins.then_inc(rpad_in, 1)
                act.wait_ge(shifted, 13)
                act.activation(lora_t, lora_t, ACT.Tanh).then_inc(lora_ready, 1)
                act.wait_ge(shifted, 14)
                act.activation(gl_r, gl_r, ACT.Sigmoid).then_inc(gl_ready, 1)
                for a in range(NT):
                    full(act, use_vt[a])
                    emptied(use_vt[a], act.activation(v_tok[:, a, :], ps[:, use_vt[a][0], :], ACT.Copy))
                for j in range(RT):
                    full(act, use_a[j])
                    emptied(use_a[j], act.activation(aT[:, j, :], ps[:, use_a[j][0], :], ACT.Sigmoid, bias=vec("a0", j, j + 1)))
                for i in range(2):
                    full(act, use_g[i])
                    emptied(use_g[i], act.activation(flat(gT[:, 2 * i:2 * i + 2, :]), ps[:, use_g[i][0], :], ACT.Copy))
                for j in range(RT):
                    act.wait_ge(kk_raw, j + 1)
                    if j >= 2:
                        full(act, use_kk[j - 2])
                    act.activation(sq_r[:, j % 2, :].rearrange("p (c t) -> p c t", c=2), kkT(j), ACT.Square).then_inc(kk_sq, 1)
                for j in range(RT):
                    full(act, use_kk[j])
                    if j == 1:
                        act.wait_ge(rk_ready, RT)
                    if j >= 2:
                        act.wait_ge(kk_ready, j - 1)
                    emptied(use_kk[j], act.activation((rt_r, t1_r)[j % 2], ps[:, use_kk[j][0], :], ACT.Sqrt, bias=eps(EPS_KK)))

            def vector(dve, own):
                dve.wait_ge(ssd_ready, ST)
                own.step(dve.memset(rpads.rearrange("p r c t -> p (r c t)"), 0.0))
                own.settle()
                dve.sem_inc(rpad_zero, 1)
                pads_in = 0
                for t in range(R_TILES):
                    n, o = t // 2, t % 2
                    rows = P if t < 14 else LORA
                    ctx_too = n >= 2 and t != 13
                    pads_in += ctx_too
                    if t < 14 and not (n < 2 and o == 0):
                        evacuated(dve, rw_uses[n][o if n >= 2 else 0])
                    else:
                        pads_in += 1
                    if pads_in:
                        dve.wait_ge(rpad_in, pads_in)
                    c = 2 if ctx_too else 1
                    pad = rpads[0:rows, t % 2, 0:c]
                    mid = pad[:, :, 1:1 + T]
                    tmp = t1_r[0:rows, 0:c * T].rearrange("p (c t) -> p c t", c=c)
                    dst = shift_dst(t).rearrange("p (c t) -> p c t", c=c)
                    own.settle()
                    if t:
                        dve.wait_ge(shifted, t)
                    own.step(dve.tensor_tensor(tmp, pad[:, :, 0:T], pad[:, :, 2:2 + T], ALU.add))
                    own.settle()
                    own.step(dve.scalar_tensor_tensor(tmp, tmp, 0.5, mid, ALU.mult, ALU.subtract))
                    own.settle()
                    dve.scalar_tensor_tensor(dst, tmp, vec("mu", t, t + 1)[0:rows], mid, ALU.mult, ALU.add).then_inc(shifted, 1)
                    first_columns(dve, 1 if n < 2 else 3 if n < 6 else 0)
                dve.wait_ge(shifted, R_TILES)
                dve.sem_inc(al_ready, 1)
                for j in range(RT):
                    own.step(dve.tensor_scalar(kkT(j), kT[:, j, :].rearrange("p (c t) -> p c t", c=2), vec("k_k", j, j + 1), None, ALU.mult))
                    own.settle()
                    dve.sem_inc(kk_raw, 1)
                for j in range(RT):
                    evacuated(dve, use_a[j])
                    own.settle()
                    own.step(dve.tensor_scalar(t1_r, aT[:, j, :], 1.0, vec("k_a", j, j + 1), ALU.subtract, ALU.mult))
                    own.settle()
                    own.step(dve.scalar_tensor_tensor(kT[:, j, :], t1_r, 1.0, kT[:, j, :], ALU.add, ALU.mult))
                own.settle()
                for j in range(RT):
                    dve.scalar_tensor_tensor(rk_t[:, j, :], rT[:, j, :], vec("r_k", j, j + 1), kT[:, j, 0:T], ALU.mult, ALU.mult).then_inc(rk_ready, 1)
                for j in range(RT):
                    rt = (rt_r, t1_r)[j % 2]
                    evacuated(dve, use_kk[j])
                    own.step(dve.reciprocal(rt, rt))
                    own.settle()
                    dve.tensor_tensor(kkT(j), kkT(j), rt.rearrange("p (c t) -> p c t", c=2), ALU.mult).then_inc(kk_ready, 1)
                    dve.wait_ge(kk_ready, j + 1)
                    own.step(dve.tensor_tensor(kaT(j), kkT(j), aT[:, j, :].rearrange("p (c t) -> p c t", c=2), ALU.mult))
                for i in range(2):
                    full(dve, use_bonus[i])
                    emptied(use_bonus[i], dve.tensor_tensor(bonusT[:, 2 * i:2 * i + 2, :],
                                                            ps[:, use_bonus[i][0], :].rearrange("p (a t) -> p a t", a=2),
                                                            vT[:, 2 * i:2 * i + 2, 0:T], ALU.mult))
                    evacuated(dve, use_bonus[i])
                dve.sem_inc(prep_ready, 1)

        CH = T // RW_C
        UN = 4 * P

        def d_mem(d):
            if d == 0:
                at = G0
                e = [w(at + n * T, T) for n in range(5)]
                return e, [w(at + 1280 + n * T, TT * P, a=TT) for n in range(2)], w(at + 1792, CH * RW_N, a=CH)
            free = WORK - SMALL_N + SMALLS["a2"][0]
            e = [w(RW0 + n * T, T) for n in range(4)] + [w(free, T)]
            return e, [w(free + T + n * T, TT * P, a=TT) for n in range(2)], w(G0 + 2048, CH * RW_N, a=CH)

        assert G0 + 2304 + 10 * UN <= WORK - SMALL_N + SMALLS["w2"][0]
        MEM = [d_mem(d) for d in range(2)]
        BIG = [[w(G0 + 2304 + (5 * h + n) * UN, UN) for n in range(5)] for h in range(2)]
        ROUNDS = [(j, half) for j in range(RT) for half in (1, 0)]
        rsem = {n: [sem(f"{n}{d}") for d in range(2)] for n in ("dec_sum", "dec_exp", "w_exp", "abkr", "r_ready", "t_init", "q_ready", "s_zero")}
        def dec_mem(n, d):
            return c_row[:, 0, (2 * n + d) * T:(2 * n + d + 1) * T]

        rounds = []
        next_z = [aux() for _ in range(2)]
        for r, (j, half) in enumerate(ROUNDS):
            u = dict(z=next_z, m=[], mt=[])
            for h in range(2):
                u["mt"].append(aux())
                u["m"].append(aux())
            u["bt"] = [aux() for _ in range(2)]
            u["lev"] = []
            for s in LEVELS[1:]:
                x = [aux() for _ in range(2)]
                tx, xt = [], []
                for h in range(2):
                    tx.append(aux() if s != LEVELS[-1] else None)
                    xt.append(aux())
                u["lev"].append((x, tx, xt))
            u["at"] = aux()
            u["nt"] = [[aux() for _ in range(1 if half else 3)] for _ in range(2)]
            next_z = [aux() for _ in range(2)] if r + 1 < len(ROUNDS) else None
            u["nv"] = [aux() for _ in range(2)]
            u["tav"] = [aux() for _ in range(2)]
            u["du"] = [aux() for _ in range(2)]
            u["rh"] = [aux() for _ in range(2)] if not half else None
            u["s"] = [[aux() for _ in range(2)] for _ in range(CH if half else CH - 1)]
            u["y"] = [aux() for _ in range(2)] if not half else None
            rounds.append(u)

        def chunks(d):
            return list(range(CH)) if d == 0 else list(range(CH - 1, -1, -1))

        def blk4(i):
            return slice(i * P, (i + 1) * P)

        def hrows(i):
            return slice(i * RW_N, (i + 1) * RW_N)

        def da(v):
            return v.rearrange("p (d a t) -> p d a t", d=2, a=TT)

        def mask_da(name, swap=False):
            o = CONSTS[name + "0"][0]
            m = K[:, o:o + 2 * P].rearrange("p (d t) -> p d t", d=2)
            if swap:
                m = m[:, ::-1, :]
            return m.unsqueeze(2).to_broadcast([P, 2, TT, P])

        def ident_da():
            return kc("ident").unsqueeze(1).unsqueeze(1).to_broadcast([P, 2, TT, P])

        UNITS = [(d, a) for d in range(2) for a in range(TT)]

        def half_blocks(v, s, second):
            return v.rearrange("p (b i s) -> p b i s", i=2, s=s)[:, :, 1 if second else 0, :]

        def dir_cols(v, d):
            return v[:, d * TT * P:(d + 1) * TT * P]

        class RwScan:
            def tensor(pe, own):
                pe.wait_ge(lora_ready, 1)

                def decays(r):
                    j, half = ROUNDS[r]
                    for d in range(2):
                        use = rounds[r]["z"][d]
                        acquire(pe, use)
                        pe.matmul(ps[:, use[0], 0:T], small("w2")[d * LORA:(d + 1) * LORA, j * P:(j + 1) * P],
                                  lora_t[d * LORA:(d + 1) * LORA, half * T:(half + 1) * T], start=True, stop=True).then_inc(bk.full[use[0]], 1)

                decays(0)
                pe.wait_ge(prep_ready, 1)
                for r, (j, half) in enumerate(ROUNDS):
                    u = rounds[r]

                    def v_of(h, a, rows=slice(0, P)):
                        return v_tok[rows, half * TT + a, j * P + h * RW_N:j * P + (h + 1) * RW_N]

                    def products(use, h, left, right):
                        acquire(pe, use)
                        for i, (d, a) in enumerate(UNITS):
                            mm = pe.matmul(ps[:, use[0], blk4(i)], MEM[d][0][left][hrows(h), blk4(a)], MEM[d][0][right][hrows(h), blk4(a)],
                                           start=True, stop=True)
                        mm.then_inc(bk.full[use[0]], 1)

                    def squares(use, left, right):
                        acquire(pe, use)
                        for i in range(4):
                            mm = pe.matmul(ps[:, use[0], blk4(i)], left[:, blk4(i)], right[:, blk4(i)], start=True, stop=True)
                        mm.then_inc(bk.full[use[0]], 1)

                    def half_squares(use, left, right, s, flip):
                        acquire(pe, use)
                        for i, (d, a) in enumerate(UNITS):
                            mm = pe.matmul(half_blocks(ps[:, use[0], blk4(i)], s, d != flip), left[:, blk4(i)],
                                           half_blocks(right[:, blk4(i)], s, d != flip), start=True, stop=True)
                        mm.then_inc(bk.full[use[0]], 1)

                    for d in range(2):
                        pe.wait_ge(rsem["abkr"][d], r + 1)
                    for h in range(2):
                        products(u["mt"][h], h, 1, 0)
                        products(u["m"][h], h, 0, 1)
                    for d in range(2):
                        A, B, E, Kd, R = MEM[d][0]
                        use = u["bt"][d]
                        acquire(pe, use)
                        for a in range(TT):
                            pe.transpose(ps[:, use[0], blk4(a)], B[:, blk4(a)], kc("ident"))
                            mm = pe.transpose(ps[:, use[0], blk4(2 + a)], Kd[:, blk4(a)], kc("ident"))
                        mm.then_inc(bk.full[use[0]], 1)
                    for n, (x, tx, xt) in enumerate(u["lev"]):
                        for h in range(2):
                            MT, Tm, Tt, X, Q = BIG[h]
                            pe.wait_ge(rsem["q_ready"][h], 5 * r + n + 1)
                            if n == 0:
                                pe.wait_ge(rsem["t_init"][h], 2 * r + 2)
                            else:
                                evacuated(pe, u["lev"][n - 1][1][h])
                                evacuated(pe, u["lev"][n - 1][2][h])
                            squares(x[h], Q, Tm)
                        for h in range(2):
                            MT, Tm, Tt, X, Q = BIG[h]
                            evacuated(pe, x[h])
                            if tx[h] is not None:
                                half_squares(tx[h], Tt, X, LEVELS[n + 1], 0)
                            half_squares(xt[h], X, Tt, LEVELS[n + 1], 1)
                    use = u["at"]
                    acquire(pe, use)
                    for i, (d, a) in enumerate(UNITS):
                        mm = pe.transpose(ps[:, use[0], blk4(i)], MEM[d][0][0][:, blk4(a)], kc("ident"))
                    mm.then_inc(bk.full[use[0]], 1)
                    if not half:
                        for d in range(2):
                            pe.wait_ge(rsem["r_ready"][d], j + 1)
                    for h in range(2):
                        for use, (left, right) in zip(u["nt"][h], ((3, 0), (1, 4), (3, 4))):
                            products(use, h, left, right)
                    if r + 1 < len(ROUNDS):
                        decays(r + 1)
                    for h in range(2):
                        use = u["nv"][h]
                        evacuated(pe, u["nt"][h][0])
                        acquire(pe, use)
                        for i, (d, a) in enumerate(UNITS):
                            mm = pe.matmul(ps[:, use[0], i * RW_N:(i + 1) * RW_N], BIG[h][0][:, blk4(i)], v_of(h, a), start=True, stop=True)
                        mm.then_inc(bk.full[use[0]], 1)
                    evacuated(pe, u["at"])
                    for h in range(2):
                        evacuated(pe, u["nv"][h])
                        evacuated(pe, u["lev"][-1][2][h])
                        squares(u["tav"][h], BIG[h][2], BIG[h][4])
                    for n in range(2):
                        evacuated(pe, u["tav"][n])
                        evacuated(pe, u["bt"][n])
                    for odd in range(2):
                        use = u["du"][odd]
                        acquire(pe, use)
                        rows = hrows(odd)
                        for h in range(2):
                            nta = BIG[h][0]
                            for i, (d, a) in enumerate(UNITS):
                                b_t, k_t = MEM[d][1]
                                to = slice(i * RW_N, (i + 1) * RW_N)
                                pe.matmul(ps[hrows(h), use[0], to], nta[rows, i * P:i * P + RW_N], b_t[rows, a, hrows(h)], start=True, stop=True)
                                to = slice((4 + i) * RW_N, (5 + i) * RW_N)
                                pe.matmul(ps[hrows(h), use[0], to], k_t[rows, a, hrows(h)], v_of(h, a, rows), start=True, stop=False)
                                mm = pe.matmul(ps[hrows(h), use[0], to], b_t[rows, a, hrows(h)], nta[rows, i * P + RW_N:(i + 1) * P],
                                               start=False, stop=True)
                        mm.then_inc(bk.full[use[0]], 1)
                    if not half:
                        for h in range(2):
                            evacuated(pe, u["nt"][h][1])
                        for d in range(2):
                            use = u["rh"][d]
                            acquire(pe, use)
                            for h in range(2):
                                for a in range(TT):
                                    i = TT * d + a
                                    mm = pe.matmul(ps[hrows(h), use[0], blk4(a)], BIG[h][0][:, i * P:i * P + RW_N], BIG[h][1][:, blk4(i)],
                                                   start=True, stop=True)
                            mm.then_inc(bk.full[use[0]], 1)
                    for odd in range(2):
                        evacuated(pe, u["du"][odd])
                    for n in range(len(u["s"])):
                        for d in range(2):
                            st = MEM[d][2]
                            c = chunks(d)[n]
                            i = TT * d + c // 2
                            use = u["s"][n][d]
                            if n:
                                evacuated(pe, u["s"][n - 1][d])
                            elif half:
                                pe.wait_ge(rsem["s_zero"][d], j + 1)
                            else:
                                evacuated(pe, rounds[r - 1]["s"][CH - 1][d])
                            acquire(pe, use)
                            for h in range(2):
                                mm = pe.matmul(ps[hrows(h), use[0], 0:RW_N], BIG[c % 2][4][hrows(h), i * RW_N:(i + 1) * RW_N], st[hrows(h), n, :],
                                               start=True, stop=True)
                            mm.then_inc(bk.full[use[0]], 1)
                    if not half:
                        for d in range(2):
                            evacuated(pe, u["rh"][d])
                            evacuated(pe, u["s"][CH - 2][d])
                        for h in range(2):
                            nta, rb, _, rk, _ = BIG[h]
                            use = u["y"][h]
                            evacuated(pe, u["nt"][h][2])
                            acquire(pe, use)
                            for a in range(TT):
                                to = slice(a * RW_N, (a + 1) * RW_N)
                                for d in range(2):
                                    i = TT * d + a
                                    pe.matmul(ps[:, use[0], to], rk[:, blk4(i)], v_of(h, a), start=d == 0, stop=False)
                                    pe.matmul(ps[:, use[0], to], rb[:, blk4(i)], nta[:, i * P + RW_N:(i + 1) * P], start=False, stop=False)
                                for d in range(2):
                                    for odd in range(2):
                                        c = 2 * a + odd
                                        mm = pe.matmul(ps[hrows(odd), use[0], to], MEM[d][0][1][hrows(h), c * RW_C:(c + 1) * RW_C],
                                                       MEM[d][2][hrows(h), chunks(d).index(c), :], start=False, stop=d == 1)
                            mm.then_inc(bk.full[use[0]], 1)

            def scalar(act, own):
                act.wait_ge(col_done, G_SLOTS + ADA0)

                def decay_gates(r):
                    j = ROUNDS[r][0]
                    for d in range(2):
                        use = rounds[r]["z"][d]
                        if r:
                            act.wait_ge(rsem["abkr"][d], r)
                        full(act, use)
                        emptied(use, act.activation(dec_mem(0, d), ps[:, use[0], 0:T], ACT.Sigmoid, bias=vec("w0", d * RT + j, d * RT + j + 1)))

                def decay_exps(r):
                    for d in range(2):
                        act.wait_ge(rsem["dec_sum"][d], r + 1)
                        act.activation(dec_mem(0, d), dec_mem(0, d), ACT.Exp, scale=-DECAY).then_inc(rsem["dec_exp"][d], 1)
                        act.activation(dec_mem(2, d), dec_mem(1, d), ACT.Exp, scale=DECAY).then_inc(rsem["dec_exp"][d], 1)

                decay_gates(0)
                decay_exps(0)
                act.wait_ge(prep_ready, 1)
                for r, (j, half) in enumerate(ROUNDS):
                    u = rounds[r]
                    if r:
                        last = rounds[r - 1]
                        for n in range(2):
                            full(act, last["du"][n])
                            if last["y"]:
                                full(act, last["y"][n])
                        for d in range(2):
                            evacuated(act, last["s"][-1][d])
                    for d in range(2):
                        act.activation(MEM[d][0][2], dec_mem(1, d), ACT.Exp, scale=-DECAY).then_inc(rsem["w_exp"][d], 1)
                    for h in range(2):
                        full(act, u["mt"][h])
                        emptied(u["mt"][h], act.activation(BIG[h][0], ps[:, u["mt"][h][0], :], ACT.Copy))
                    for d in range(2):
                        b_t, k_t = MEM[d][1]
                        use = u["bt"][d]
                        full(act, use)
                        own.step(act.activation(b_t, ps[:, use[0], 0:2 * P].rearrange("p (a n) -> p a n", a=TT), ACT.Copy))
                        emptied(use, act.activation(k_t, ps[:, use[0], 2 * P:].rearrange("p (a n) -> p a n", a=TT), ACT.Copy))
                    for n, (x, tx, xt) in enumerate(u["lev"]):
                        for h in range(2):
                            full(act, x[h])
                            emptied(x[h], act.activation(BIG[h][3], ps[:, x[h][0], :], ACT.Copy))
                    if r + 1 < len(ROUNDS):
                        decay_gates(r + 1)
                    for h in range(2):
                        use = u["nv"][h]
                        full(act, use)
                        rhs = BIG[h][4].rearrange("p (u n) -> p u n", u=4)
                        emptied(use, act.activation(rhs[:, :, RW_N:], ps[:, use[0], 0:4 * RW_N].rearrange("p (u n) -> p u n", u=4), ACT.Copy))
                    for h in range(2):
                        use = u["tav"][h]
                        full(act, use)
                        emptied(use, act.activation(BIG[h][0], ps[:, use[0], :], ACT.Copy, scale=-1.0))
                    if r + 1 < len(ROUNDS):
                        decay_exps(r + 1)

            def vector(dve, own):
                def decay_sums(r):
                    for d in range(2):
                        gate, total = dec_mem(0, d), dec_mem(1, d)
                        evacuated(dve, rounds[r]["z"][d])
                        if r:
                            dve.wait_ge(rsem["w_exp"][d], r)
                        step = 1 if d == 0 else -1
                        own.step(dve.tensor_tensor_scan(total[:, ::step], kc(f"reset{d}")[:, ::step], gate[:, ::step], 0.0, ALU.mult, ALU.add))
                        own.settle()
                        dve.tensor_tensor(gate, total, gate, ALU.subtract).then_inc(rsem["dec_sum"][d], 1)

                decay_sums(0)
                for r, (j, half) in enumerate(ROUNDS):
                    u = rounds[r]
                    if half:
                        for d in range(2):
                            own.step(dve.memset(MEM[d][2][:, 0, :], 0.0))
                            own.settle()
                            dve.sem_inc(rsem["s_zero"][d], 1)
                    for d in range(2):
                        A, B, E, Kd, R = MEM[d][0]
                        dve.wait_ge(rsem["dec_exp"][d], 2 * r + 2)
                        own.step(dve.tensor_tensor(A, dec_mem(0, d), kkT(j)[:, half, :], ALU.mult))
                        own.step(dve.tensor_tensor(B, dec_mem(2, d), kaT(j)[:, half, :], ALU.mult))
                        own.settle()
                        dve.tensor_tensor(Kd, dec_mem(2, d), kT[:, j, half * T:(half + 1) * T], ALU.mult).then_inc(rsem["abkr"][d], 1)
                    if not half:
                        for d in range(2):
                            dve.wait_ge(rsem["w_exp"][d], r + 1)
                            dve.tensor_tensor(MEM[d][0][4], MEM[d][0][2], rT[:, j, :], ALU.mult).then_inc(rsem["r_ready"][d], 1)
                    for h in range(2):
                        Tm = da(BIG[h][1])
                        use = u["m"][h]
                        full(dve, use)
                        emptied(use, dve.tensor_tensor(Tm, da(ps[:, use[0], :]), mask_da("lev1_", swap=True), ALU.mult))
                        evacuated(dve, use)
                        dve.tensor_tensor(Tm, Tm, ident_da(), ALU.add).then_inc(rsem["t_init"][h], 1)
                    for n, (x, tx, xt) in enumerate(u["lev"]):
                        for h in range(2):
                            full(dve, xt[h])
                            for use, m, flip in ((tx[h], BIG[h][1], 0), (xt[h], BIG[h][2], 1)):
                                if use is not None:
                                    full(dve, use)
                                    for d in range(2):
                                        part = half_blocks(dir_cols(m, d), LEVELS[n + 1], d != flip)
                                        ins = dve.tensor_tensor(part, part, half_blocks(dir_cols(ps[:, use[0], :], d), LEVELS[n + 1], d != flip),
                                                                ALU.subtract)
                                        if d == 0:
                                            own.step(ins)
                                    emptied(use, ins)
                    use = u["at"]
                    full(dve, use)
                    for h in range(2):
                        rhs = BIG[h][4].rearrange("p (u n) -> p u n", u=4)
                        ins = dve.tensor_copy(rhs[:, :, 0:RW_N], ps[:, use[0], :].rearrange("p (u n) -> p u n", u=4)[:, :, hrows(h)])
                        if h == 0:
                            own.step(ins)
                    emptied(use, ins)
                    for h in range(2):
                        for use, m, mask in zip(u["nt"][h], (BIG[h][0], BIG[h][1], BIG[h][3]), ("strict", "incl", "incl")):
                            full(dve, use)
                            emptied(use, dve.tensor_tensor(da(m), da(ps[:, use[0], :]), mask_da(mask), ALU.mult))
                    if r + 1 < len(ROUNDS):
                        decay_sums(r + 1)
                    for odd in range(2):
                        use = u["du"][odd]
                        full(dve, use)
                        dt_m, u_m = (BIG[odd][4][:, n * 4 * RW_N:(n + 1) * 4 * RW_N].rearrange("p (u n) -> p u n", u=4) for n in range(2))
                        src = ps[:, use[0], :].rearrange("p (u n) -> p u n", n=RW_N)
                        own.step(dve.tensor_tensor(dt_m, src[:, 0:4, :], bc(kc("eye64"), 4), ALU.add))
                        for d in range(2):
                            end = odd * RW_C + (RW_C - 1 if d == 0 else 0)
                            ins = dve.tensor_tensor(u_m[:, TT * d:TT * d + TT, :], src[:, 4 + TT * d:4 + TT * d + TT, :],
                                                    heads_bc(MEM[d][0][2][:, end:end + P + 1:P], RW_N), ALU.mult)
                            if d == 0:
                                own.step(ins)
                        emptied(use, ins)
                    if not half:
                        for d in range(2):
                            use = u["rh"][d]
                            full(dve, use)
                            emptied(use, dve.tensor_tensor(MEM[d][0][1], ps[:, use[0], 0:T], MEM[d][0][4], ALU.add))
                    for odd in range(2):
                        evacuated(dve, u["du"][odd])
                    for n in range(len(u["s"])):
                        for d in range(2):
                            c = chunks(d)[n]
                            use = u["s"][n][d]
                            E, st = MEM[d][0][2], MEM[d][2]
                            at = c * RW_C + (RW_C - 1 if d == 0 else 0)
                            i = 4 + TT * d + c // 2
                            full(dve, use)
                            emptied(use, dve.scalar_tensor_tensor(st[:, (n + 1) % CH, :], ps[:, use[0], 0:RW_N], E[:, at:at + 1],
                                                                  BIG[c % 2][4][:, i * RW_N:(i + 1) * RW_N], ALU.mult, ALU.add))
                    if not half:
                        for h in range(2):
                            use = u["y"][h]
                            full(dve, use)
                            emptied(use, dve.tensor_copy(y_tok[:, :, j * P + h * RW_N:j * P + (h + 1) * RW_N],
                                                         ps[:, use[0], 0:P].rearrange("p (a n) -> p a n", a=TT)))

            def gpsimd(pool, own):
                pool.wait_ge(consts_in, 16)
                for r, (j, half) in enumerate(ROUNDS):
                    u = rounds[r]
                    if r:
                        for d in range(2):
                            evacuated(pool, rounds[r - 1]["s"][-1][d])
                    for h in range(2):
                        MT, _, Tt, _, Q = (da(v) for v in BIG[h])
                        evacuated(pool, u["mt"][h])
                        own.step(pool.tensor_tensor(Tt, MT, mask_da("lev1_"), ALU.mult))
                        pool.tensor_tensor(Q, MT, mask_da("lev2_"), ALU.mult).then_inc(rsem["q_ready"][h], 1)
                        own.settle()
                        pool.tensor_tensor(Tt, Tt, ident_da(), ALU.add).then_inc(rsem["t_init"][h], 1)
                    for n, s in enumerate(LEVELS[2:]):
                        for h in range(2):
                            full(pool, u["lev"][n][0][h])
                            pool.tensor_tensor(da(BIG[h][4]), da(BIG[h][0]), mask_da(f"lev{s}_"), ALU.mult).then_inc(rsem["q_ready"][h], 1)

        use_gt = [aux() for _ in range(2 * TT)]
        gn = w(G0, 4 * TT * RW_H).rearrange("p (i a h) -> p i a h", i=4, a=TT)
        gsq = w(G0 + 64, TT * RW_DIM, a=TT)
        yT = w(G0 + 64 + TT * RW_DIM, RT * T, a=RT)
        gn_sq, gn_rt, gn_y, yt_aff, rw_ready = (sem(n) for n in ("gn_sq", "gn_rt", "gn_y", "yt_aff", "rw_ready"))

        class RwOut:
            def tensor(pe, own):
                pe.wait_ge(gn_y, 1)
                for n in range(2 * TT):
                    a, q = n // 2, n % 2
                    use = use_gt[n]
                    acquire(pe, use)
                    for i in range(2):
                        mm = pe.transpose(ps[:, use[0], blk4(i)], y_tok[:, a, blk4(2 * q + i)], kc("ident"))
                    mm.then_inc(bk.full[use[0]], 1)

            def vector(dve, own):
                for h in range(2):
                    for u in rounds:
                        if u["y"]:
                            evacuated(dve, u["y"][h])
                y3 = y_tok.rearrange("p a (h n) -> p (a h) n", n=RW_N)
                sq3 = gsq.rearrange("p a (h n) -> p (a h) n", n=RW_N)
                s, m, v, rt = (gn[:, i].rearrange("p a h -> p (a h)") for i in range(4))
                own.step(dve.tensor_reduce(s, y3, AX.X, ALU.add))
                own.settle()
                own.step(dve.tensor_scalar(m, s, 1.0 / RW_N, None, ALU.mult))
                own.settle()
                own.step(dve.tensor_tensor(y3, y3, heads_bc(m, RW_N), ALU.subtract))
                own.settle()
                own.step(dve.tensor_tensor(sq3, y3, y3, ALU.mult))
                own.settle()
                dve.tensor_reduce(v, sq3, AX.X, ALU.add).then_inc(gn_sq, 1)
                dve.wait_ge(gn_rt, 1)
                own.step(dve.reciprocal(rt, rt))
                own.settle()
                dve.tensor_tensor(y3, y3, heads_bc(rt, RW_N), ALU.mult).then_inc(gn_y, 1)
                for j in range(RT):
                    dve.wait_ge(yt_aff, j + 1)
                    own.step(dve.tensor_tensor(yT[:, j, :], yT[:, j, :], bonusT[:, j, :], ALU.add))
                    own.settle()
                    dve.tensor_tensor(rwT[:, j, :].rearrange("p (r w) -> p w r", r=ROWS), yT[:, j, :].rearrange("p (w r) -> p w r", r=ROWS),
                                      gT[:, j, :].rearrange("p (w r) -> p w r", r=ROWS), ALU.mult).then_inc(rw_ready, 1)

            def scalar(act, own):
                v, rt = (gn[:, i].rearrange("p a h -> p (a h)") for i in (2, 3))
                act.wait_ge(gn_sq, 1)
                act.activation(rt, v, ACT.Sqrt, bias=eps(EPS_GN), scale=1.0 / RW_N).then_inc(gn_rt, 1)
                for n in range(2 * TT):
                    a, q = n // 2, n % 2
                    full(act, use_gt[n])
                    emptied(use_gt[n], act.activation(yT[:, 2 * q:2 * q + 2, blk4(a)],
                                                      ps[:, use_gt[n][0], 0:2 * P].rearrange("p (i t) -> p i t", i=2), ACT.Copy))
                for n in range(2 * TT):
                    evacuated(act, use_gt[n])
                for j in range(RT):
                    act.activation(yT[:, j, :], yT[:, j, :], ACT.Identity, bias=vec("rln_b", j, j + 1), scale=vec("rln_g", j, j + 1))\
                        .then_inc(yt_aff, 1)

        PAIRS2 = KT // 2
        seg_merge = segment(8 * PAIRS2)
        bo_buf = [w(W0 + n * BO_K * 2 * P, BO_K * 2 * P, k=BO_K) for n in range(2)]
        gates = [w(W0 + 2 * BO_K * 2 * P + n * 8 * T, 8 * T, b=4) for n in range(2)]
        use_gate = [bk.take(b, 2 * PAIRS2) for b in range(2)]
        use_bo = [bk.take(3 + b, PAIRS2) for b in range(4)]
        bo_ready = [sem(f"bo_ready{n}") for n in range(2)]
        merged = sem("merged")
        BRANCHES = ((convT, CT), (ssdT, ST), (fftT, FT), (rwT, RT))

        class Merge:
            def sync(sp):
                def a_pair(jj, it, first):
                    for b in range(4):
                        for o in range(2):
                            n = 2 * (4 * jj + b) + o
                            u = seg_merge + n
                            sp.wait_ge(w_used, it * 16 + (u - SLOTS + 1))
                            sp.dma_start(slot(u), gate_u[it * 16 + n]).then_inc(w_ready[u % SLOTS], 16)
                        if b == 1:
                            if first:
                                sp.wait_ge(rw_ready, RT)
                                if jj == 0:
                                    sp.dma_start(xT[:, :, :], x_t).then_inc(x_in, 16)
                            else:
                                sp.wait_ge(bk.full[6], it * 2 + (use_bo[3][1] + jj - 1))
                            sp.dma_start(bo_buf[jj].rearrange("p k n -> p (k n)"), bo_u[it * 2 + jj]).then_inc(bo_ready[jj], 16)
                a_pair(0, 0, True)
                a_pair(1, 0, True)
                with sp.Fori(1, PAIRS2 // 2) as it:
                    for jj in range(2):
                        a_pair(jj, it, False)

            def tensor(pe, own):
                with pe.Fori(0, PAIRS2 // 2) as it:
                    for jj in range(2):
                        for b in range(4):
                            n = 4 * jj + b
                            gemm_pair(pe, seg_merge + 2 * n, main_rhs, pair(n % 2), [(n % 2, use_gate[n % 2][1] + n // 2)], it=it, k=4, step=16)
                        if jj == 0:
                            pe.wait_ge(conv_ready, CT)
                            evacuated(pe, use_f2[1])
                            pe.wait_ge(ssd_ready, ST)
                            pe.wait_ge(rw_ready, RT)
                        pe.wait_ge(bo_ready[jj], it * 16 + 16)
                        at = 0
                        for b, (src, kts) in enumerate(BRANCHES):
                            acquire(pe, (3 + b, use_bo[b][1] + jj), it, 2)
                            for o in range(2):
                                for kt in range(kts):
                                    mm = pe.matmul(ps[:, 3 + b, o * T:(o + 1) * T], bo_buf[jj][:, at + kt, o * P:(o + 1) * P], src[:, kt, :],
                                                   start=kt == 0, stop=kt == kts - 1)
                            mm.then_inc(bk.full[3 + b], 1)
                            at += kts

            def scalar(act, own):
                act.wait_ge(rw_ready, RT)
                with act.Fori(0, PAIRS2 // 2) as it:
                    for jj in range(2):
                        act.wait_ge(merged, it * 2 + (jj + 1))
                        for b in range(4):
                            n = 4 * jj + b
                            unit_done(act, seg_merge + 2 * n + 1, it, 16)
                            act.activation(gates[jj][:, b, :], ps[:, n % 2, :], ACT.Sigmoid).then_inc(bk.free[n % 2], 1)

            def gpsimd(pool, own):
                fetch_rows(pool, ada_r, ADA0, 96)

            def vector(dve, own):
                dve.sem_inc(merged, 2)
                with dve.Fori(0, PAIRS2 // 2) as it:
                    for jj in range(2):
                        for n in range(12):
                            column(dve, adaT, vec("ada_b"), 1, ADA0 + 12 * jj + n, 12 * jj + n, it, 24)
                        for b in range(2):
                            dve.wait_ge(bk.free[b], it * 4 + (use_gate[b][1] + 2 * jj + 2))
                        for b in range(4):
                            dve.wait_ge(bk.full[3 + b], it * 2 + (use_bo[b][1] + jj + 1))
                            g = gates[jj][:, b, :]
                            dve.tensor_tensor(g, g, ps[:, 3 + b, :], ALU.mult).then_inc(bk.free[3 + b], 1)
                        for b in range(4):
                            dve.wait_ge(bk.free[3 + b], it * 2 + (use_bo[b][1] + jj + 1))
                        g = gates[jj].rearrange("p b (o t) -> p b o t", o=2)
                        dve.tensor_tensor(g[:, 0], g[:, 0], g[:, 1], ALU.add).then_inc(merge_sum, 1)
                        dve.wait_ge(merge_sum, it * 4 + (2 * jj + 1))
                        dve.tensor_tensor(g[:, 0], g[:, 0], g[:, 2], ALU.add).then_inc(merge_sum, 1)
                        dve.wait_ge(merge_sum, it * 4 + (2 * jj + 2))
                        dve.tensor_tensor(m_pairs[:, it * 2 + jj], g[:, 0], g[:, 3], ALU.add).then_inc(merged, 1)
                dve.wait_ge(col_done, G_SLOTS + ADA0 + 96)
                own.step(dve.tensor_tensor(gn1, modx[:, 0:KT], vec("norm_g", KT, 2 * KT), ALU.mult))
                own.step(dve.scalar_tensor_tensor(gsc2, modx[:, 2 * KT:3 * KT], 1.0, vec("norm_g", 2 * KT, 3 * KT), ALU.add, ALU.mult))
                own.step(dve.tensor_tensor(gn3, modx[:, 3 * KT:4 * KT], vec("norm_g", 3 * KT, 4 * KT), ALU.mult))
                own.settle()
        m_pairs = hT[:, :, T:].rearrange("p (j o) t -> p j o t", o=2)
        merge_sum = sem("merge_sum")
        gn1, gsc2, gn3 = coef[:, 2 * KT:3 * KT], coef[:, 3 * KT:4 * KT], coef[:, 4 * KT:5 * KT]

        rtn = w(WORK - T, T)
        nsq, nrs, nadd, hsc, hrd = (sem(n) for n in ("norm_squares", "norm_root", "x_added", "h2_scaled", "h2_ready"))
        norms = [0]

        NPAIR = KT // 2

        class Rms:

            def __init__(self, src, ready, squares=None):
                self.src, self.ready = src, ready
                self.squares = hT[:, :, 0:T] if squares is None else squares
                norms[0] += 1
                self.k = norms[0]
                self.use = aux()

            def tensor(self, pe):
                acquire(pe, self.use)
                for kt in range(KT):
                    if kt % 2 == 0:
                        pe.wait_ge(nsq, NPAIR * (self.k - 1) + kt // 2 + 1)
                    mm = pe.matmul(ps[:, self.use[0], 0:T], kc("ones"), self.squares[:, kt, :], start=kt == 0, stop=kt == KT - 1)
                mm.then_inc(bk.full[self.use[0]], 1)

            def scalar(self, act, squared=False):
                if not squared:
                    for n in range(NPAIR):
                        self.ready(act, n)
                        both = slice(2 * n, 2 * n + 2)
                        act.activation(self.squares[:, both, :], self.src[:, both, :], ACT.Square).then_inc(nsq, 1)
                full(act, self.use)
                emptied(self.use, act.activation(rtn, ps[:, self.use[0], 0:T], ACT.Sqrt, bias=eps(EPS_RMS), scale=1.0 / D))

            def vector(self, dve):
                evacuated(dve, self.use)
                dve.reciprocal(rtn, rtn).then_inc(nrs, 1)
                dve.wait_ge(nrs, self.k)

        def add_scaled(dve, own, src, col):
            for kt in range(KT + 1):
                if kt < KT:
                    own.step(dve.tensor_tensor(src[:, kt, :], src[:, kt, :], rtn, ALU.mult))
                if kt:
                    own.settle(1 if kt < KT else 0)
                    t = kt - 1
                    dve.scalar_tensor_tensor(xT[:, t, :], src[:, t, :], col[:, t:t + 1], xT[:, t, :], ALU.mult, ALU.add).then_inc(nadd, 1)

        def scale_split(dve, k, col, shift):
            lag = 2
            for n in range(KT + lag):
                if n < KT:
                    dve.scalar_tensor_tensor(hT[:, n, 0:T], xT[:, n, :], col[:, n:n + 1], rtn, ALU.mult, ALU.mult).then_inc(hsc, 1)
                if n >= lag:
                    t = n - lag
                    dve.wait_ge(hrd, k * KT + t + 1)
                    dve.scalar_tensor_tensor(h_low[:, t, :], hT[:, t, 0:T], shift[:, t:t + 1], h_high[:, t, :].bitcast(F32), ALU.add, ALU.subtract)\
                        .then_inc(x_split, 1)

        def shift_round(act, k, shift):
            for kt in range(KT):
                act.wait_ge(hsc, k * KT + kt + 1)
                act.activation(h_high[:, kt, :], hT[:, kt, 0:T], ACT.Identity, bias=shift[:, kt:kt + 1]).then_inc(hrd, 1)

        SPLIT0 = units[0]
        hi_done, w_split, x_split = sem("hi_done"), sem("w_split"), sem("x_split")

        def split_unit(dve, u, off=0, size=UNIT):
            raw, low, high = slot(u)[:, 0:size], ring_parts[:, u % SLOTS, 0:size], w_high[:, u % 2, 0:size]
            dve.wait_ge(w_ready[u % SLOTS], 16 * (u // SLOTS + 1) + off * (16 // SLOTS))
            dve.wait_ge(w_used, off + (u - 1))
            dve.tensor_copy(high, raw).then_inc(hi_done, 1)
            dve.wait_ge(hi_done, off + (u - SPLIT0 + 1))
            dve.tensor_tensor(low, raw, high.bitcast(F32), ALU.subtract).then_inc(w_split, 1)

        def split_units(dve, u, n):
            with dve.Fori(0, n // 4) as it:
                for j in range(4):
                    split_unit(dve, u + j, it * 4)
            for j in range(n // 4 * 4, n):
                split_unit(dve, u + j)

        def split_x(dve, own, x, high, low, unit=None):
            for n in range(0, KT, 4):
                own.step(dve.tensor_copy(high[:, n:n + 4, :], x[:, n:n + 4, :]))
                own.settle()
                dve.tensor_tensor(low[:, n:n + 4, :], x[:, n:n + 4, :], high[:, n:n + 4, :].bitcast(F32), ALU.subtract).then_inc(x_split, 4)
                if n == 0 and unit is not None:
                    split_unit(dve, unit)

        def halves(high, low):
            return lambda kt: (high[:, kt, :], low[:, kt, :])

        def split_pair(pe, u, rhs, outs, uses, off=0, it=None, k=0, kts=KT, split=None, ready=None):
            for o in range(2):
                pe.wait_ge(w_split, off + (u + o - SPLIT0 + 1))
                if o < len(uses):
                    acquire(pe, uses[o], it, k)
                for kt in range(kts):
                    if split is not None and o == 0 and kt % 4 == 0:
                        pe.wait_ge(x_split, split + kt + 4)
                    if ready is not None and o == 0:
                        ready(kt)
                    x_high, x_low = rhs(kt)
                    columns = slice(kt * P, (kt + 1) * P)
                    high, low = w_high[:, (u + o) % 2, columns], ring_parts[:, (u + o) % SLOTS, columns]
                    pe.matmul(outs[o], high, x_high, start=kt == 0, stop=False)
                    pe.matmul(outs[o], high, x_low, start=False, stop=False)
                    mm = pe.matmul(outs[o], low, x_high, start=False, stop=kt == kts - 1)
                mm.then_inc(w_used, 1)

        h_low, h_high = hT_parts[:, :, 0:T], hT_parts[:, :, T:]

        def to_width(pe, seg, use, rhs, split):
            with pe.Fori(0, PAIRS2 // 2) as it:
                for j in range(2):
                    split_pair(pe, seg + 2 * j, rhs, pair(j), [(j, use[j][1])], it * 4, it, 1, split=split if j == 0 else None)

        def from_width(act, seg, use, dst, squares=None):
            with act.Fori(0, PAIRS2 // 2) as it:
                for j in range(2):
                    unit_done(act, seg + 2 * j + 1, it, 4)
                    if squares is not None:
                        act.activation(squares[:, it * 2 + j], ps[:, j, :].rearrange("p (o t) -> p o t", o=2), ACT.Square).then_inc(nsq, 1)
                    act.activation(dst[:, it * 2 + j], ps[:, j, :].rearrange("p (o t) -> p o t", o=2), ACT.Copy).then_inc(bk.free[j], 1)

        def width_done(eng, use):
            for b in range(2):
                eng.wait_ge(bk.free[b], use[b][1] + PAIRS2 // 2)

        seg_wo = segment(2 * PAIRS2)
        use_wo = [bk.take(b, PAIRS2 // 2) for b in range(2)]
        yT1 = w(W0, KT * T, a=KT)
        y1_pairs = yT1.rearrange("p (j o) t -> p j o t", o=2)
        sq1 = w(W0 + KT * T, KT * T, a=KT)
        rms_y1 = Rms(yT1, None, sq1)
        rms_x1 = Rms(xT[:, :, :], lambda e, n: e.wait_ge(nadd, 2 * n + 2))
        smallw2 = w(WORK - T - SMALL2_N, SMALL2_N)
        smalls2_in = sem("smalls2_in")

        class Mix:
            def sync(sp):
                fetch(sp, wo_u, seg_wo, 2 * PAIRS2)
                sp.wait_ge(merged, 2 + PAIRS2)
                sp.dma_start(smallw2, smalls2).then_inc(smalls2_in, 16)

            def tensor(pe, own):
                to_width(pe, seg_wo, use_wo, halves(h_low, h_high), 0)
                rms_y1.tensor(pe)
                rms_x1.tensor(pe)

            def scalar(act, own):
                from_width(act, seg_wo, use_wo, y1_pairs, sq1.rearrange("p (j o) t -> p j o t", o=2))
                rms_y1.scalar(act, squared=True)
                rms_x1.scalar(act)
                shift_round(act, 0, modx[:, KT:2 * KT])

            def vector(dve, own):
                dve.wait_ge(merged, 2 + PAIRS2)
                split_x(dve, own, hT[:, :, T:], h_low, h_high, seg_wo)
                split_units(dve, seg_wo + 1, 2 * PAIRS2 + 1)
                rms_y1.vector(dve)
                dve.wait_ge(x_in, 48)
                add_scaled(dve, own, yT1, gn1)
                rms_x1.vector(dve)
                scale_split(dve, 0, gsc2, modx[:, KT:2 * KT])

        QUARTERS = KF // KT
        seg_mlp = segment(QUARTERS * 4 * PAIRS2)
        use_mlp = [bk.take(b, QUARTERS * PAIRS2) for b in range(2)]
        act_high, act_low = (work_parts[:, n * KT * T:(n + 1) * KT * T].rearrange("p (a t) -> p a t", a=KT) for n in range(2))
        yT2 = w(2 * KT * T, KT * T, a=KT)
        rl = w(3 * KT * T, 4 * T).rearrange("p (r o t) -> p r o t", r=2, o=2)
        sqr_done, act_split, act_hi = sem("sqr_done"), sem("act_split"), sem("act_hi")
        rms_y2 = Rms(yT2, lambda e, n: e.wait_ge(bk.free[n % 2], use_mlp[n % 2][1] + QUARTERS * PAIRS2 - PAIRS2 // 2 + n // 2 + 1))

        class Mlp:
            def sync(sp):
                fetch(sp, mlp_u, seg_mlp, QUARTERS * 4 * PAIRS2)

            def tensor(pe, own):
                with pe.Fori(0, QUARTERS) as q:
                    for n in range(2 * PAIRS2):
                        rhs = halves(h_high, h_low) if n < PAIRS2 else halves(act_high, act_low)

                        def hidden_ready(kt):
                            if n == PAIRS2 and kt in (0, KT - 2):
                                pe.wait_ge(act_split, q * PAIRS2 + (2 + PAIRS2 - (kt == 0)))

                        split_pair(pe, seg_mlp + 2 * n, rhs, pair(n % 2), [(n % 2, use_mlp[n % 2][1] + n // 2)], q * (4 * PAIRS2), q, PAIRS2,
                                   split=KT if n == 0 else None, ready=hidden_ready)
                rms_y2.tensor(pe)

            def scalar(act, own):
                act.wait_ge(nadd, KT)
                with act.Fori(0, QUARTERS) as q:
                    for n in range(PAIRS2):
                        act.wait_ge(act_split, q * PAIRS2 + (n + 1))
                        unit_done(act, seg_mlp + 2 * n + 1, q, 4 * PAIRS2)
                        b, k = n % 2, n // 2
                        act.activation(rl[:, b], ps[:, b, :].rearrange("p (o t) -> p o t", o=2), ACT.Relu).then_inc(bk.free[b], 1)
                        act.wait_ge(bk.free[b], q * PAIRS2 + (use_mlp[b][1] + k + 1))
                        act.activation(rl[:, b], rl[:, b], ACT.Square).then_inc(sqr_done, 1)
                rms_y2.scalar(act)

            def vector(dve, own):
                dve.wait_ge(nadd, KT)
                own.step(dve.memset(flat(yT2), 0.0))
                own.settle()
                dve.sem_inc(act_split, 2)
                with dve.Fori(0, QUARTERS) as q:
                    for n in range(2 * PAIRS2):
                        split_unit(dve, seg_mlp + 2 * n + 2, q * (4 * PAIRS2))
                        if n != PAIRS2 - 1:
                            split_unit(dve, seg_mlp + 2 * n + 3, q * (4 * PAIRS2))
                        b, k, j = n % 2, n // 2, n % PAIRS2
                        if n < PAIRS2:
                            dve.wait_ge(sqr_done, q * PAIRS2 + (n + 1))
                            high, low = act_high[:, 2 * j:2 * j + 2, :], act_low[:, 2 * j:2 * j + 2, :]
                            dve.wait_ge(w_used, q * (4 * PAIRS2) + seg_mlp)
                            dve.tensor_copy(high, rl[:, b]).then_inc(act_hi, 1)
                            dve.wait_ge(act_hi, q * PAIRS2 + (n + 1))
                            dve.tensor_tensor(low, rl[:, b], high.bitcast(F32), ALU.subtract).then_inc(act_split, 1)
                            if n == PAIRS2 - 1:
                                split_unit(dve, seg_mlp + 2 * n + 3, q * (4 * PAIRS2))
                        else:
                            y = yT2[:, 2 * j:2 * j + 2, :]
                            unit_done(dve, seg_mlp + 2 * n + 1, q, 4 * PAIRS2)
                            dve.wait_ge(bk.free[b], q * PAIRS2 + (use_mlp[b][1] + k))
                            dve.tensor_tensor(y, y, ps[:, b, :].rearrange("p (o t) -> p o t", o=2), ALU.add).then_inc(bk.free[b], 1)
                rms_y2.vector(dve)
                add_scaled(dve, own, yT2, gn3)

        gmix, gffn = coef[:, 0:KT], coef[:, KT:2 * KT]
        seg_in2 = segment(36)
        use_in2 = [bk.take(b, 9) for b in range(2)]
        u2_pairs = w(0, 36 * T, j=18)
        u2 = w(0, 36 * T, a=36)
        zp, zq, zk, zv, zx, zy = (u2[:, a:b, :] for a, b in ((0, 4), (4, 12), (12, 20), (20, 28), (28, 32), (32, 36)))
        use_f = aux()
        rms_x2 = Rms(xT[:, :, :], lambda e, n: e.wait_ge(nadd, KT + 2 * n + 2))

        def small2(name):
            o, n = SMALLS2[name]
            return smallw2[:, o:o + n]

        class In2:
            def sync(sp):
                fetch(sp, in2_u, seg_in2, 36)

            def tensor(pe, own):
                rms_x2.tensor(pe)
                with pe.Fori(0, 9) as it:
                    for j in range(2):
                        split_pair(pe, seg_in2 + 2 * j, halves(h_high, h_low), pair(j), [(j, use_in2[j][1])], it * 4, it, 1, split=2 * KT if j == 0 else None)
                pe.wait_ge(smalls2_in, 16)
                acquire(pe, use_f)
                wf = small2("wf").rearrange("p (k n) -> p k n", k=KT)
                for a in range(TT):
                    for n in range(2 * KT):
                        part = hT_parts[:, n // 2, n % 2 * T + a * P:n % 2 * T + (a + 1) * P].bitcast(F32)
                        mm = pe.matmul(ps[:, use_f[0], a * AH:(a + 1) * AH], part, wf[:, n // 2, :], start=n == 0, stop=n == 2 * KT - 1)
                mm.then_inc(bk.full[use_f[0]], 1)

            def scalar(act, own):
                rms_x2.scalar(act)
                shift_round(act, 1, adaT[:, 0:KT])
                with act.Fori(0, 9) as it:
                    for j in range(2):
                        unit_done(act, seg_in2 + 2 * j + 1, it, 4)
                        act.activation(u2_pairs[:, it * 2 + j], ps[:, j, :], ACT.Copy).then_inc(bk.free[j], 1)

            def vector(dve, own):
                own.step(dve.scalar_tensor_tensor(gmix, adaT[:, KT:2 * KT], 1.0, vec("g_mix"), ALU.add, ALU.mult))
                own.step(dve.scalar_tensor_tensor(gffn, adaT[:, 4 * KT:5 * KT], 1.0, vec("g_ffn"), ALU.add, ALU.mult))
                own.settle()
                rms_x2.vector(dve)
                scale_split(dve, 1, gmix, adaT[:, 0:KT])
                split_units(dve, seg_in2 + 2, 36)

        mixT = hT[:, :, T:]
        B0 = 36 * T
        PW = T + 16
        pool_in = w(B0, 2 * 4 * PW).rearrange("p (i a t) -> p i a t", i=2, a=4)
        pool_d = w(B0 + 8 * PW, 4 * T, a=4)
        L0 = B0 + 8 * PW + 4 * T
        LW = T + LRU_TAPS - 1
        lru_pad = w(L0, 4 * LW, a=4)
        xc = w(L0 + 4 * LW, 4 * T, a=4)
        A0 = L0 + 4 * LW + 4 * T
        gr, gi = zx, w(A0, 4 * T, a=4)
        vt2 = hT[:, :, 0:T]
        F0 = A0 + 4 * T
        fz = [w(F0 + n * TT * AH, TT * AH, a=TT) for n in range(4)]
        sp_l = [w(F0 + 64 + n * 4, 4) for n in range(4)]
        mx = w(F0 + 80, 2 * 8).rearrange("p (i n) -> p i n", i=2)
        F1 = F0 + 96
        assert F1 <= WORK - T - SMALL2_N
        prob = w(B0, 2 * TT * T).rearrange("p (r a s) -> p r a s", r=2, a=TT)
        probT = w(B0 + 2 * TT * T, 2 * TT * T).rearrange("p (r s t) -> p r s t", r=2, s=TT)
        use_pool = [aux() for _ in range(2)]
        use_lr = [aux() for _ in range(4)]
        use_v2 = [aux() for _ in range(4)]
        ATT = []
        for h in range(AH):
            ATT.append(dict(l=aux(), t=aux(), o=aux()))
        (pool_ready, xc_ready, lf_abs, lf_e, lf_u, lf_ln, lf_ready, lam_e, lam_ln, pmax, pexp, pnorm, lru_tanh, lru_sq, lru_a, gelu_in, gelu_t,
         lru_h, lru_done) = (sem(n) for n in (
             "pool_ready", "xc_ready", "lf_abs", "lf_e", "lf_u", "lf_ln", "lf_ready", "lam_e", "lam_ln", "pmax", "pexp", "pnorm",
             "lru_tanh", "lru_sq", "lru_a", "gelu_in", "gelu_t", "lru_h", "lru_done"))
        SCALE = float(P) ** -0.5

        def v_head(a, h):
            return vt2[:, 4 * a + h // 2, h % 2 * P:(h % 2 + 1) * P]

        GELU_C = float(np.sqrt(2.0 / np.pi))

        class Mix2:
            def tensor(pe, own):
                wp, wa, wi = (small2(n).rearrange("p (b n) -> p b n", b=4) for n in ("pool_w", "lru_wa", "lru_wi"))
                pe.wait_ge(pool_ready, 4)
                for g in range(4):
                    use = use_pool[g // 2]
                    if g % 2 == 0:
                        acquire(pe, use)
                    mm = pe.matmul(ps[:, use[0], g % 2 * T:(g % 2 + 1) * T], wp[:, g, :], pool_d[:, g, :], start=True, stop=True)
                    if g % 2:
                        mm.then_inc(bk.full[use[0]], 1)
                for i in range(4):
                    use = use_lr[i]
                    wm = (wa, wi)[i // 2]
                    acquire(pe, use)
                    for o in range(2):
                        b = i % 2 * 2 + o
                        pe.wait_ge(xc_ready, b + 1)
                        mm = pe.matmul(ps[:, use[0], o * T:(o + 1) * T], wm[:, b, :], xc[:, b, :], start=True, stop=True)
                    mm.then_inc(bk.full[use[0]], 1)
                for n in range(4):
                    a, q = n // 2, n % 2
                    use = use_v2[n]
                    acquire(pe, use)
                    for i in range(4):
                        mm = pe.transpose(ps[:, use[0], blk4(i)], zv[:, 4 * q + i, a * P:(a + 1) * P], kc("ident"))
                    mm.then_inc(bk.full[use[0]], 1)
                pe.wait_ge(lf_ready, 1)
                lf = fz[3]

                def logits(h):
                    use = ATT[h]["l"]
                    acquire(pe, use)
                    for a in range(TT):
                        s1 = (a + 1) * P
                        out = ps[:, use[0], a * T:a * T + s1]
                        pe.matmul(out, zq[:, h, a * P:(a + 1) * P], zk[:, h, 0:s1], start=True, stop=False)
                        for s in range(a + 1):
                            o = ps[:, use[0], a * T + s * P:a * T + (s + 1) * P]
                            for i in range(s + 1):
                                pe.matmul(o, lf[:, i, h:h + 1].to_broadcast([P, P]), kc("upto") if i == s else kc("ones"), start=False, stop=False)
                        mm = pe.matmul(ps[:, use[0], a * T + a * P:a * T + s1], kc("ident"), kc("neg_b"), start=False, stop=True)
                    mm.then_inc(bk.full[use[0]], 1)

                def turn(h):
                    use = ATT[h]["t"]
                    pe.wait_ge(pnorm, h + 1)
                    acquire(pe, use)
                    for s in range(TT):
                        for a in range(s, TT):
                            mm = pe.transpose(ps[:, use[0], s * T + a * P:s * T + (a + 1) * P], prob[:, h % 2, a, s * P:(s + 1) * P], kc("ident"))
                    mm.then_inc(bk.full[use[0]], 1)

                def weigh(h):
                    evacuated(pe, ATT[h]["t"])
                    for n in range(4):
                        evacuated(pe, use_v2[n])
                    use = ATT[h]["o"]
                    acquire(pe, use)
                    pe.matmul(ps[:, use[0], 0:T], v_head(0, h), probT[:, h % 2, 0, :], start=True, stop=False)
                    pe.matmul(ps[:, use[0], P:T], v_head(1, h), probT[:, h % 2, 1, P:], start=False, stop=True).then_inc(bk.full[use[0]], 1)

                logits(0)
                for h in range(AH):
                    if h + 1 < AH:
                        logits(h + 1)
                    turn(h)
                    weigh(h)

            def scalar(act, own):
                act.wait_ge(lf_abs, 1)
                act.activation(fz[1], fz[1], ACT.Exp, scale=-1.0).then_inc(lf_e, 1)
                act.activation(sp_l[1], sp_l[1], ACT.Exp, scale=-1.0).then_inc(lam_e, 1)
                act.wait_ge(lf_u, 1)
                act.activation(fz[3], fz[2], ACT.Ln).then_inc(lf_ln, 1)
                act.activation(sp_l[3], sp_l[2], ACT.Ln).then_inc(lam_ln, 1)
                for i in range(2):
                    use = use_pool[i]
                    full(act, use)
                    for o in range(2):
                        ins = act.activation(mixT[:, 2 * i + o, :], ps[:, use[0], o * T:(o + 1) * T], ACT.Copy, scale=vec("pool_scale", 2 * i + o, 2 * i + o + 1))
                        if o == 0:
                            own.step(ins)
                    emptied(use, ins)
                act.wait_ge(xc_ready, 4)
                for i in range(4):
                    use = use_lr[i]
                    full(act, use)
                    for o in range(2):
                        b = i % 2 * 2 + o
                        dst, bias = ((gr, "lru_ba"), (gi, "lru_bi"))[i // 2]
                        ins = act.activation(dst[:, b, :], ps[:, use[0], o * T:(o + 1) * T], ACT.Sigmoid, bias=vec(bias, b, b + 1))
                        if o == 0:
                            own.step(ins)
                    emptied(use, ins)
                for n in range(4):
                    a, q = n // 2, n % 2
                    full(act, use_v2[n])
                    emptied(use_v2[n], act.activation(vt2[:, 4 * a + 2 * q:4 * a + 2 * q + 2, :],
                                                               ps[:, use_v2[n][0], :].rearrange("p (o t) -> p o t", o=2), ACT.Copy))
                act.wait_ge(lru_a, 1)
                act.activation(lru_t, gr, ACT.Tanh).then_inc(lru_tanh, 1)
                act.wait_ge(gelu_in, 1)
                act.activation(gel, gel, ACT.Tanh, scale=GELU_C).then_inc(gelu_t, 1)
                act.wait_ge(lru_tanh, 1)
                act.activation(gr, gr, ACT.Exp).then_inc(lru_tanh, 1)
                act.wait_ge(lru_sq, 1)
                act.activation(lru_t, lru_t, ACT.Sqrt).then_inc(lru_h, 1)
                for h in range(AH):
                    d = ATT[h]
                    act.wait_ge(pmax, h + 1)
                    if h >= 2:
                        full(act, ATT[h - 2]["t"])
                    full(act, d["l"])
                    for a in range(TT):
                        ins = act.activation(prob[:, h % 2, a, 0:(a + 1) * P], ps[:, d["l"][0], a * T:a * T + (a + 1) * P], ACT.Exp, scale=SCALE,
                                             bias=mx[:, 0, a + 2 * (h % 2):a + 2 * (h % 2) + 1], accum_out=mx[:, 1, a + 2 * (h % 2):a + 2 * (h % 2) + 1])
                        if a == 0:
                            own.step(ins)
                    emptied(d["l"], ins)
                    full(act, d["t"])
                    own.step(act.activation(probT[:, h % 2, 0, :], ps[:, d["t"][0], 0:T], ACT.Copy))
                    emptied(d["t"], act.activation(probT[:, h % 2, 1, P:], ps[:, d["t"][0], T + P:], ACT.Copy))
                    full(act, d["o"])
                    emptied(d["o"], act.activation(mixT[:, 4 + h, :], ps[:, d["o"][0], 0:T], ACT.Copy))

            def vector(dve, own):
                for b in range(2):
                    dve.wait_ge(bk.free[b], use_in2[b][1] + 9)
                own.step(dve.memset(lru_pad.rearrange("p a t -> p (a t)"), 0.0))
                own.step(dve.memset(pool_in.rearrange("p i a t -> p (i a t)"), 0.0))
                own.settle()
                own.step(dve.tensor_copy(lru_pad[:, :, LRU_TAPS - 1:], zx))
                own.step(dve.tensor_copy(pool_in[:, 0, :, 16:], zp))
                own.settle()
                for k in range(LRU_TAPS):
                    for b in range(4):
                        own.settle(3 if k < LRU_TAPS - 1 else 3 - b)
                        tap = vec("lru_cw", k * 4 + b, k * 4 + b + 1)
                        src = lru_pad[:, b, k:k + T]
                        if k == 0:
                            ins = dve.tensor_scalar(xc[:, b, :], src, tap, vec("lru_cb", b, b + 1), ALU.mult, ALU.add)
                        else:
                            ins = dve.scalar_tensor_tensor(xc[:, b, :], src, tap, xc[:, b, :], ALU.mult, ALU.add)
                        if k == LRU_TAPS - 1:
                            ins.then_inc(xc_ready, 1)
                        else:
                            own.step(ins)
                own.settle()
                for n in range(4):
                    src, dst = pool_in[:, n % 2], pool_in[:, (n + 1) % 2]
                    s = 1 << n
                    own.settle()
                    own.step(dve.tensor_tensor(dst[:, :, s:], src[:, :, s:], src[:, :, 0:PW - s], ALU.add))
                    own.settle()
                    o = CONSTS["pool_inv"][0] + 16 * n
                    own.step(dve.tensor_tensor(pool_d[:, n, 0:16], dst[:, n, 16:32], K[:, o:o + 16], ALU.mult))
                    own.step(dve.tensor_scalar(pool_d[:, n, 16:], dst[:, n, 32:], 1.0 / POOL_WINDOWS[n], None, ALU.mult))
                    own.settle()
                    dve.tensor_tensor(pool_d[:, n, :], pool_d[:, n, :], zp[:, n, :], ALU.subtract).then_inc(pool_ready, 1)
                full(dve, use_f)
                z, e, u, l = fz
                emptied(use_f, dve.tensor_tensor(z, ps[:, use_f[0], 0:TT * AH].rearrange("p (a h) -> p a h", a=TT), bc(vec("b_f"), TT), ALU.add))
                evacuated(dve, use_f)
                own.step(dve.tensor_scalar(sp_l[0], vec("lru_lam"), -1.0, None, ALU.mult))
                own.settle()
                own.step(dve.scalar_tensor_tensor(sp_l[1], sp_l[0], -1.0, sp_l[0], ALU.mult, ALU.max))
                own.settle()
                dve.scalar_tensor_tensor(e, z, -1.0, z, ALU.mult, ALU.max).then_inc(lf_abs, 1)
                dve.wait_ge(lf_e, 1)
                dve.wait_ge(lam_e, 1)
                own.step(dve.tensor_scalar(sp_l[2], sp_l[1], 1.0, None, ALU.add))
                own.settle()
                dve.tensor_scalar(u, e, 1.0, None, ALU.add).then_inc(lf_u, 1)
                dve.wait_ge(lf_u, 1)
                dve.wait_ge(lf_ln, 1)
                dve.wait_ge(lam_ln, 1)
                for zz, ee, uu, ll in ((z, e, u, l), (sp_l[0], sp_l[1], sp_l[2], sp_l[3])):
                    own.step(dve.scalar_tensor_tensor(ee, uu, -1.0, ee, ALU.add, ALU.subtract))
                    own.settle()
                    own.step(dve.reciprocal(uu, uu))
                    own.settle()
                    own.step(dve.tensor_tensor(ee, ee, uu, ALU.mult))
                    own.settle()
                    own.step(dve.tensor_tensor(ll, ll, ee, ALU.subtract))
                    own.settle()
                own.step(dve.scalar_tensor_tensor(l, z, 0.0, l, ALU.min, ALU.subtract))
                own.step(dve.scalar_tensor_tensor(sp_l[3], sp_l[0], 0.0, sp_l[3], ALU.max, ALU.add))
                own.settle()
                own.step(dve.tensor_scalar(sp_l[3], sp_l[3], -8.0, None, ALU.mult))
                dve.tensor_scalar(l, l, -1.0 / SCALE, None, ALU.mult).then_inc(lf_ready, 1)
                own.settle()
                for n in use_lr:
                    evacuated(dve, n)
                for b in range(4):
                    ins = dve.tensor_scalar(gr[:, b, :], gr[:, b, :], sp_l[3][:, b:b + 1], None, ALU.mult)
                    if b < 3:
                        own.step(ins)
                    else:
                        ins.then_inc(lru_a, 1)
                own.step(dve.tensor_tensor(gi, gi, xc, ALU.mult))
                own.step(dve.tensor_tensor(gel, zy, zy, ALU.mult))
                own.settle()
                own.step(dve.tensor_tensor(gel, gel, zy, ALU.mult))
                own.settle()
                dve.scalar_tensor_tensor(gel, gel, 0.044715, zy, ALU.mult, ALU.add).then_inc(gelu_in, 1)
                dve.wait_ge(lru_tanh, 1)
                own.step(dve.tensor_scalar(lru_u, lru_t, -1.0, 1.0, ALU.mult, ALU.add))
                own.settle()
                own.step(dve.reciprocal(lru_u, lru_u))
                own.settle()
                dve.scalar_tensor_tensor(lru_t, lru_t, -2.0, lru_u, ALU.mult, ALU.mult).then_inc(lru_sq, 1)
                dve.wait_ge(lru_h, 1)
                own.step(dve.tensor_tensor(gi, gi, lru_t, ALU.mult))
                own.settle()
                dve.wait_ge(gelu_t, 1)
                own.step(dve.scalar_tensor_tensor(gel, gel, 1.0, zy, ALU.add, ALU.mult))
                dve.wait_ge(lru_tanh, 2)
                for b in range(4):
                    own.step(dve.tensor_tensor_scan(xc[:, b, :], gr[:, b, :], gi[:, b, :], 0.0, ALU.mult, ALU.add))
                own.settle()
                dve.scalar_tensor_tensor(mixT[:, 12:16, :], gel, 0.5, xc, ALU.mult, ALU.mult).then_inc(lru_done, 1)
                dve.wait_ge(pool_ready, 4)
                for h in range(AH):
                    d = ATT[h]
                    full(dve, d["l"])
                    m = 2 * (h % 2)
                    for a in range(TT):
                        own.step(dve.tensor_reduce(mx[:, 0, m + a:m + a + 1], ps[:, d["l"][0], a * T:a * T + (a + 1) * P], AX.X, ALU.max))
                    own.settle()
                    dve.tensor_scalar(mx[:, 0, m:m + 2], mx[:, 0, m:m + 2], -SCALE, None, ALU.mult).then_inc(pmax, 1)
                    evacuated(dve, d["l"])
                    own.step(dve.reciprocal(mx[:, 1, m:m + 2], mx[:, 1, m:m + 2]))
                    own.settle()
                    own.step(dve.tensor_scalar(prob[:, h % 2, 0, 0:P], prob[:, h % 2, 0, 0:P], mx[:, 1, m:m + 1], None, ALU.mult))
                    dve.tensor_scalar(prob[:, h % 2, 1, :], prob[:, h % 2, 1, :], mx[:, 1, m + 1:m + 2], None, ALU.mult).then_inc(pnorm, 1)
        lru_t = zv[:, 0:4, :]
        lru_u = zv[:, 4:8, :]
        gel = zp

        seg_out2 = segment(2 * PAIRS2)
        use_out2 = [bk.take(b, PAIRS2 // 2) for b in range(2)]
        y3 = w(0, KT * T, a=KT)
        y3_pairs = y3.rearrange("p (j o) t -> p j o t", o=2)
        rms_x3 = Rms(xT[:, :, :], lambda e, n: e.wait_ge(nadd, 2 * KT + 2 * n + 2))
        seg_ffn, seg_dn, use_ffn, use_dn = [], [], [], []
        for tiles in PARTS2:
            seg_ffn.append(segment(2 * tiles))
            use_ffn.append([bk.take(b, tiles // 2) for b in range(2)])
            seg_dn.append(segment(2 * PAIRS2))
            use_dn.append([bk.take(b, PAIRS2 // 2) for b in range(2)])
        act2_high, act2_low, y4 = act_high, act_low, yT2
        FW = T + FFN_TAPS - 1
        F2 = 3 * KT * T
        gpad = w(F2, 2 * FW, r=2)
        upb = w(F2 + 2 * FW, 2 * T, r=2)
        gcv = w(F2 + 2 * FW + 2 * T, 2 * T, r=2)
        gpad_zero, gconv, gsilu, gmul, ghi, gact, gtap, out_done = (sem(n) for n in (
            "gpad_zero", "gconv", "gsilu", "gmul", "ghi", "gact", "gtap", "out_done"))
        rms_x4 = Rms(xT[:, :, :], lambda e, n: e.wait_ge(nadd, 3 * KT + 2 * n + 2))
        taps2 = vec("ffn_cw").rearrange("p (a k) -> p a k", k=FFN_TAPS)

        class Ffn2:
            def sync(sp):
                fetch(sp, out2_u, seg_out2, 2 * PAIRS2)
                first = 0
                for n, tiles in enumerate(PARTS2):
                    fetch(sp, ffn_u[2 * first:2 * (first + tiles)], seg_ffn[n], 2 * tiles)
                    fetch(sp, down2_u[2 * PAIRS2 * n:2 * PAIRS2 * (n + 1)], seg_dn[n], 2 * PAIRS2, size=tiles * P)
                    first += tiles
                for n in range(0, KT, 4):
                    sp.wait_ge(out_done, n + 4)
                    sp.dma_start(out_t[:, n:n + 4, :], y3[:, n:n + 4, :]).then_inc(x_in, 16)
                sp.wait_ge(x_in, 48 + KT // 4 * 16)

            def tensor(pe, own):
                to_width(pe, seg_out2, use_out2, halves(h_low, h_high), 3 * KT)
                rms_x3.tensor(pe)
                done = 2
                for n, tiles in enumerate(PARTS2):
                    with pe.Fori(0, tiles // 2) as it:
                        for r in range(2):
                            split_pair(pe, seg_ffn[n] + 2 * r, halves(h_high, h_low), pair(r), [(r, use_ffn[n][r][1])], it * 4, it, 1,
                                       split=4 * KT if n + r == 0 else None)
                    done += tiles

                    def hidden_ready(kt):
                        if kt in (0, tiles - 1):
                            pe.wait_ge(gact, done - (kt == 0))

                    with pe.Fori(0, PAIRS2 // 2) as it:
                        for j in range(2):
                            split_pair(pe, seg_dn[n] + 2 * j, halves(act2_high, act2_low), pair(j), [(j, use_dn[n][j][1])], it * 4, it, 1, kts=tiles,
                                       ready=hidden_ready if j == 0 else None)
                rms_x4.tensor(pe)

            def scalar(act, own):
                from_width(act, seg_out2, use_out2, y3_pairs)
                rms_x3.scalar(act)
                shift_round(act, 2, adaT[:, 3 * KT:4 * KT])
                act.wait_ge(gpad_zero, 1)
                first = 0
                for n, tiles in enumerate(PARTS2):
                    with act.Fori(0, tiles // 2) as it:
                        for r in range(2):
                            act.wait_ge(gact, it * 2 + (first + r + 1))
                            unit_done(act, seg_ffn[n] + 2 * r + 1, it, 4)
                            act.activation(gpad[:, r, FFN_TAPS - 1:], ps[:, r, 0:T], ACT.Copy).then_inc(gup, 1)
                            act.activation(upb[:, r, :], ps[:, r, T:], ACT.Copy).then_inc(bk.free[r], 1)
                            act.wait_ge(gconv, it * 2 + (first + r + 1))
                            act.activation(gcv[:, r, :], gcv[:, r, :], ACT.Silu).then_inc(gsilu, 1)
                    first += tiles
                rms_x4.scalar(act)

            def vector(dve, own):
                dve.wait_ge(lru_done, 1)
                evacuated(dve, use_pool[0])
                evacuated(dve, use_pool[1])
                for h in range(AH):
                    evacuated(dve, ATT[h]["o"])
                split_x(dve, own, mixT, h_low, h_high)
                split_units(dve, seg_out2 + 2, 2 * PAIRS2)
                for kt in range(KT):
                    if kt % 2 == 0:
                        b = kt // 2 % 2
                        dve.wait_ge(bk.free[b], use_out2[b][1] + kt // 4 + 1)
                    dve.scalar_tensor_tensor(xT[:, kt, :], y3[:, kt, :], adaT[:, 2 * KT + kt:2 * KT + kt + 1], xT[:, kt, :], ALU.mult, ALU.add).then_inc(nadd, 1)
                own.step(dve.memset(gpad.rearrange("p r t -> p (r t)"), 0.0))
                own.settle()
                dve.sem_inc(gpad_zero, 1)
                rms_x3.vector(dve)
                scale_split(dve, 2, gffn, adaT[:, 3 * KT:4 * KT])
                own.step(dve.memset(flat(y4), 0.0))
                dve.sem_inc(gact, 2)
                dve.wait_ge(nadd, 3 * KT)
                own.settle()
                first = 0
                for n, tiles in enumerate(PARTS2):
                    def finish(at, t, r):
                        dve.wait_ge(gsilu, at + 1)
                        dve.tensor_tensor(gcv[:, r, :], gcv[:, r, :], upb[:, r, :], ALU.mult).then_inc(gmul, 1)
                        dve.wait_ge(gmul, at + 1)
                        high, low = act2_high[:, t, :], act2_low[:, t, :]
                        dve.tensor_copy(high, gcv[:, r, :]).then_inc(ghi, 1)
                        dve.wait_ge(ghi, at + 1)
                        dve.tensor_tensor(low, gcv[:, r, :], high.bitcast(F32), ALU.subtract).then_inc(gact, 1)

                    def hidden(it, last_size, begin=False):
                        for r in range(2):
                            size = last_size if r == 1 else UNIT
                            at = it * 2 + (first + r)
                            split_unit(dve, seg_ffn[n] + 2 * r + 2, it * 4, size)
                            if not (begin and r == 0):
                                finish(at - 1, it * 2 + (r - 1), 1 - r)
                            split_unit(dve, seg_ffn[n] + 2 * r + 3, it * 4, size)
                            dve.wait_ge(bk.free[r], it + (use_ffn[n][r][1] + 1))
                            dve.wait_ge(gup, at + 1)
                            for k in range(FFN_TAPS):
                                tap = taps2[:, bass.ds(at, 1), k]
                                if k == 0:
                                    bias = vec("ffn_cb")[:, bass.ds(at, 1)]
                                    ins = dve.tensor_scalar(gcv[:, r, :], gpad[:, r, 0:T], tap, bias, ALU.mult, ALU.add)
                                else:
                                    dve.wait_ge(gtap, at * 2 + k)
                                    ins = dve.scalar_tensor_tensor(gcv[:, r, :], gpad[:, r, k:k + T], tap, gcv[:, r, :], ALU.mult, ALU.add)
                                ins.then_inc(gconv if k == FFN_TAPS - 1 else gtap, 1)

                    def down(it, last_size):
                        for j in range(2):
                            if last_size or j == 0:
                                for o in range(2):
                                    split_unit(dve, seg_dn[n] + 2 * j + 2 + o, it * 4, last_size if j == 1 else tiles * P)
                            unit_done(dve, seg_dn[n] + 2 * j + 1, it, 4)
                            y = y4.rearrange("p (j o) t -> p j o t", o=2)[:, it * 2 + j]
                            dve.tensor_tensor(y, y, ps[:, j, :].rearrange("p (o t) -> p o t", o=2), ALU.add).then_inc(bk.free[j], 1)

                    if n:
                        for b in range(2):
                            dve.wait_ge(bk.free[b], use_dn[n - 1][b][1] + PAIRS2 // 2)
                    hidden(0, UNIT, begin=True)
                    with dve.Fori(1, tiles // 2 - 1) as it:
                        hidden(it, UNIT)
                    hidden(tiles // 2 - 1, tiles * P)
                    finish(first + tiles - 1, tiles - 1, 1)
                    with dve.Fori(0, PAIRS2 // 2 - 1) as it:
                        down(it, tiles * P)
                    down(PAIRS2 // 2 - 1, UNIT if n + 1 < len(PARTS2) else 0)
                    first += tiles
                width_done(dve, use_dn[-1])
                for kt in range(KT):
                    dve.scalar_tensor_tensor(xT[:, kt, :], y4[:, kt, :], adaT[:, 5 * KT + kt:5 * KT + kt + 1], xT[:, kt, :], ALU.mult, ALU.add).then_inc(nadd, 1)
                rms_x4.vector(dve)
                for kt in range(KT):
                    dve.scalar_tensor_tensor(y3[:, kt, :], xT[:, kt, :], vec("final_g", kt, kt + 1), rtn, ALU.mult, ALU.mult).then_inc(out_done, 1)
        gup = sem("gup")

        with nc.Block() as block:
            @block.sync
            def _(sp):
                Mod.sync(sp)
                ConvFft.sync(sp)
                SsdIn.sync(sp)
                RwIn.sync(sp)
                Merge.sync(sp)
                Mix.sync(sp)
                Mlp.sync(sp)
                In2.sync(sp)
                Ffn2.sync(sp)

            @block.tensor
            def _(pe):
                own = Own(pe, pe_done)
                Mod.tensor(pe, own)
                Norm0.tensor(pe, own)
                ConvFft.tensor(pe, own)
                SsdIn.tensor(pe, own)
                SsdScan.tensor(pe, own)
                RwIn.tensor(pe, own)
                RwScan.tensor(pe, own)
                RwOut.tensor(pe, own)
                Merge.tensor(pe, own)
                Mix.tensor(pe, own)
                Mlp.tensor(pe, own)
                In2.tensor(pe, own)
                Mix2.tensor(pe, own)
                Ffn2.tensor(pe, own)

            @block.scalar
            def _(act):
                own = Own(act, act_done)
                Mod.scalar(act, own)
                Norm0.scalar(act, own)
                ConvFft.scalar(act, own)
                ConvFft.scalar_norm(act, own)
                SsdIn.scalar(act, own)
                SsdScan.scalar(act, own)
                RwIn.scalar(act, own)
                RwScan.scalar(act, own)
                RwOut.scalar(act, own)
                Merge.scalar(act, own)
                Mix.scalar(act, own)
                Mlp.scalar(act, own)
                In2.scalar(act, own)
                Mix2.scalar(act, own)
                Ffn2.scalar(act, own)

            @block.vector
            def _(dve):
                own = Own(dve, dve_done)
                Mod.vector(dve, own)
                Norm0.vector(dve, own)
                ConvFft.vector(dve, own)
                ConvFft.vector_norm(dve, own)
                SsdIn.vector(dve, own)
                SsdScan.vector(dve, own)
                RwIn.vector(dve, own)
                RwScan.vector(dve, own)
                RwOut.vector(dve, own)
                Merge.vector(dve, own)
                Mix.vector(dve, own)
                Mlp.vector(dve, own)
                In2.vector(dve, own)
                Mix2.vector(dve, own)
                Ffn2.vector(dve, own)

            @block.gpsimd
            def _(pool):
                own = Own(pool, pool_done)
                SsdIn.gpsimd(pool, own)
                RwScan.gpsimd(pool, own)
                Merge.gpsimd(pool, own)



def cols(a):
    return np.ascontiguousarray(np.asarray(a).reshape(-1, P).T)


def by_units(wm, width=P):
    k, c = wm.shape
    v = wm.reshape(k // P, P, c // width, width).transpose(2, 1, 0, 3)
    return np.ascontiguousarray(v.reshape(c // width, P, -1))


def by_rows(wm):
    return np.ascontiguousarray(wm.T).reshape(-1, P, wm.shape[0])


def k_major(wm):
    k, c = wm.shape
    return np.ascontiguousarray(wm.reshape(k // P, P, c).transpose(1, 0, 2).reshape(P, -1))


def tokens_last(x):
    return np.ascontiguousarray(np.asarray(x)[0].reshape(T, KT, P).transpose(2, 1, 0))


def lay_out(i):
    i = {k: np.asarray(v) for k, v in i.items()}
    vecs = np.zeros((P, VEC_N), np.float32)

    def put(name, a, rows=P):
        o, n = VECS[name]
        vecs[0:rows, o:o + n] = a

    def rows(a):
        return np.broadcast_to(a.reshape(1, -1), (P, a.size))

    def taps(a):
        return a.reshape(a.shape[0], -1, P).transpose(2, 0, 1).reshape(P, -1)

    put("c", np.stack([cols(i["c"]), cols(i["c_ctx"])], 2).reshape(P, -1))
    put("mod_b", cols(i["mod_b"]))
    put("ada_b", cols(i["b_ada_2"]))
    put("norm_g", cols(i["norm_g"]))
    put("conv_w", taps(i["conv_w"][0]))
    for name, key in (("conv_b", "conv_b"), ("conv_ln_g", "conv_ln_g"), ("conv_ln_b", "conv_ln_b"), ("ssd_cb", "ssd_conv_b"),
                      ("ssd_ng", "ssd_norm_g"), ("w0", "rwkv_w0"), ("a0", "rwkv_a0"), ("k_k", "rwkv_k_k"), ("k_a", "rwkv_k_a"),
                      ("r_k", "rwkv_r_k"), ("rln_g", "rwkv_ln_g"), ("rln_b", "rwkv_ln_b"), ("g_mix", "g_mix_2"),
                      ("g_ffn", "g_ffn_2"), ("final_g", "final_g_2"), ("pool_scale", "pool_scale_2"), ("lru_cb", "lru_conv_b_2"),
                      ("lru_ba", "lru_ba_2"), ("lru_bi", "lru_bi_2"), ("lru_lam", "lru_lambda_2"), ("ffn_cb", "ffn_conv_b_2")):
        put(name, cols(i[key]))
    put("ssd_cw", taps(i["ssd_conv_w"][0]))
    put("lru_cw", taps(i["lru_conv_w_2"][0]))
    put("ffn_cw", i["ffn_conv_w_2"][0].reshape(FFN_TAPS, KF2, P).transpose(2, 1, 0).reshape(P, -1))
    put("A_log", rows(i["ssd_A_log"]))
    put("dt_bias", rows(i["ssd_dt_bias"]))
    put("ssd_D", rows(i["ssd_D"]))
    put("b_f", rows(i["b_f_2"]))
    mu = i["rwkv_mu"][0]
    put("mu", np.pad(cols(mu[0:3 * RW_DIM]), ((0, 0), (0, 3))))
    o = VECS["mu"][0]
    lo = 3 * RW_DIM
    vecs[:, o + 12] = mu[lo:lo + 2 * LORA]
    vecs[:, o + 13] = mu[lo + 3 * LORA:]
    vecs[0:LORA, o + 14] = mu[lo + 2 * LORA:lo + 3 * LORA]

    w_in = i["w_in"][0]
    rw = SSD_IN
    cv = REC_IN
    ff = REC_IN + 2 * CONV
    gt = ff + FFT
    smalls = np.zeros((P, SMALL_N), np.float32)
    smalls[:, 0:KT * 88] = k_major(np.concatenate([w_in[:, rw + lo + 2 * LORA:rw + lo + 3 * LORA], w_in[:, SSD_IN - 2 * SSD_H:SSD_IN]], 1))
    for name, a in (("w2", i["rwkv_w2"].reshape(2 * LORA, RW_DIM)), ("a2", i["rwkv_a2"][0]), ("g2", i["rwkv_g2"][0])):
        at, n = SMALLS[name]
        smalls[0:a.shape[0], at:at + n] = a
    w_in2 = i["w_in_2"][0]
    fcol = POOL + 3 * ATTN
    smalls2 = np.concatenate([k_major(w_in2[:, fcol:fcol + AH])] + [
        np.ascontiguousarray(i[k][0].transpose(1, 0, 2).reshape(P, -1)) for k in ("pool_w_2", "lru_wa_2", "lru_wi_2")], 1)

    bo = np.concatenate([i[k][0] for k in ("conv_out", "ssd_out", "fourier_out", "rwkv_out")], 0)
    gates = w_in[:, gt:].reshape(D, 4, KT // 2, 2 * P).transpose(0, 2, 1, 3).reshape(D, -1)
    ffn = np.stack([i["w_ffn_gate_2"][0].reshape(D, KF2, P), i["w_ffn_up_2"][0].reshape(D, KF2, P)], 2).reshape(D, -1)
    up, down = i["mlp_up"][0], i["mlp_down"][0]
    mlp = np.concatenate([u for q in range(0, D_FF, D) for u in (by_units(up[:, q:q + D]), by_units(down[q:q + D]))], 0)
    down2 = np.zeros((len(PARTS2) * KT, P, UNIT), np.float32)
    first = 0
    for n, tiles in enumerate(PARTS2):
        down2[n * KT:(n + 1) * KT, :, 0:tiles * P] = by_units(i["w_ffn_down_2"][0][first * P:(first + tiles) * P])
        first += tiles
    return dict(
        x_t=tokens_last(i["x"]), ctx_t=tokens_last(i["ctx"]), vecs=vecs, consts=shape_constants(), smalls=smalls, smalls2=smalls2,
        c_rows=np.concatenate([i["c"], i["c_2"]], 0), mod_u=by_units(i["mod_w"][0][:, 0:2 * D]), mod_r=by_rows(i["mod_w"][0][:, 2 * D:]),
        ada_r=by_rows(i["w_ada_2"][0]),
        conv_u=by_units(np.concatenate([w_in[:, cv + CONV:ff], w_in[:, cv:cv + CONV], w_in[:, ff:gt]], 1)),
        ssd_u=by_units(w_in[:, 0:SSD_IN - 2 * SSD_H]),
        rw_u=by_units(np.concatenate([w_in[:, rw:rw + lo + 2 * LORA], w_in[:, rw + lo + 3 * LORA:rw + RW_IN]], 1)),
        gate_u=by_units(gates), bo_u=by_units(bo, 2 * P), wo_u=by_units(i["w_o"][0]), mlp_u=mlp,
        in2_u=by_units(np.concatenate([w_in2[:, 0:fcol], w_in2[:, fcol + AH:]], 1)),
        out2_u=by_units(i["w_out_2"][0]), ffn_u=by_units(ffn), down2_u=down2)


def kernel(**inputs):
    import concourse.bacc as bacc
    from concourse.bass_utils import run_bass_kernel_spmd

    arrays = lay_out(inputs)
    nc = bacc.Bacc("TRN2", target_bir_lowering=False, num_devices=1)
    args = {n: nc.dram_tensor(f"in_{n}", a.shape, mybir.dt.from_np(a.dtype), kind="ExternalInput").ap() for n, a in arrays.items()}
    out = nc.dram_tensor("out_t", (P, KT, T), F32, kind="ExternalOutput").ap()
    branch_kernel(nc, out_t=out, **args)
    r = run_bass_kernel_spmd(nc, [{f"in_{n}": a for n, a in arrays.items()}], core_ids=[0])
    y = r.results[0]["out_t"]
    return np.ascontiguousarray(y.transpose(2, 1, 0)).reshape(1, T, D)
```
